# Optimizing a Trainium2 kernel written in Bass

```python
import math
import jax, jax.numpy as jnp
from jax import lax
import numpy as np
import jax
import jax.numpy as jnp

D_MODEL = 1024
BATCH = 1
SEQ = 256
DEPTH = 2

N_MIXERS = 2
N_A = (DEPTH + 1) // 2
N_B = DEPTH // 2

LRU_WIDTH = D_MODEL
N_LRU_BLOCKS = 4
LRU_BLOCK = LRU_WIDTH // N_LRU_BLOCKS
CONV_WIDTH = 4
LRU_C = 8.0
A_MIN = 0.9
A_MAX = 0.999

HEAD_DIM = 64
N_HEADS = D_MODEL // HEAD_DIM
Q_BLOCK = 128

D_FF = int(math.ceil(8 * D_MODEL / 3 / 256)) * 256

RMS_EPS = 1e-6


def rms_norm(x, g):
    xf = x.astype(jnp.float32)
    y = xf * lax.rsqrt(jnp.mean(xf * xf, axis=-1, keepdims=True) + RMS_EPS)
    return (y * g.astype(jnp.float32)).astype(x.dtype)

def causal_depthwise_conv(x, w, b):
    c = x.shape[-1]
    y = lax.conv_general_dilated(
        x, w.reshape(CONV_WIDTH, 1, c).astype(x.dtype),
        window_strides=(1,), padding=[(CONV_WIDTH - 1, 0)],
        dimension_numbers=("NWC", "WIO", "NWC"), feature_group_count=c)
    return y + b

def _linear_recurrence_combine(e1, e2):
    a1, b1 = e1
    a2, b2 = e2
    return a1 * a2, a2 * b1 + b2

def rg_lru_block(x, w_in, b_in, conv_w, conv_b, gate_w, gate_b, lam, w_out, b_out):
    bsz, seq, _ = x.shape
    u = jnp.einsum("bsd,de->bse", x, w_in) + b_in
    gate_branch, rec = u[..., :LRU_WIDTH], u[..., LRU_WIDTH:]
    rec = causal_depthwise_conv(rec, conv_w, conv_b)
    rec_blk = rec.reshape(bsz, seq, N_LRU_BLOCKS, LRU_BLOCK)
    gl = jnp.einsum("bsnc,gncd->gbsnd", rec_blk, gate_w).reshape(2, bsz, seq, LRU_WIDTH)
    gl = gl.astype(jnp.float32) + gate_b.astype(jnp.float32)[:, None, None, :]
    r_gate = jax.nn.sigmoid(gl[0])
    i_gate = jax.nn.sigmoid(gl[1])
    log_a = -LRU_C * r_gate * jax.nn.softplus(-lam.astype(jnp.float32))
    a = jnp.exp(log_a)
    mult = jnp.sqrt(-jnp.expm1(2.0 * log_a))
    b = mult * (i_gate * rec.astype(jnp.float32))
    _, h = lax.associative_scan(_linear_recurrence_combine, (a, b), axis=1)
    y = jax.nn.gelu(gate_branch, approximate=True) * h.astype(x.dtype)
    return jnp.einsum("bse,ed->bsd", y, w_out) + b_out

def stick_breaking_attention(x, w_qkv, w_o):
    bsz, seq, _ = x.shape
    qkv = jnp.einsum("bsd,de->bse", x, w_qkv).reshape(bsz, seq, 3, N_HEADS, HEAD_DIM)
    q = jnp.transpose(qkv[:, :, 0], (0, 2, 1, 3))
    k = jnp.transpose(qkv[:, :, 1], (0, 2, 1, 3))
    v = jnp.transpose(qkv[:, :, 2], (0, 2, 1, 3))
    scale = 1.0 / math.sqrt(HEAD_DIM)
    outs = []
    for blk in range(seq // Q_BLOCK):
        t0 = blk * Q_BLOCK
        t1 = t0 + Q_BLOCK
        qb = q[:, :, t0:t1]
        kb = k[:, :, :t1]
        vb = v[:, :, :t1]
        z = jnp.einsum("bhqd,bhkd->bhqk", qb, kb).astype(jnp.float32) * scale
        t_idx = t0 + jnp.arange(Q_BLOCK)[:, None]
        s_idx = jnp.arange(t1)[None, :]
        strict = s_idx < t_idx
        log_fail = jnp.where(strict, jax.nn.log_sigmoid(-z), 0.0)
        suffix = lax.cumsum(log_fail, axis=3, reverse=True) - log_fail
        weights = jnp.where(strict, jnp.exp(jax.nn.log_sigmoid(z) + suffix), 0.0)
        outs.append(jnp.einsum("bhqk,bhkd->bhqd", weights.astype(vb.dtype), vb))
    o = jnp.concatenate(outs, axis=2)
    o = jnp.transpose(o, (0, 2, 1, 3)).reshape(bsz, seq, N_HEADS * HEAD_DIM)
    return jnp.einsum("bse,ed->bsd", o, w_o)

def swiglu_ffn(x, w_in, w_out):
    gu = jnp.einsum("bsd,df->bsf", x, w_in)
    h = jax.nn.silu(gu[..., :D_FF]) * gu[..., D_FF:]
    return jnp.einsum("bsf,fd->bsd", h, w_out)

def first_inputs(seed: int = 0) -> dict:
    key = jax.random.key(seed)
    ks = jax.random.split(key, 20)
    f32 = jnp.float32

    def nrm(k, shape, fan_in):
        return jax.random.normal(k, shape, f32) * (fan_in ** -0.5)

    x = jax.random.normal(ks[0], (BATCH, SEQ, D_MODEL), f32)
    mix_norm = 1.0 + 0.05 * jax.random.normal(ks[1], (DEPTH, D_MODEL), f32)
    ffn_norm = 1.0 + 0.05 * jax.random.normal(ks[2], (DEPTH, D_MODEL), f32)
    final_norm = 1.0 + 0.05 * jax.random.normal(ks[3], (D_MODEL,), f32)

    lru_w_in = nrm(ks[4], (N_A, D_MODEL, 2 * LRU_WIDTH), D_MODEL)
    lru_b_in = 0.02 * jax.random.normal(ks[5], (N_A, 2 * LRU_WIDTH), f32)
    lru_conv_w = nrm(ks[6], (N_A, CONV_WIDTH, LRU_WIDTH), CONV_WIDTH)
    lru_conv_b = 0.02 * jax.random.normal(ks[7], (N_A, LRU_WIDTH), f32)
    lru_gate_w = nrm(ks[8], (N_A, 2, N_LRU_BLOCKS, LRU_BLOCK, LRU_BLOCK), LRU_BLOCK)
    lru_gate_b = 0.02 * jax.random.normal(ks[9], (N_A, 2, LRU_WIDTH), f32)
    u = jax.random.uniform(ks[10], (N_A, LRU_WIDTH), f32, A_MIN, A_MAX)
    a0 = u ** (1.0 / LRU_C)
    lru_lambda = jnp.log(a0) - jnp.log1p(-a0)
    lru_w_out = nrm(ks[11], (N_A, LRU_WIDTH, D_MODEL), LRU_WIDTH)
    lru_b_out = 0.02 * jax.random.normal(ks[12], (N_A, D_MODEL), f32)

    attn_w_qkv = nrm(ks[13], (N_B, D_MODEL, 3 * N_HEADS * HEAD_DIM), D_MODEL)
    attn_w_o = nrm(ks[14], (N_B, N_HEADS * HEAD_DIM, D_MODEL), N_HEADS * HEAD_DIM)

    ffn_w_in = nrm(ks[15], (DEPTH, D_MODEL, 2 * D_FF), D_MODEL)
    ffn_w_out = nrm(ks[16], (DEPTH, D_FF, D_MODEL), D_FF)

    return {
        "x": x, "mix_norm": mix_norm, "ffn_norm": ffn_norm, "final_norm": final_norm,
        "lru_w_in": lru_w_in, "lru_b_in": lru_b_in, "lru_conv_w": lru_conv_w,
        "lru_conv_b": lru_conv_b, "lru_gate_w": lru_gate_w, "lru_gate_b": lru_gate_b,
        "lru_lambda": lru_lambda, "lru_w_out": lru_w_out, "lru_b_out": lru_b_out,
        "attn_w_qkv": attn_w_qkv, "attn_w_o": attn_w_o,
        "ffn_w_in": ffn_w_in, "ffn_w_out": ffn_w_out,
    }

def first_block(x, mix_norm, ffn_norm, final_norm, lru_w_in, lru_b_in, lru_conv_w,
              lru_conv_b, lru_gate_w, lru_gate_b, lru_lambda, lru_w_out, lru_b_out,
              attn_w_qkv, attn_w_o, ffn_w_in, ffn_w_out):
    h = x
    for layer in range(DEPTH):
        mixer = layer % N_MIXERS
        j = layer // N_MIXERS
        hn = rms_norm(h, mix_norm[layer])
        if mixer == 0:
            mixed = rg_lru_block(hn, lru_w_in[j], lru_b_in[j], lru_conv_w[j], lru_conv_b[j],
                                 lru_gate_w[j], lru_gate_b[j], lru_lambda[j],
                                 lru_w_out[j], lru_b_out[j])
        else:
            mixed = stick_breaking_attention(hn, attn_w_qkv[j], attn_w_o[j])
        h = h + mixed
        h = h + swiglu_ffn(rms_norm(h, ffn_norm[layer]), ffn_w_in[layer], ffn_w_out[layer])
    return rms_norm(h, final_norm)


DEPTH_2 = 1

MOBA_HEADS = 8
MOBA_HEAD_DIM = 64
MOBA_WIDTH = MOBA_HEADS * MOBA_HEAD_DIM
MOBA_BLOCK = 256
MOBA_TOPK = 3
MOBA_QCHUNK = 128
HGRN_HEADS = 4
HGRN_KDIM = 128
HGRN_VDIM = 128
HGRN_WIDTH = HGRN_HEADS * HGRN_VDIM
HGRN_CHUNK = 64
LOG_DECAY_MASK = -1e4
EXP_CLIP = 30.0
REL_BUCKETS = 32
REL_MAX_DIST = 2048
PLE_DIM = 256
NEG_INF = -1e30
IN_COLS = (MOBA_WIDTH,) * 4 + (HGRN_HEADS * HGRN_KDIM,) * 2 + (HGRN_WIDTH,) * 2 + (D_MODEL,) * 2
IN_WIDTH = sum(IN_COLS)


def rmsnorm(x, gain):
    xf = x.astype(jnp.float32)
    return xf * lax.rsqrt(jnp.mean(xf * xf, axis=-1, keepdims=True) + RMS_EPS) * gain.astype(jnp.float32)

def t5_bucket(rel):
    n = jnp.maximum(rel, 0)
    max_exact = REL_BUCKETS // 2
    nf = jnp.maximum(n, max_exact).astype(jnp.float32)
    large = max_exact + (jnp.log(nf / max_exact) / math.log(REL_MAX_DIST / max_exact)
                         * (REL_BUCKETS - max_exact)).astype(jnp.int32)
    large = jnp.minimum(large, REL_BUCKETS - 1)
    return jnp.where(n < max_exact, n, large)

def moba_attention(q, k, v, rel_bias):
    b, h, s, dh = q.shape
    nb = -(-s // MOBA_BLOCK)
    s_pad = nb * MOBA_BLOCK
    pad = ((0, 0), (0, 0), (0, s_pad - s), (0, 0))
    q, k, v = jnp.pad(q, pad), jnp.pad(k, pad), jnp.pad(v, pad)
    k_blk = k.reshape(b, h, nb, MOBA_BLOCK, dh)
    v_blk = v.reshape(b, h, nb, MOBA_BLOCK, dh)
    k_mean = jnp.mean(k_blk, axis=3)
    q_blk = jnp.arange(s_pad) // MOBA_BLOCK
    gate = jnp.einsum('bhsd,bhnd->bhsn', q, k_mean)
    fully_past = jnp.arange(nb)[None, :] < q_blk[:, None]
    gate = jnp.where(fully_past, gate, NEG_INF)
    topk = min(MOBA_TOPK, nb)
    _, sel = lax.top_k(gate, topk)

    bias_table = rel_bias.astype(jnp.float32).T
    b_ix = jnp.arange(b)[:, None, None]
    h_ix = jnp.arange(h)[None, :, None]
    h4 = jnp.arange(h)[None, :, None, None]
    offs = jnp.arange(MOBA_BLOCK)
    scale = dh ** -0.5
    nqc = s_pad // MOBA_QCHUNK
    q_c = jnp.moveaxis(q.reshape(b, h, nqc, MOBA_QCHUNK, dh), 2, 0)
    sel_c = jnp.moveaxis(sel.reshape(b, h, nqc, MOBA_QCHUNK, topk), 2, 0)

    def chunk(args):
        qc, sc, c = args
        qpos = c * MOBA_QCHUNK + jnp.arange(MOBA_QCHUNK)
        blk = (c * MOBA_QCHUNK) // MOBA_BLOCK
        logits = []
        for j in range(topk):
            idx = sc[..., j]
            kg = k_blk[b_ix, h_ix, idx]
            rel = qpos[:, None] - (idx[..., None] * MOBA_BLOCK + offs)
            lg = jnp.einsum('bhqd,bhqkd->bhqk', qc, kg) * scale + bias_table[h4, t5_bucket(rel)]
            logits.append(jnp.where(j < blk, lg, NEG_INF))
        k_own = lax.dynamic_index_in_dim(k_blk, blk, axis=2, keepdims=False)
        v_own = lax.dynamic_index_in_dim(v_blk, blk, axis=2, keepdims=False)
        rel_own = qpos[:, None] - (blk * MOBA_BLOCK + offs)[None, :]
        lg_own = jnp.einsum('bhqd,bhkd->bhqk', qc, k_own) * scale + bias_table[:, t5_bucket(rel_own)]
        logits.append(jnp.where(rel_own >= 0, lg_own, NEG_INF))
        probs = jax.nn.softmax(jnp.concatenate(logits, axis=-1), axis=-1)
        out = jnp.einsum('bhqk,bhkd->bhqd', probs[..., topk * MOBA_BLOCK:], v_own)
        for j in range(topk):
            vg = v_blk[b_ix, h_ix, sc[..., j]]
            out = out + jnp.einsum('bhqk,bhqkd->bhqd', probs[..., j * MOBA_BLOCK:(j + 1) * MOBA_BLOCK], vg)
        return out

    out = lax.map(chunk, (q_c, sel_c, jnp.arange(nqc)))
    return jnp.moveaxis(out, 0, 2).reshape(b, h, s_pad, dh)[:, :, :s]

def hgrn2_chunkwise(q, k, v, g):
    b, s, h, dk = q.shape
    dv = v.shape[-1]
    nc = s // HGRN_CHUNK

    def chunks(t):
        return t.reshape(b, nc, HGRN_CHUNK, h, t.shape[-1]).transpose(1, 0, 3, 2, 4)

    causal = jnp.tril(jnp.ones((HGRN_CHUNK, HGRN_CHUNK), dtype=bool))

    def step(state, inp):
        qc, kc, vc, gc = inp
        cum = jnp.cumsum(gc, axis=2)
        o_inter = jnp.einsum('bhtk,bhkv->bhtv', qc * jnp.exp(cum), state)
        diff = jnp.where(causal[:, :, None], cum[:, :, :, None, :] - cum[:, :, None, :, :], LOG_DECAY_MASK)
        scores = jnp.einsum('bhtk,bhsk,bhtsk->bhts', qc, kc, jnp.exp(diff))
        o_intra = jnp.einsum('bhts,bhsv->bhtv', scores, vc)
        last = cum[:, :, -1:, :]
        state = state * jnp.exp(last[:, :, 0, :, None]) + jnp.einsum('bhsk,bhsv->bhkv', kc * jnp.exp(last - cum), vc)
        return state, o_inter + o_intra

    state0 = jnp.zeros((b, h, dk, dv), jnp.float32)
    _, out = lax.scan(step, state0, (chunks(q), chunks(k), chunks(v), chunks(g)))
    return out.transpose(1, 0, 3, 2, 4).reshape(b, s, h, dv)

def second_inputs(seed: int = 0) -> dict:
    key = jax.random.key(seed)
    ks = jax.random.split(key, 14)
    f32 = jnp.float32
    nrm = lambda k, shp: jax.random.normal(k, shp, f32)
    return {
        'x': nrm(ks[0], (BATCH, SEQ, D_MODEL)),
        'p': nrm(ks[1], (DEPTH_2, BATCH, SEQ, PLE_DIM)),
        'norm_gain': 1.0 + 0.05 * nrm(ks[2], (DEPTH_2, D_MODEL)),
        'w_in': nrm(ks[3], (DEPTH_2, D_MODEL, IN_WIDTH)) * D_MODEL ** -0.5,
        'q_norm_gain': 1.0 + 0.05 * nrm(ks[4], (DEPTH_2, MOBA_HEAD_DIM)),
        'k_norm_gain': 1.0 + 0.05 * nrm(ks[5], (DEPTH_2, MOBA_HEAD_DIM)),
        'rel_bias': 0.5 * nrm(ks[6], (REL_BUCKETS, MOBA_HEADS)),
        'hgrn_lb_logits': 0.1 * nrm(ks[7], (DEPTH_2, HGRN_HEADS * HGRN_KDIM)),
        'hgrn_out_gain': 1.0 + 0.05 * nrm(ks[8], (DEPTH_2, HGRN_WIDTH)),
        'w_up_a': nrm(ks[9], (DEPTH_2, MOBA_WIDTH, D_MODEL)) * MOBA_WIDTH ** -0.5,
        'w_up_b': nrm(ks[10], (DEPTH_2, HGRN_WIDTH, D_MODEL)) * HGRN_WIDTH ** -0.5,
        'w_out': nrm(ks[11], (DEPTH_2, D_MODEL, D_MODEL)) * D_MODEL ** -0.5,
        'w_ple': nrm(ks[12], (DEPTH_2, PLE_DIM, D_MODEL)) * PLE_DIM ** -0.5,
        'w_ple_gate': nrm(ks[13], (DEPTH_2, D_MODEL, D_MODEL)) * D_MODEL ** -0.5,
    }

def second_block(x, p, norm_gain, w_in, q_norm_gain, k_norm_gain, rel_bias, hgrn_lb_logits,
              hgrn_out_gain, w_up_a, w_up_b, w_out, w_ple, w_ple_gate):
    f32 = jnp.float32
    dt = x.dtype
    b, s, _ = x.shape
    split_pts = []
    acc = 0
    for w in IN_COLS[:-1]:
        acc += w
        split_pts.append(acc)
    lb_sm = jax.nn.softmax(hgrn_lb_logits.astype(f32), axis=0)
    lower_bounds = jnp.cumsum(lb_sm, axis=0) - lb_sm[0:1]

    h = x
    for i in range(DEPTH_2):
        xn = rmsnorm(h, norm_gain[i]).astype(dt)
        proj = xn @ w_in[i]
        aq, ak, av, ag, bq, bf, bi, bg, gate_a, gate_b = jnp.split(proj, split_pts, axis=-1)

        def heads(t):
            return t.reshape(b, s, MOBA_HEADS, MOBA_HEAD_DIM).transpose(0, 2, 1, 3)
        qa = rmsnorm(heads(aq), q_norm_gain[i])
        ka = rmsnorm(heads(ak), k_norm_gain[i])
        va = heads(av).astype(f32)
        ya = moba_attention(qa, ka, va, rel_bias).transpose(0, 2, 1, 3).reshape(b, s, MOBA_WIDTH)
        ya = (ya * jax.nn.silu(ag.astype(f32))).astype(dt) @ w_up_a[i]

        lb = lower_bounds[i].reshape(HGRN_HEADS, HGRN_KDIM)
        fpre = bf.astype(f32).reshape(b, s, HGRN_HEADS, HGRN_KDIM)
        log_f = jax.nn.log_sigmoid(fpre) + jnp.log1p(lb * jnp.exp(jnp.minimum(-fpre, EXP_CLIP)))
        kb = (1.0 - lb) * jax.nn.sigmoid(-fpre)
        qb = jax.nn.silu(bq.astype(f32)).reshape(b, s, HGRN_HEADS, HGRN_KDIM)
        vb = bi.astype(f32).reshape(b, s, HGRN_HEADS, HGRN_VDIM)
        yb = hgrn2_chunkwise(qb, kb, vb, log_f)
        yb = rmsnorm(yb, hgrn_out_gain[i].reshape(HGRN_HEADS, HGRN_VDIM)).reshape(b, s, HGRN_WIDTH)
        yb = (yb * jax.nn.silu(bg.astype(f32))).astype(dt) @ w_up_b[i]

        merged = jax.nn.sigmoid(gate_a.astype(f32)) * ya.astype(f32) + jax.nn.sigmoid(gate_b.astype(f32)) * yb.astype(f32)
        h = h + merged.astype(dt) @ w_out[i]

        ple = (p[i] @ w_ple[i]).astype(f32) * jax.nn.sigmoid((h @ w_ple_gate[i]).astype(f32))
        h = h + ple.astype(dt)
    return h


def setup_inputs(seed=0):
    out = dict(first_inputs(seed))
    for name, value in second_inputs(seed + 1).items():
        if name != "x":
            out[name + "_2"] = value
    return out


def reference(
    x, mix_norm, ffn_norm, final_norm, lru_w_in, lru_b_in, lru_conv_w, lru_conv_b, lru_gate_w,
    lru_gate_b, lru_lambda, lru_w_out, lru_b_out, attn_w_qkv, attn_w_o, ffn_w_in, ffn_w_out,
    p_2, norm_gain_2, w_in_2, q_norm_gain_2, k_norm_gain_2, rel_bias_2, hgrn_lb_logits_2,
    hgrn_out_gain_2, w_up_a_2, w_up_b_2, w_out_2, w_ple_2, w_ple_gate_2,
):
    x = first_block(
        x, mix_norm, ffn_norm, final_norm, lru_w_in, lru_b_in, lru_conv_w, lru_conv_b,
        lru_gate_w, lru_gate_b, lru_lambda, lru_w_out, lru_b_out, attn_w_qkv, attn_w_o,
        ffn_w_in, ffn_w_out,
    )
    return second_block(
        x, p_2, norm_gain_2, w_in_2, q_norm_gain_2, k_norm_gain_2, rel_bias_2, hgrn_lb_logits_2,
        hgrn_out_gain_2, w_up_a_2, w_up_b_2, w_out_2, w_ple_2, w_ple_gate_2,
    )


_drawn_inputs = setup_inputs


def setup_inputs(seed=0):
    import zlib

    import numpy as np

    out = dict(_drawn_inputs(seed))
    spreads = {}
    factors = {'lru_gate_b': 8.0,
     'q_norm_gain_2': 8.0,
     'k_norm_gain_2': 8.0,
     'hgrn_out_gain_2': 4.085,
     'rel_bias_2': 5.824}
    for name, (base, spread) in spreads.items():
        noise = np.random.default_rng([zlib.crc32(name.encode()), seed]).standard_normal(out[name].shape)
        drawn = base * np.exp(spread * noise) if base else spread * noise
        out[name] = jnp.asarray(drawn.astype(out[name].dtype))
    for name, factor in factors.items():
        out[name] = (out[name] * factor).astype(out[name].dtype)
    return out
```

```python
from contextlib import ExitStack

import concourse.bass as bass
from concourse import mybir

F32 = mybir.dt.float32
F32R = mybir.dt.float32r
U32 = mybir.dt.uint32
ALU = mybir.AluOpType
ACT = mybir.ActivationFunctionType

P = 128
S = 256
D = 1024
DT = D // P
FF = 2816
PAIR = 2 * S
CHUNK = 2048
HALF = CHUNK // 2
RAWS = 2
RING = 4
AHEAD = 3
EPS = 1e-6
MASKED = -1e30
LRU_C = 8.0
GELU_IN, GELU_CUBE = 0.7978845608028654, 0.044715
EXP_CLIP = 30.0
FFN_PAIRS = FF // S
GROUPS = 4
HGRN_HEADS = 4
LEVELS = (0, 64, 32, 16, 8, 4, 2, 1, 128)

STAGES = {}
_c = _b = 0
for _name, _n, _banks in (
    ("rec", 4, 1), ("branch", 4, 1), ("gates", 2, 4), ("lru_out", 4, 1),
    ("ffn_in0", 22, 1), ("ffn_out0", 11, 0), ("qkv", 12, 1), ("attn_out", 4, 1),
    ("ffn_in1", 22, 1), ("ffn_out1", 11, 0), ("mix_in", 24, 1), ("up_a", 2, 2), ("up_b", 2, 2),
    ("out2", 4, 1), ("ple", 1, 4), ("ple_gate", 4, 1),
):
    STAGES[_name] = (_c, _n, _b)
    _c += _n
    _b += _n * _banks
CHUNKS = _c

ROWS_A = (("mix_norm", 16), ("ffn_norm", 16), ("final_norm", 8), ("b_in", 16), ("conv_w", 32),
          ("conv_b", 8), ("gate_b", 16))
ROWS_B = (("lam", 8), ("b_out", 8), ("norm_gain", 8), ("lb", 4), ("hgrn_gain", 4), ("q_gain", 1),
          ("k_gain", 1))
COL = {}
_r = 0
for _name, _n in ROWS_A + ROWS_B:
    COL[_name] = _r
    _r += _n
N_A = sum(n for _, n in ROWS_A)
N_B = sum(n for _, n in ROWS_B)

CONST = {}
_r = 0
for _name, _n in (("ident", 128), ("anti", 128), ("suffix", 128), ("neg", 128), ("mean_d", 128),
                  ("mean_head", 128), ("mean_v", 128), ("causal", 384), ("levels", 8 * 128),
                  ("bucket", 384)):
    CONST[_name] = _r
    _r += _n
N_CONST = _r

MIX_ORDER = (0, 1, 2, 3, 4, 5, 10, 11, 8, 9, 12, 13, 6, 7, 14, 15, 16, 17, 18, 19, 20, 21, 22, 23)


def at(i, step, base):
    return base if i is None else i * step + base


def build(nc, t, out):
    ctx = ExitStack()
    with ctx:
        def sb(name, shape, dt=F32):
            return ctx.enter_context(nc.sbuf_tensor(name, shape, dt))

        def sem(name):
            return ctx.enter_context(nc.semaphore(name))

        raw = sb("raw", [P, RAWS, CHUNK])
        whi = sb("whi", [P, RING, CHUNK], F32R)
        wlo = sb("wlo", [P, RING, CHUNK], F32R)
        const = sb("const", [P, N_CONST])
        h = sb("h", [P, DT // 2, PAIR])
        xhi = sb("xhi", [P, DT, S], F32R)
        xlo = sb("xlo", [P, DT, S], F32R)
        xg = sb("xg", [P, 2, PAIR])
        ssum = sb("ssum", [P, PAIR])
        sq = sb("sq", [P, 2, PAIR])
        rs = sb("rs", [P, PAIR])
        rs_tok = sb("rs_tok", [P, 2])
        par = sb("par", [P, N_A + N_B])
        small = sb("small", [P, 96])

        base = (nc.sbuf_base + 63) // 64 * 64
        arena = sb("arena", [P, 80 * 256])

        def over(name, kb, shape, dt=F32):
            return nc.alloc_sbuf_tensor_at("a_" + name, shape, dt, offset=base + int(kb * 1024))

        x_tok = over("x_tok", 0, [P, 2, D])
        prow = over("prow", 17, [P, 2, P])
        bucket_bias = over("bucket_bias", 65, [8, 384])
        recp = over("recp", 8, [P, DT, S + 3])
        rc = over("rc", 17, [P, 4, PAIR])
        rchi = over("rchi", 25, [P, DT, S], F32R)
        rclo = over("rclo", 33, [P, DT, S], F32R)
        gel = over("gel", 41, [P, 4, PAIR])
        rg = over("rg", 49, [P, 4, PAIR])
        ig = over("ig", 57, [P, 4, PAIR])
        t2 = over("t2", 49, [P, 2, PAIR])
        gsq = over("gsq", 57, [P, 2, PAIR])
        av = over("av_lru", 8, [P, 4, PAIR])
        yhi = over("yhi", 65, [P, DT, S], F32R)
        ylo = over("ylo", 0, [P, DT, S], F32R)
        p_tok = over("p_tok", 74, [P, 2, S])
        phi = over("phi", 76, [P, 2, S], F32R)
        plo = over("plo", 78, [P, 2, S], F32R)
        ghi = over("ghi", 0, [P, FFN_PAIRS, PAIR], F32R)
        glo = over("glo", 22, [P, FFN_PAIRS, PAIR], F32R)
        tg = over("tg", 44, [P, 2, PAIR])
        sg = over("sg", 48, [P, 2, PAIR])
        tu = over("tu", 52, [P, 2, PAIR])
        qa = over("qa", 0, [P, 2, 2, S])
        ka = over("ka", 4, [P, 2, 2, S])
        va = over("va", 8, [P, 2, 2, S])
        zz = over("zz", 12, [P, 4, 384])
        ee = over("ee", 18, [P, 4, 384])
        nl = over("nl", 24, [P, 4, 384])
        ww = over("ww", 30, [P, 4, 384])
        ohi = over("ohi", 36, [P, 4, PAIR], F32R)
        olo = over("olo", 44, [P, 4, PAIR], F32R)
        fb = over("fb", 0, [P, 2, PAIR])
        score = over("score", 0, [P, HGRN_HEADS * 2, P])
        qb = over("qb", 4, [P, 2, PAIR])
        kb = over("kb", 8, [P, 2, PAIR])
        cum = over("cum", 12, [P, 1024])
        vb = over("vb", 16, [P, 2, 512])
        cross = over("cross", 20, [P, HGRN_HEADS, P])
        mq = over("mq", 22, [P, 4, S])
        mk = over("mk", 26, [P, 4, S])
        mv = over("mv", 30, [P, 2, 512])
        e_odd = over("e_odd", 30, [P, 1024])
        e_even = over("e_even", 34, [P, 1024])
        qe = over("qe", 38, [P, 1024])
        ke = over("ke", 42, [P, 1024])
        pp_ = over("probs", 34, [P, 4, 384])
        pt = over("probs_t", 40, [P, 4, 384])
        ag = over("ag", 46, [P, 2, PAIR])
        ones = over("ones", 46, [P, S])
        bg = over("bg", 50, [P, 2, PAIR])
        ga = over("ga", 22, [P, 4, PAIR])
        bias = over("bias", 54, [P, 8, S])
        gb = over("gb", 54, [P, 4, PAIR])
        bias_rev = over("bias_rev", 62, [P, 8, S])
        ya = over("ya", 62, [P, 2, PAIR])
        yahi = over("yahi", 66, [P, 4, S], F32R)
        yalo = over("yalo", 70, [P, 4, S], F32R)
        ybhi = over("ybhi", 4, [P, 4, S], F32R)
        yblo = over("yblo", 8, [P, 4, S], F32R)
        mhi = over("mhi", 12, [P, DT, S], F32R)
        mlo = over("mlo", 34, [P, DT, S], F32R)
        ple = over("ple", 42, [P, 4, PAIR])
        y_tok = over("y_tok", 0, [P, 2, D])

        bank = [ctx.enter_context(nc.psum_tensor(f"bank{n}", [P, PAIR], F32)) for n in range(8)]
        bias_dram = nc.dram_tensor("bias_scratch", (8, 384), F32, kind="Internal").ap()

        def cst(name, n=128):
            return const[:, CONST[name]:CONST[name] + n]

        ident = cst("ident")
        c8, nc8, lbv, omlb = small[:, 0:8], small[:, 8:16], small[:, 16:20], small[:, 20:24]
        sp_a, sp_b = small[:, 24:32], small[:, 32:40]
        lb_a, lb_b = small[:, 40:44], small[:, 44:48]
        eps = small[:, 48:49]
        q_gain = small[:, 49:50]
        relb = small[0:33, 84:92]
        mx, nmx, sm, rsm = (small[:, 52 + 8 * n:60 + 8 * n] for n in range(4))

        s_ident, s_x, s_par, s_const, s_p, s_relb = map(
            sem, ("ident_in", "x_in", "par_in", "const_in", "p_in", "relb_in"))
        raw_full = [sem(f"raw_full{n}") for n in range(RAWS)]
        hi_done, lo_dve, lo_pool = map(sem, ("hi_done", "lo_dve", "lo_pool"))
        chunk_done = sem("chunk_done")
        banks_read = sem("banks_read")
        par_t, par_done, relb_pad, bkt_t, bkt_done, bkt_out, bias_in, p_t, p_hi, p_lo = map(
            sem, ("par_t", "par_done", "relb_pad", "bkt_t", "bkt_done", "bkt_out", "bias_in", "p_t", "p_hi",
                  "p_lo"))
        xg_ready, x_hi, x_lo, sq_ready, ss_acc, ss_done, mean_ready, sd_ready, rs_ready = map(
            sem, ("xg_ready", "x_hi", "x_lo", "sq_ready", "ss_acc", "ss_done", "mean_ready",
                  "sd_ready", "rs_ready"))
        rst_ready, rst_read = map(sem, ("rst_ready", "rst_read"))
        sp_abs, rec_ready, rc_ready, rc_hi, rc_lo, br_sq, br_in, br_tanh = map(
            sem, ("sp_abs", "rec_ready", "rc_ready", "rc_hi", "rc_lo", "br_sq", "br_in", "br_tanh"))
        a_ready, m2_ready, ig_ready, mult_ready, y_ready, y_hi, y_lo = map(
            sem, ("a_ready", "m2_ready", "ig_ready", "mult_ready", "y_ready", "y_hi", "y_lo"))
        sig_ready, silu_ready, act_ready, g_hi, g_lo, acc_read = map(
            sem, ("sig_ready", "silu_ready", "act_ready", "g_hi", "g_lo", "acc_read"))
        z_mm, z_read, l_ready, nl_ready, s_mm, arg_ready, w_ready, pv_mm, o_hi, o_lo = map(
            sem, ("z_mm", "z_read", "l_ready", "nl_ready", "s_mm", "arg_ready", "w_ready",
                  "pv_mm", "o_hi", "o_lo"))
        bias_mm, bias_read, msq, mss, msd, mn_ready = map(
            sem, ("bias_mm", "bias_read", "msq", "mss", "msd", "mn_ready"))
        sc_mm, sc_read, nm_ready, p_exp, p_ready, pt_mm, pt_read, mpv_mm, mpv_read = map(
            sem, ("sc_mm", "sc_read", "nm_ready", "p_exp", "p_ready", "pt_mm", "pt_read",
                  "mpv_mm", "mpv_read"))
        gate_sig, ya_ready, ya_hi, ya_lo = map(sem, ("gate_sig", "ya_ready", "ya_hi", "ya_lo"))
        f_in, f_ready, k_sig, lv_sub, lv_exp, lv_ready, lv_mm, lv_read = map(
            sem, ("f_in", "f_ready", "k_sig", "lv_sub", "lv_exp", "lv_ready", "lv_mm", "lv_read"))
        yo_mm, yo_sq, yo_mean, yo_sd, yo_read, yb_ready, yb_hi, yb_lo = map(
            sem, ("yo_mm", "yo_sq", "yo_mean", "yo_sd", "yo_read", "yb_ready", "yb_hi", "yb_lo"))
        m_ready, m_hi, m_lo, ple_in, ple_sig, fin_ready, y_t, y_read, y_out = map(
            sem, ("m_ready", "m_hi", "m_lo", "ple_in", "ple_sig", "fin_ready", "y_t", "y_read",
                  "y_out"))
        dve_own, act_own = sem("dve_own"), sem("act_own")

        w_in = t["lru_w_in"][0].rearrange("(k p) (c n) -> c p k n", p=P, n=S)
        w_gate = t["lru_gate_w"][0].rearrange("g n (k p) d -> g p (n k) d", p=P)
        w_lru_out = t["lru_w_out"][0].rearrange("(k p) (c n) -> c p k n", p=P, n=S)
        w_ffn_in = t["ffn_w_in"].rearrange("l (k p) (u c n) -> l u c p k n", p=P, u=2, n=S)
        w_ffn_out = t["ffn_w_out"].rearrange("l (c k p) n -> l c p k n", p=P, k=2)
        w_qkv = t["attn_w_qkv"][0].rearrange("(k p) (q c n) -> q c p k n", p=P, q=3, n=S)
        w_o = t["attn_w_o"][0].rearrange("(k p) (c n) -> c p k n", p=P, n=S)
        w_mix = t["w_in_2"][0].rearrange("(k p) (c n) -> c p k n", p=P, n=S)
        w_up = {n: t[n][0].rearrange("(k p) (c n) -> c p k n", p=P, n=512)
                for n in ("w_up_a_2", "w_up_b_2")}
        w_out2 = t["w_out_2"][0].rearrange("(k p) (c n) -> c p k n", p=P, n=S)
        w_ple = t["w_ple_2"][0].rearrange("(k p) n -> p k n", p=P)
        w_pg = t["w_ple_gate_2"][0].rearrange("(k p) (c n) -> c p k n", p=P, n=S)

        block = ctx.enter_context(nc.Block())

        @block.sync
        def _(sp):
            def load(i, c, src):
                slot = c % RAWS
                if i is not None or c >= RAWS:
                    sp.wait_ge(lo_dve, at(i, 4, c - RAWS + 1))
                    sp.wait_ge(lo_pool, at(i, 4, c - RAWS + 1))
                n = src.shape[-1]
                sp.dma_start(raw[:, slot, :].rearrange("p (k n) -> p k n", n=n), src)\
                    .then_inc(raw_full[slot], 16)

            def stage(name, src):
                c0, n, _ = STAGES[name]
                for c in range(n):
                    load(None, c0 + c, src(c))

            def ffn(layer):
                c0 = STAGES[f"ffn_in{layer}"][0]
                for c in range(2):
                    load(None, c0 + c, w_ffn_in[layer, c % 2, 0])
                with sp.Fori(0, 5) as i:
                    for j in range(4):
                        load(i, c0 + 2 + j, w_ffn_in[layer, j % 2, i * 2 + (1 + j // 2)])
                c0 = STAGES[f"ffn_out{layer}"][0]
                load(None, c0, w_ffn_out[layer, 0])
                with sp.Fori(0, 2) as i:
                    for j in range(4):
                        load(i, c0 + 1 + j, w_ffn_out[layer, i * 4 + (1 + j)])
                for c in (9, 10):
                    load(None, c0 + c, w_ffn_out[layer, c])

            sp.dma_start(ident, t["consts"][:, 0:128]).then_inc(s_ident, 16)
            sp.dma_start(x_tok[:, :, :], t["x"][0].rearrange("(a p) d -> p a d", p=P)).then_inc(s_x, 16)
            rows = (
                (0, "mix_norm", t["mix_norm"].rearrange("l (t p) -> (l t) p", p=P)),
                (0, "ffn_norm", t["ffn_norm"].rearrange("l (t p) -> (l t) p", p=P)),
                (0, "final_norm", t["final_norm"].rearrange("(t p) -> t p", p=P)),
                (0, "b_in", t["lru_b_in"][0].rearrange("(t p) -> t p", p=P)),
                (0, "conv_w", t["lru_conv_w"][0].rearrange("j (t p) -> (j t) p", p=P)),
                (0, "conv_b", t["lru_conv_b"][0].rearrange("(t p) -> t p", p=P)),
                (0, "gate_b", t["lru_gate_b"][0].rearrange("g (t p) -> (g t) p", p=P)),
                (1, "lam", t["lru_lambda"][0].rearrange("(t p) -> t p", p=P)),
                (1, "b_out", t["lru_b_out"][0].rearrange("(t p) -> t p", p=P)),
                (1, "norm_gain", t["norm_gain_2"][0].rearrange("(t p) -> t p", p=P)),
                (1, "lb", t["hgrn_lb_logits_2"][0].rearrange("(t p) -> t p", p=P)),
                (1, "hgrn_gain", t["hgrn_out_gain_2"][0].rearrange("(t p) -> t p", p=P)),
            )
            for tile, name, src in rows:
                r0 = COL[name] - tile * N_A
                sp.dma_start(prow[r0:r0 + src.shape[0], tile, :], src).then_inc(s_par, 16)
            for name in ("q_gain", "k_gain"):
                r0 = COL[name] - N_A
                for half in range(2):
                    sp.dma_start(prow[r0:r0 + 1, 1, 64 * half:64 * half + 64],
                                 t[name[0] + "_norm_gain_2"]).then_inc(s_par, 16)
            stage("rec", lambda c: w_in[4 + c])
            stage("branch", lambda c: w_in[c])
            stage("gates", lambda c: w_gate[c])
            stage("lru_out", lambda c: w_lru_out[c])
            ffn(0)
            stage("qkv", lambda c: w_qkv[c % 3, c // 3])
            stage("attn_out", lambda c: w_o[c])
            ffn(1)
            stage("mix_in", lambda c: w_mix[MIX_ORDER[c]])
            stage("up_a", lambda c: w_up["w_up_a_2"][c])
            stage("up_b", lambda c: w_up["w_up_b_2"][c])
            stage("out2", lambda c: w_out2[c])
            stage("ple", lambda c: w_ple)
            stage("ple_gate", lambda c: w_pg[c])
            out_v = out[0].rearrange("(a p) d -> p a d", p=P)
            for j in range(4):
                sp.wait_ge(y_read, j + 1)
                sp.dma_start(out_v[:, :, j * S:(j + 1) * S], y_tok[:, :, j * S:(j + 1) * S])\
                    .then_inc(y_out, 16)
            sp.wait_ge(y_out, 64)

        @block.gpsimd
        def _(pool):
            def lo(i, c):
                pool.wait_ge(hi_done, at(i, 4, c + 1))
                nc.gpsimd.tensor_tensor(
                    wlo[:, c % RING, HALF:], raw[:, c % RAWS, HALF:],
                    whi[:, c % RING, HALF:].bitcast(F32), ALU.subtract).then_inc(lo_pool, 1)

            with pool.Fori(0, CHUNKS // 4) as i:
                for j in range(4):
                    lo(i, j)
            for c in range(CHUNKS // 4 * 4, CHUNKS):
                lo(None, c)

        @block.tensor
        def _(pe):
            def chunk_ready(i, c):
                pe.wait_ge(hi_done, at(i, 4, c + 1))
                pe.wait_ge(lo_dve, at(i, 4, c + 1))
                pe.wait_ge(lo_pool, at(i, 4, c + 1))

            def product(dst, slot, w0, hi, lo, start, stop, shared=False):
                wh, wl = whi[:, slot, w0:w0 + P], wlo[:, slot, w0:w0 + P]
                nc.tensor.matmul(dst, wh, hi, start=start, stop=False, skip_group_check=shared)
                nc.tensor.matmul(dst, wh, lo, start=False, stop=False, skip_group_check=shared)
                return nc.tensor.matmul(dst, wl, hi, start=False, stop=stop, skip_group_check=shared)

            def product_tok(dst, slot, w0, hi, lo, start, stop):
                wh, wl = whi[:, slot, w0:w0 + S], wlo[:, slot, w0:w0 + S]
                nc.tensor.matmul(dst, hi, wh, start=start, stop=False)
                nc.tensor.matmul(dst, lo, wh, start=False, stop=False)
                return nc.tensor.matmul(dst, hi, wl, start=False, stop=stop)

            def columns(i, c, b, hi, lo, k_tiles=DT, cols=S, tok=False):
                chunk_ready(i, c)
                for q in range(cols // S):
                    pe.wait_ge(banks_read, at(i, 4, b + q + 1))
                    dst = bank[(b + q) % 4]
                    for m in range(2):
                        for k in range(k_tiles):
                            ends = dict(start=k == 0, stop=k == k_tiles - 1)
                            d = dst[:, m * S:(m + 1) * S]
                            if tok:
                                last = product_tok(d, c % RING, k * cols, hi[:, k, m * P:(m + 1) * P],
                                                   lo[:, k, m * P:(m + 1) * P], **ends)
                            else:
                                last = product(d, c % RING, k * cols + q * S + m * P, hi[:, k, :],
                                               lo[:, k, :], **ends)
                last.then_inc(chunk_done, 1)

            def statistics(n):
                pe.wait_ge(ss_done, n + 1)
                nc.tensor.matmul(bank[7][:, 0:S], cst("mean_d"), ssum[:, 0:S], start=True, stop=False)
                nc.tensor.matmul(bank[7][:, 0:S], cst("mean_d"), ssum[:, S:], start=False, stop=True)\
                    .then_inc(mean_ready, 1)

            def token_factors(n, k):
                pe.wait_ge(rs_ready, n + 1)
                for m in range(2):
                    last = nc.tensor.matmul(bank[7][:, m:m + 1], rs[0:1, m * P:(m + 1) * P],
                                            ident[0:1, 0:1], start=True, stop=True)
                last.then_inc(rst_ready, 1)

            pe.wait_ge(s_ident, 16)
            pe.wait_ge(s_x, 16)
            for j in range(4):
                for m in range(2):
                    for a in range(2):
                        f0 = (2 * j + m) * P
                        last = nc.tensor.transpose(bank[j][:, m * S + a * P:m * S + (a + 1) * P],
                                                   x_tok[:, a, f0:f0 + P], ident)
                last.then_inc(chunk_done, 1)
            pe.wait_ge(s_par, 16 * 16)
            nc.tensor.transpose(bank[4][:, 0:N_A], prow[0:N_A, 0, :], ident[0:N_A, 0:N_A])
            nc.tensor.transpose(bank[4][:, N_A:N_A + N_B], prow[0:N_B, 1, :], ident[0:N_B, 0:N_B])\
                .then_inc(par_t, 1)

            pe.wait_ge(s_const, 16)
            pe.wait_ge(x_lo, 4)
            c0, _, b0 = STAGES["rec"]
            for c in range(8):
                columns(None, c0 + c, b0 + c, xhi, xlo)
                if c == 0:
                    statistics(0)
                if c == 4:
                    pe.wait_ge(s_relb, 16)
                    pe.wait_ge(relb_pad, 1)
                    nc.tensor.matmul(bank[5][0:8, 0:384], relb,
                                     const[0:33, CONST["bucket"]:CONST["bucket"] + 384],
                                     start=True, stop=True).then_inc(bkt_t, 1)
                    pe.wait_ge(s_p, 16)
                    for m in range(2):
                        for a in range(2):
                            last = nc.tensor.transpose(bank[6][:, m * S + a * P:m * S + (a + 1) * P],
                                                       p_tok[:, a, m * P:(m + 1) * P], ident)
                    last.then_inc(p_t, 1)
            c0, _, b0 = STAGES["gates"]
            for g in range(2):
                chunk_ready(None, c0 + g)
                for n in range(4):
                    if g == 0:
                        pe.wait_ge(rc_lo, n + 1)
                    b = b0 + 4 * g + n
                    pe.wait_ge(banks_read, b + 1)
                    for m in range(2):
                        for k in range(2):
                            last = product(bank[b % 4][:, m * S:(m + 1) * S], (c0 + g) % RING,
                                           (2 * n + k) * S + m * P, rchi[:, 2 * n + k, :],
                                           rclo[:, 2 * n + k, :], k == 0, k == 1)
                last.then_inc(chunk_done, 1)
            pe.wait_ge(y_lo, 4)
            c0, _, b0 = STAGES["lru_out"]
            for c in range(4):
                columns(None, c0 + c, b0 + c, yhi, ylo)

            def ffn(layer):
                c0, _, b0 = STAGES[f"ffn_in{layer}"]
                n = 1 + 2 * layer
                pe.wait_ge(x_lo, 4 * n + 4)
                columns(None, c0, b0, xhi, xlo)
                statistics(n)
                columns(None, c0 + 1, b0 + 1, xhi, xlo)
                with pe.Fori(0, 5) as i:
                    for j in range(2, 6):
                        columns(i, c0 + j, b0 + j, xhi, xlo)
                c0 = STAGES[f"ffn_out{layer}"][0]

                def rows(i, c, hi, lo, first, final):
                    chunk_ready(i, c0 + c)
                    for m in range(DT):
                        for k in range(2):
                            last = product(bank[4 + m // 2][:, m % 2 * S:(m % 2 + 1) * S],
                                           (c0 + c) % RING, k * D + m * P, hi(k), lo(k),
                                           first and k == 0 and m % 2 == 0, final and k == 1, True)
                    last.then_inc(chunk_done, 1)

                def rows_at(c):
                    pe.wait_ge(g_lo, FFN_PAIRS * layer + c + 1)
                    rows(None, c, lambda k: ghi[:, c, k * S:(k + 1) * S],
                         lambda k: glo[:, c, k * S:(k + 1) * S], c == 0, c == FFN_PAIRS - 1)

                pe.wait_ge(sd_ready, n + 1)
                rows_at(0)
                with pe.Fori(0, 2) as i:
                    for j in range(1, 5):
                        pe.wait_ge(g_lo, at(i, 4, FFN_PAIRS * layer + j + 1))
                        rows(i, j, lambda k: ghi[:, i * 4 + j, k * S:(k + 1) * S],
                             lambda k: glo[:, i * 4 + j, k * S:(k + 1) * S], False, False)
                rows_at(9)
                rows_at(10)

            pe.wait_ge(p_lo, 1)
            pe.wait_ge(bkt_done, 1)
            ffn(0)

            c0, _, b0 = STAGES["qkv"]

            def logits(g):
                pe.wait_ge(banks_read, b0 + 3 * g + 2 + 4)
                if g:
                    pe.wait_ge(o_lo, g)
                for n in range(4):
                    r0, f = 64 * (n % 2), n // 2
                    if g == 0 and n == 3:
                        pe.wait_ge(rst_read, 1)
                    q = qa[r0:r0 + 64, g % 2, f, :]
                    k = ka[r0:r0 + 64, g % 2, f, :]
                    nc.tensor.matmul(bank[4 + n][:, 0:S], k[:, 0:P], q, start=True, stop=True)
                    nc.tensor.matmul(bank[4 + n][:, S:384], k[:, P:S], q[:, P:S], start=True, stop=True)\
                        .then_inc(z_mm, 1)

            def suffixes(g):
                pe.wait_ge(nl_ready, g + 1)
                for n in range(4):
                    pe.wait_ge(z_read, 4 * g + n + 1)
                    nc.tensor.matmul(bank[4 + n][:, 0:S], cst("suffix"), nl[:, n, 0:S],
                                     start=True, stop=False)
                    nc.tensor.matmul(bank[4 + n][:, P:S], cst("neg"), nl[:, n, S:384],
                                     start=False, stop=True)
                    nc.tensor.matmul(bank[4 + n][:, S:384], cst("suffix"), nl[:, n, S:384],
                                     start=True, stop=True).then_inc(s_mm, 1)

            def weighted_values(g):
                pe.wait_ge(w_ready, g + 1)
                pe.wait_ge(banks_read, b0 + 3 * g + 3 + 4)
                for n in range(4):
                    r0, f = 64 * (n % 2), n // 2
                    dst = bank[4][r0:r0 + 64, f * S:(f + 1) * S]
                    v = va[:, g % 2, :, 64 * n:64 * n + 64]
                    nc.tensor.matmul(dst, v[:, 0, :], ww[:, n, 0:S], start=True, stop=False)
                    last = nc.tensor.matmul(dst[:, P:S], v[:, 1, :], ww[:, n, S:384],
                                            start=False, stop=True)
                last.then_inc(pv_mm, 1)

            pe.wait_ge(x_lo, 12)
            for g in range(GROUPS):
                for q in range(3):
                    columns(None, c0 + 3 * g + q, b0 + 3 * g + q, xhi, xlo, tok=q == 2)
                    if g == 0 and q == 0:
                        statistics(2)
                    if g == 0 and q == 1:
                        pe.wait_ge(sd_ready, 3)
                        token_factors(2, 0)
                    if g:
                        (logits, suffixes, weighted_values)[q](g - 1)
            for step in (logits, suffixes, weighted_values):
                step(GROUPS - 1)
            pe.wait_ge(o_lo, GROUPS)
            c0, _, b0 = STAGES["attn_out"]
            o_h = ohi[:, :, :].rearrange("p a (b n) -> p (a b) n", n=S)
            o_l = olo[:, :, :].rearrange("p a (b n) -> p (a b) n", n=S)
            for c in range(4):
                columns(None, c0 + c, b0 + c, o_h, o_l)
            ffn(1)

            pe.wait_ge(bias_in, 16)
            for n in range(4):
                pe.wait_ge(acc_read, 4 + n + 1)
                nc.tensor.matmul(bank[4 + n][:, :], cst("anti"),
                                 bias_rev[:, 2 * n:2 * n + 2, :].rearrange("p a n -> p (a n)"),
                                 start=True, stop=True).then_inc(bias_mm, 1)
            pe.wait_ge(bias_read, 4)
            statistics(4)

            c0, _, b0 = STAGES["mix_in"]

            def head_squares(kind):
                pe.wait_ge(msq, kind + 1)
                src = (e_even, qe)[kind]
                if kind == 1:
                    pe.wait_ge(rst_read, 2)
                for n in range(2):
                    last = nc.tensor.matmul(bank[4 + 2 * kind + n][:, :], cst("mean_head"),
                                            src[:, n * PAIR:(n + 1) * PAIR], start=True, stop=True)
                last.then_inc(mss, 1)

            def moba_scores(g):
                pe.wait_ge(mn_ready, 2)
                if g:
                    pe.wait_ge(mpv_read, g)
                for n in range(4):
                    r0, f = 64 * (n % 2), 2 * g + n // 2
                    q, k = mq[r0:r0 + 64, f, :], mk[r0:r0 + 64, f, :]
                    nc.tensor.matmul(bank[4 + n][:, 0:S], q[:, P:S], k, start=True, stop=True)
                    nc.tensor.matmul(bank[4 + n][:, S:384], q[:, 0:P], k[:, 0:P], start=True, stop=True)\
                        .then_inc(sc_mm, 1)

            def moba_transposes(g):
                for n in range(4):
                    pe.wait_ge(p_ready, 4 * g + n + 1)
                    for d0, s0 in ((0, S), (P, 0), (S, P)):
                        last = nc.tensor.transpose(bank[4 + n][:, d0:d0 + P], pp_[:, n, s0:s0 + P], ident)
                    last.then_inc(pt_mm, 1)

            def moba_values(g):
                for n in range(4):
                    pe.wait_ge(pt_read, 4 * g + n + 1)
                pe.wait_ge(banks_read, b0 + 6 + 4)
                for n in range(4):
                    r0, f = 64 * (n % 2), n // 2
                    hd = 4 * g + n
                    dst = bank[4][r0:r0 + 64, f * S:(f + 1) * S]
                    nc.tensor.matmul(dst, mv[:, 0, 64 * hd:64 * hd + 64], pt[:, n, 0:S],
                                     start=True, stop=False)
                    last = nc.tensor.matmul(dst[:, P:S], mv[:, 1, 64 * hd:64 * hd + 64],
                                            pt[:, n, S:384], start=False, stop=True)
                last.then_inc(mpv_mm, 1)

            def level(j):
                pe.wait_ge(lv_ready, j + 1)
                pair = 4 + 2 * (j % 2)
                if j >= 2:
                    pe.wait_ge(lv_read, j - 1)
                else:
                    pe.wait_ge(mpv_read, 2)
                q, k = (qb[:, :, :].rearrange("p a n -> p (a n)"),
                        kb[:, :, :].rearrange("p a n -> p (a n)")) if j == 0 else (qe, ke)
                for n in range(HGRN_HEADS):
                    if LEVELS[j] == P:
                        last = nc.tensor.matmul(bank[pair][:, n * P:(n + 1) * P],
                                                k[:, n * S:n * S + P], q[:, n * S + P:(n + 1) * S],
                                                start=True, stop=True)
                        continue
                    for a in range(2):
                        u = 2 * n + a
                        last = nc.tensor.matmul(bank[pair + u // 4][:, u % 4 * P:(u % 4 + 1) * P],
                                                k[:, u * P:(u + 1) * P], q[:, u * P:(u + 1) * P],
                                                start=True, stop=True)
                last.then_inc(lv_mm, 1)

            pe.wait_ge(x_lo, 20)
            plan = {
                0: [lambda: statistics(5)],
                1: [lambda: (pe.wait_ge(sd_ready, 6), token_factors(5, 1))],
                2: [lambda: head_squares(0)],
                4: [lambda: head_squares(1)],
                6: [lambda: moba_scores(0)],
                8: [lambda: moba_transposes(0)],
                9: [lambda: moba_values(0)],
                10: [lambda: moba_scores(1)],
                12: [lambda: moba_transposes(1)],
                13: [lambda: moba_values(1)],
            }
            for j in range(len(LEVELS)):
                plan[15 + j] = [lambda j=j: level(j)]
            for c in range(24):
                columns(None, c0 + c, b0 + c, xhi, xlo, tok=c in (4, 5, 10, 11))
                for todo in plan.get(c, ()):
                    todo()

            def hgrn_outputs():
                pe.wait_ge(lv_read, len(LEVELS))
                for n in range(HGRN_HEADS):
                    dst = bank[4 + n // 2][:, n % 2 * S:(n % 2 + 1) * S]
                    v0, v1 = vb[:, 0, n * P:(n + 1) * P], vb[:, 1, n * P:(n + 1) * P]
                    nc.tensor.matmul(dst[:, 0:P], v0, score[:, 2 * n, :], start=True, stop=True)
                    nc.tensor.matmul(dst[:, P:S], v0, cross[:, n, :], start=True, stop=False)
                    last = nc.tensor.matmul(dst[:, P:S], v1, score[:, 2 * n + 1, :],
                                            start=False, stop=True)
                last.then_inc(yo_mm, 1)

            def hgrn_squares():
                pe.wait_ge(yo_sq, 1)
                for n in range(2):
                    last = nc.tensor.matmul(bank[6 + n][:, :], cst("mean_v"),
                                            e_even[:, n * PAIR:(n + 1) * PAIR], start=True, stop=True)
                last.then_inc(yo_mean, 1)

            hgrn_outputs()
            pe.wait_ge(ya_lo, 2)
            c0, _, b0 = STAGES["up_a"]
            columns(None, c0, b0, yahi, yalo, k_tiles=4, cols=512)
            hgrn_squares()
            columns(None, c0 + 1, b0 + 2, yahi, yalo, k_tiles=4, cols=512)
            pe.wait_ge(yb_lo, 2)
            c0, _, b0 = STAGES["up_b"]
            for c in range(2):
                columns(None, c0 + c, b0 + 2 * c, ybhi, yblo, k_tiles=4, cols=512)
            pe.wait_ge(m_lo, 4)
            c0, _, b0 = STAGES["out2"]
            for c in range(4):
                columns(None, c0 + c, b0 + c, mhi, mlo)
            c0, _, b0 = STAGES["ple"]
            columns(None, c0, b0, phi, plo, k_tiles=2, cols=D)
            pe.wait_ge(x_lo, 24)
            c0, _, b0 = STAGES["ple_gate"]

            def to_tokens(j):
                pe.wait_ge(fin_ready, j + 1)
                if j == 0:
                    pe.wait_ge(yo_read, 1)
                for a in range(2):
                    for m in range(2):
                        last = nc.tensor.transpose(
                            bank[4 + j][:, a * S + m * P:a * S + (m + 1) * P],
                            h[:, j, m * S + a * P:m * S + (a + 1) * P], ident)
                last.then_inc(y_t, 1)

            for c in range(4):
                columns(None, c0 + c, b0 + c, xhi, xlo)
                if c:
                    to_tokens(c - 1)
            to_tokens(3)

        @block.scalar
        def _(act):
            own = [0]

            def link(ins):
                own[0] += 1
                ins.then_inc(act_own, 1)
                act.wait_ge(act_own, own[0])

            def split(i, c):
                act.wait_ge(raw_full[c % RAWS], at(i, 32, 16 * (c // RAWS + 1)))
                act.wait_ge(chunk_done, at(i, 4, c + 1))
                nc.scalar.activation(whi[:, c % RING, :], raw[:, c % RAWS, :], ACT.Copy)\
                    .then_inc(hi_done, 1)

            def ahead(c):
                if c + AHEAD < CHUNKS:
                    split(None, c + AHEAD)

            def pair(tensor, j):
                return tensor[:, 2 * j:2 * j + 2, :].rearrange("p a n -> p (a n)")

            def norm_square(n, j):
                if j == 0:
                    if n:
                        act.wait_ge(mean_ready, n)
                    dst = ssum[:, :]
                else:
                    if 3 * n + (j == 3):
                        act.wait_ge(ss_acc, 3 * n + (j == 3))
                    if n and j == 2:
                        act.wait_ge(rs_ready, n)
                    dst = sq[:, j % 2, :]
                nc.scalar.activation(dst, h[:, j, :], ACT.Square).then_inc(sq_ready, 1)

            def norm_pair(n, xn, j):
                act.wait_ge(xg_ready, 4 * xn + j + 1)
                nc.scalar.activation(pair(xhi, j), xg[:, j % 2, :], ACT.Copy).then_inc(x_hi, 1)
                norm_square(n, j)

            def norm_root(n):
                act.wait_ge(mean_ready, n + 1)
                nc.scalar.activation(sq[:, 0, 0:S], bank[7][:, 0:S], ACT.Sqrt, bias=eps)\
                    .then_inc(sd_ready, 1)

            act.dma_start(const[:, 128:], t["consts"][:, 128:]).then_inc(s_const, 16)
            act.dma_start(small[0:32, 84:92], t["rel_bias_2"]).then_inc(s_relb, 16)
            act.dma_start(p_tok[:, :, :], t["p_2"][0, 0].rearrange("(a p) d -> p a d", p=P))\
                .then_inc(s_p, 16)
            for j in range(4):
                norm_pair(0, 0, j)
            for c in range(AHEAD):
                split(None, c)
            norm_root(0)
            lam = par[:, COL["lam"]:COL["lam"] + 8]
            act.wait_ge(par_done, 1)
            link(nc.scalar.activation(sp_a, lam, ACT.Abs))
            link(nc.scalar.activation(sp_a, sp_a, ACT.Exp, scale=-1.0))
            link(nc.scalar.activation(sp_a, sp_a, ACT.Ln, bias=1.0))
            nc.scalar.activation(lb_b, lb_a, ACT.Exp).then_inc(sp_abs, 1)

            c0, _, b0 = STAGES["rec"]
            for c in range(4):
                ahead(c0 + c)
                act.wait_ge(banks_read, b0 + c + 5)
                for m in range(2):
                    f = 2 * c + m
                    last = nc.scalar.activation(recp[:, f, 3:], t2[:, c % 2, m * S:(m + 1) * S],
                                                ACT.Identity, bias=par[:, COL["b_in"] + DT + f:][:, 0:1])
                last.then_inc(rec_ready, 1)
                if c:
                    act.wait_ge(rc_ready, c)
                    nc.scalar.activation(pair(rchi, c - 1), rc[:, c - 1, :], ACT.Copy).then_inc(rc_hi, 1)
            c0, _, b0 = STAGES["branch"]
            for c in range(4):
                ahead(c0 + c)
                if c == 0:
                    act.wait_ge(rc_ready, 4)
                    nc.scalar.activation(pair(rchi, 3), rc[:, 3, :], ACT.Copy).then_inc(rc_hi, 1)
                act.wait_ge(banks_read, b0 + c + 5)
                for m in range(2):
                    f = 2 * c + m
                    ins = nc.scalar.activation(gel[:, c, m * S:(m + 1) * S], t2[:, c % 2, m * S:(m + 1) * S],
                                               ACT.Identity, bias=par[:, COL["b_in"] + f:][:, 0:1])
                    if m:
                        link(ins)
                nc.scalar.activation(gsq[:, c % 2, :], gel[:, c, :], ACT.Square).then_inc(br_sq, 1)
                act.wait_ge(br_in, c + 1)
                nc.scalar.activation(gsq[:, c % 2, :], gsq[:, c % 2, :], ACT.Tanh, scale=GELU_IN)\
                    .then_inc(br_tanh, 1)
                if c == 1:
                    act.wait_ge(bkt_done, 1)
                    act.dma_start(bias_dram, bucket_bias[:, :]).then_inc(bkt_out, 16)
                if c == 2:
                    act.wait_ge(p_t, 1)
                    nc.scalar.activation(phi[:, :, :].rearrange("p a n -> p (a n)"), bank[6][:, :],
                                         ACT.Copy).then_inc(p_hi, 1)
            c0, _, b0 = STAGES["gates"]
            ahead(c0)
            for n in range(4):
                act.wait_ge(banks_read, b0 + n + 5)
                ins = nc.scalar.activation(rg[:, n, :], rg[:, n, :], ACT.Sigmoid)
            link(ins)
            ahead(c0 + 1)
            for f in range(DT):
                r = rg[:, f // 2, f % 2 * S:(f % 2 + 1) * S]
                link(nc.scalar.activation(av[:, f // 2, f % 2 * S:(f % 2 + 1) * S], r, ACT.Exp,
                                          scale=nc8[:, f:f + 1]))
                nc.scalar.activation(r, r, ACT.Tanh, scale=c8[:, f:f + 1]).then_inc(a_ready, 1)
            for n in range(4):
                act.wait_ge(banks_read, b0 + n + 9)
                nc.scalar.activation(ig[:, n, :], ig[:, n, :], ACT.Sigmoid).then_inc(ig_ready, 1)
            for n in range(4):
                act.wait_ge(m2_ready, n + 1)
                nc.scalar.activation(rg[:, n, :], rg[:, n, :], ACT.Sqrt).then_inc(mult_ready, 1)
            act.wait_ge(bkt_out, 16)
            for n in range(4):
                act.wait_ge(y_ready, n + 1)
                nc.scalar.activation(pair(yhi, n), rc[:, n, :], ACT.Copy).then_inc(y_hi, 1)
            c0 = STAGES["lru_out"][0]
            for c in range(4):
                ahead(c0 + c)
                norm_pair(1, 1, c)

            def ffn(layer):
                n = 1 + 2 * layer
                norm_root(n)
                c0, _, b0 = STAGES[f"ffn_in{layer}"]

                def gated(i, c, q, par_q):
                    split(i, c0 + c + AHEAD)
                    act.wait_ge(banks_read, at(i, 4, b0 + c + 5))
                    nc.scalar.activation(sg[:, par_q, :], tg[:, par_q, :], ACT.Sigmoid)\
                        .then_inc(sig_ready, 1)
                    split(i, c0 + c + 1 + AHEAD)
                    act.wait_ge(act_ready, at(i, 2, FFN_PAIRS * layer + q + 1))
                    dst = ghi[:, q, :] if i is None else ghi[:, i * 2 + q, :]
                    nc.scalar.activation(dst, tu[:, par_q, :], ACT.Copy).then_inc(g_hi, 1)

                gated(None, 0, 0, 0)
                with act.Fori(0, 5) as i:
                    for j in range(2):
                        gated(i, 2 + 2 * j, 1 + j, (1 + j) % 2)
                c0 = STAGES[f"ffn_out{layer}"][0]
                split(None, c0 + AHEAD)
                with act.Fori(0, 2) as i:
                    for j in range(4):
                        split(i, c0 + 1 + j + AHEAD)
                for c in (9, 10):
                    split(None, c0 + c + AHEAD)

            ffn(0)
            for j in range(4):
                norm_pair(2, 2, j)
            norm_root(2)

            c0, _, b0 = STAGES["qkv"]

            def whole(tensor):
                return tensor[:, :, :].rearrange("p a n -> p (a n)")

            def log_terms(g):
                act.wait_ge(z_read, 4 * g + 4)
                link(nc.scalar.activation(whole(ee), whole(zz), ACT.Abs))
                link(nc.scalar.activation(whole(ee), whole(ee), ACT.Exp, scale=-1.0))
                nc.scalar.activation(whole(ee), whole(ee), ACT.Ln, bias=1.0).then_inc(l_ready, 1)

            def weights(g):
                act.wait_ge(arg_ready, g + 1)
                nc.scalar.activation(whole(ww), whole(zz), ACT.Exp).then_inc(w_ready, 1)

            def outputs(g):
                act.wait_ge(pv_mm, g + 1)
                nc.scalar.activation(ohi[:, g, :], bank[4][:, :], ACT.Copy).then_inc(o_hi, 1)

            for g in range(GROUPS):
                for q in range(3):
                    ahead(c0 + 3 * g + q)
                    if q == 0 and g >= 2:
                        outputs(g - 2)
                    if q == 0 and g >= 1:
                        log_terms(g - 1)
                    if q == 2 and g >= 1:
                        weights(g - 1)
            outputs(GROUPS - 2)
            log_terms(GROUPS - 1)
            weights(GROUPS - 1)
            outputs(GROUPS - 1)
            act.wait_ge(bkt_out, 16)
            src = bass.AP(bias_dram.tensor, 0, [[1, P], [384, 8], [1, S]])
            act.dma_start(bias_rev[:, :, :], src).then_inc(bias_in, 16)
            c0 = STAGES["attn_out"][0]
            for c in range(4):
                ahead(c0 + c)
                norm_pair(3, 3, c)
            ffn(1)
            for j in range(4):
                act.wait_ge(acc_read, 4 + j + 1)
                norm_square(4, j)
            norm_root(4)
            for j in range(4):
                norm_pair(5, 4, j)
            norm_root(5)

            c0, _, b0 = STAGES["mix_in"]

            def sigmoid_to_tmp(c, src):
                act.wait_ge(banks_read, b0 + c + 5)
                nc.scalar.activation(xg[:, c % 2, :], src, ACT.Sigmoid).then_inc(gate_sig, 1)

            def head_square(kind):
                act.wait_ge(banks_read, b0 + 2 * kind + 2 + 4)
                src, dst = ((mq, e_even), (mk, qe))[kind]
                nc.scalar.activation(dst[:, :], whole(src), ACT.Square).then_inc(msq, 1)

            def head_root(kind):
                act.wait_ge(mss, kind + 1)
                dst = (e_even, qe)[kind]
                for n in range(2):
                    nc.scalar.activation(dst[:, n * PAIR:(n + 1) * PAIR], bank[4 + 2 * kind + n][:, :],
                                         ACT.Sqrt, bias=eps).then_inc(msd, 1)

            def moba_exp(g):
                act.wait_ge(nm_ready, g + 1)
                for n in range(4):
                    for m, (s0, s1) in enumerate(((0, S), (S, 384))):
                        col = 2 * n + m
                        ins = nc.scalar.activation(pp_[:, n, s0:s1], pp_[:, n, s0:s1], ACT.Exp,
                                                   bias=nmx[:, col:col + 1],
                                                   accum_out=sm[:, col:col + 1])
                        ins.then_inc(p_exp, 1)

            def moba_copies(g):
                for n in range(4):
                    act.wait_ge(pt_mm, 4 * g + n + 1)
                    nc.scalar.activation(pt[:, n, :], bank[4 + n][:, 0:384], ACT.Copy)\
                        .then_inc(pt_read, 1)

            def decays():
                act.wait_ge(f_in, 1)
                link(nc.scalar.activation(e_even[:, :], whole(fb), ACT.Abs))
                link(nc.scalar.activation(e_even[:, :], e_even[:, :], ACT.Exp, scale=-1.0))
                link(nc.scalar.activation(qe[:, :], qe[:, :], ACT.Exp))
                for n in range(HGRN_HEADS):
                    nc.scalar.activation(qe[:, n * S:(n + 1) * S], qe[:, n * S:(n + 1) * S], ACT.Ln,
                                         scale=lbv[:, n:n + 1], bias=1.0)
                nc.scalar.activation(e_even[:, :], e_even[:, :], ACT.Ln, bias=1.0).then_inc(f_ready, 1)
                nc.scalar.activation(whole(kb), whole(fb), ACT.Sigmoid, scale=-1.0).then_inc(k_sig, 1)

            def level(j):
                e = (e_even, e_odd)[j % 2]
                act.wait_ge(lv_sub, j)
                link(nc.scalar.activation(e[:, :], e[:, :], ACT.Abs))
                nc.scalar.activation(e[:, :], e[:, :], ACT.Exp, scale=-1.0).then_inc(lv_exp, 1)

            def split_out(n, ready, src, dst, done):
                act.wait_ge(ready, n + 1)
                nc.scalar.activation(dst, src, ACT.Copy).then_inc(done, 1)

            def gate(tensor, c, j):
                act.wait_ge(banks_read, b0 + c + 5)
                nc.scalar.activation(tensor[:, j, :], tensor[:, j, :], ACT.Sigmoid).then_inc(gate_sig, 1)

            for c in range(24):
                ahead(c0 + c)
                if c == 1:
                    head_square(0)
                if c == 3:
                    head_root(0)
                    head_square(1)
                if c == 5:
                    head_root(1)
                if c == 7:
                    moba_exp(0)
                if c in (8, 9):
                    sigmoid_to_tmp(c, qb[:, c - 8, :])
                if c == 9:
                    moba_copies(0)
                if c == 11:
                    moba_exp(1)
                if c in (12, 13):
                    sigmoid_to_tmp(c, ag[:, c - 12, :])
                if c == 13:
                    moba_copies(1)
                if c in (14, 15):
                    sigmoid_to_tmp(c, bg[:, c - 14, :])
                if c == 14:
                    for n in range(2):
                        split_out(n, ya_ready, ya[:, n, :], pair(yahi, n), ya_hi)
                    decays()
                if 16 <= c < 20:
                    gate(ga, c, c - 16)
                if 20 <= c:
                    gate(gb, c, c - 20)
                if c >= 15 and c - 14 < len(LEVELS):
                    level(c - 14)
            act.wait_ge(yo_mm, 1)
            for n in range(2):
                ins = nc.scalar.activation(e_even[:, n * PAIR:(n + 1) * PAIR], bank[4 + n][:, :], ACT.Square)
            ins.then_inc(yo_sq, 1)
            ahead(STAGES["up_a"][0])
            act.wait_ge(yo_mean, 1)
            for n in range(2):
                ins = nc.scalar.activation(qe[:, n * PAIR:(n + 1) * PAIR], bank[6 + n][:, :],
                                           ACT.Sqrt, bias=eps)
            ins.then_inc(yo_sd, 1)
            ahead(STAGES["up_a"][0] + 1)
            for n in range(2):
                split_out(n, yb_ready, ke[:, n * PAIR:(n + 1) * PAIR], pair(ybhi, n), yb_hi)
            for c in range(2):
                ahead(STAGES["up_b"][0] + c)
                for n in (2 * c, 2 * c + 1):
                    split_out(n, m_ready, ga[:, n, :], pair(mhi, n), m_hi)
            for c in range(4):
                ahead(STAGES["out2"][0] + c)
                split_out(20 + c, xg_ready, h[:, c, :], pair(xhi, c), x_hi)
            ahead(STAGES["ple"][0])
            for c in range(4):
                ahead(STAGES["ple_gate"][0] + c)
                act.wait_ge(ple_in, c + 1)
                nc.scalar.activation(xg[:, c % 2, :], xg[:, c % 2, :], ACT.Sigmoid).then_inc(ple_sig, 1)
            for j in range(4):
                act.wait_ge(y_t, j + 1)
                nc.scalar.activation(y_tok[:, :, j * S:(j + 1) * S],
                                     bank[4 + j][:, :].rearrange("p (a n) -> p a n", a=2),
                                     ACT.Copy).then_inc(y_read, 1)

        @block.vector
        def _(dve):
            own = [0]

            def mark(ins):
                own[0] += 1
                ins.then_inc(dve_own, 1)
                return own[0]

            def link(ins):
                dve.wait_ge(dve_own, mark(ins))

            def split(i, c):
                dve.wait_ge(hi_done, at(i, 4, c + 1))
                nc.vector.tensor_tensor(wlo[:, c % RING, :HALF], raw[:, c % RAWS, :HALF],
                                        whi[:, c % RING, :HALF].bitcast(F32), ALU.subtract)\
                    .then_inc(lo_dve, 1)

            def ahead(c):
                if c + AHEAD < CHUNKS:
                    split(None, c + AHEAD)

            def pair(tensor, j):
                return tensor[:, 2 * j:2 * j + 2, :].rearrange("p a n -> p (a n)")

            def whole(tensor):
                return tensor[:, :, :].rearrange("p a n -> p (a n)")

            def col(name, n=0):
                return par[:, COL[name] + n:COL[name] + n + 1]

            def norm_gain(n, xn, j, gain):
                if 4 * xn + j >= 2:
                    dve.wait_ge(x_lo, 4 * xn + j - 1)
                    dve.wait_ge(x_hi, 4 * xn + j - 1)
                for m in range(2):
                    ins = nc.vector.tensor_scalar(xg[:, j % 2, m * S:(m + 1) * S],
                                                  h[:, j, m * S:(m + 1) * S],
                                                  par[:, gain + 2 * j + m:gain + 2 * j + m + 1], None,
                                                  ALU.mult)
                ins.then_inc(xg_ready, 1)

            def norm_lo(xn, j):
                dve.wait_ge(x_hi, 4 * xn + j + 1)
                nc.vector.tensor_tensor(pair(xlo, j), xg[:, j % 2, :], pair(xhi, j).bitcast(F32),
                                        ALU.subtract).then_inc(x_lo, 1)

            def norm_sum(n, j):
                dve.wait_ge(sq_ready, 4 * n + j + 1)
                if j:
                    if j > 1:
                        dve.wait_ge(ss_acc, 3 * n + j - 1)
                    nc.vector.tensor_tensor(ssum[:, :], ssum[:, :], sq[:, j % 2, :], ALU.add)\
                        .then_inc(ss_acc, 1)
                    if j == 3:
                        dve.wait_ge(ss_acc, 3 * n + 3)
                        dve.sem_inc(ss_done, 1)

            def norm_factor(n):
                dve.wait_ge(sd_ready, n + 1)
                link(nc.vector.reciprocal(rs[:, 0:S], sq[:, 0, 0:S]))
                nc.vector.tensor_copy(rs[:, S:], rs[:, 0:S]).then_inc(rs_ready, 1)
                dve.wait_ge(rs_ready, n + 1)

            def token_factors(k):
                dve.wait_ge(rst_ready, k + 1)
                nc.vector.tensor_copy(rs_tok[:, :], bank[7][:, 0:2]).then_inc(rst_read, 1)
                dve.wait_ge(rst_read, k + 1)

            def norm(n, xn, gain, update):
                for j in range(4):
                    update(j)
                    norm_gain(n, xn, j, gain)
                    if j:
                        norm_lo(xn, j - 1)
                        norm_sum(n, j - 1)
                norm_lo(xn, 3)
                norm_sum(n, 3)

            def evacuate(i, c, b, dst, op=None):
                dve.wait_ge(chunk_done, at(i, 4, c + 5))
                nc.vector.tensor_tensor(dst, bank[b % 4][:, :], rs[:, :], ALU.mult)\
                    .then_inc(banks_read, 1)

            def read(b):
                dve.wait_ge(banks_read, b + 5)

            nc.vector.memset(eps, EPS)
            link(nc.vector.memset(recp[:, :, 0:3], 0.0))
            for j in range(4):
                dve.wait_ge(chunk_done, j + 1)
                nc.vector.tensor_copy(h[:, j, :], bank[j][:, :]).then_inc(banks_read, 1)
            dve.wait_ge(par_t, 1)
            link(nc.vector.tensor_copy(par[:, :], bank[4][:, 0:N_A + N_B]))
            link(nc.vector.tensor_tensor(lb_a, par[:, COL["lb"]:COL["lb"] + 4],
                                         par[:, COL["lb"]:COL["lb"] + 4], ALU.subtract))
            nc.vector.memset(small[32:33, 84:92], MASKED).then_inc(relb_pad, 1)
            nc.vector.tensor_scalar(q_gain, col("q_gain"), 0.125, None, ALU.mult).then_inc(par_done, 1)
            dve.wait_ge(par_done, 1)
            norm(0, 0, COL["mix_norm"], lambda j: dve.wait_ge(banks_read, j + 1))
            for c in range(AHEAD):
                split(None, c)
            norm_factor(0)
            lam = par[:, COL["lam"]:COL["lam"] + 8]
            dve.wait_ge(sp_abs, 1)
            link(nc.vector.tensor_scalar(sp_b, lam, -1.0, 0.0, ALU.mult, ALU.max))
            link(nc.vector.tensor_tensor(sp_b, sp_b, sp_a, ALU.add))
            nc.vector.tensor_scalar(c8, sp_b, LRU_C, None, ALU.mult)
            link(nc.vector.tensor_scalar(nc8, sp_b, -LRU_C, None, ALU.mult))
            link(nc.vector.reciprocal(lb_a, lb_b))
            link(nc.vector.tensor_tensor(lb_a, lb_a, lb_b, ALU.mult))
            link(nc.vector.tensor_tensor(lbv, lb_a, lb_a, ALU.subtract))
            link(nc.vector.tensor_scalar(omlb, lbv, -1.0, 1.0, ALU.mult, ALU.add))

            def convolve(j):
                dve.wait_ge(rec_ready, j + 1)
                if j == 0:
                    dve.wait_ge(s_par, 256)
                for tap in (3, 2, 1, 0):
                    marks = []
                    for m in range(2):
                        f = 2 * j + m
                        dst = rc[:, j, m * S:(m + 1) * S]
                        w = col("conv_w", tap * DT + f)
                        if tap == 3:
                            marks.append(mark(nc.vector.tensor_scalar(
                                dst, recp[:, f, tap:tap + S], w, col("conv_b", f), ALU.mult, ALU.add)))
                        else:
                            dve.wait_ge(dve_own, before[m])
                            ins = nc.vector.scalar_tensor_tensor(
                                out=dst, in0=recp[:, f, tap:tap + S], scalar=w, in1=dst,
                                op0=ALU.mult, op1=ALU.add)
                            if tap == 0 and m == 1:
                                ins.then_inc(rc_ready, 1)
                            else:
                                marks.append(mark(ins))
                    before = marks

            def conv_lo(j):
                dve.wait_ge(rc_ready, j + 1)
                dve.wait_ge(rc_hi, j + 1)
                nc.vector.tensor_tensor(pair(rclo, j), rc[:, j, :], pair(rchi, j).bitcast(F32),
                                        ALU.subtract).then_inc(rc_lo, 1)

            c0, _, b0 = STAGES["rec"]
            for c in range(4):
                ahead(c0 + c)
                if c >= 2:
                    dve.wait_ge(rec_ready, c - 1)
                evacuate(None, c0 + c, b0 + c, t2[:, c % 2, :])
                if c:
                    convolve(c - 1)
                if c >= 2:
                    conv_lo(c - 2)
            convolve(3)
            conv_lo(2)
            c0, _, b0 = STAGES["branch"]
            for c in range(4):
                ahead(c0 + c)
                if c == 0:
                    conv_lo(3)
                    dve.wait_ge(rec_ready, 4)
                if c >= 2:
                    dve.wait_ge(br_sq, c - 1)
                evacuate(None, c0 + c, b0 + c, t2[:, c % 2, :])
                dve.wait_ge(br_sq, c + 1)
                link(nc.vector.tensor_scalar(gsq[:, c % 2, :], gsq[:, c % 2, :], GELU_CUBE, 1.0,
                                             ALU.mult, ALU.add))
                nc.vector.tensor_tensor(gsq[:, c % 2, :], gsq[:, c % 2, :], gel[:, c, :], ALU.mult)\
                    .then_inc(br_in, 1)
                dve.wait_ge(br_tanh, c + 1)
                link(nc.vector.scalar_tensor_tensor(out=gel[:, c, :], in0=gsq[:, c % 2, :], scalar=1.0,
                                                    in1=gel[:, c, :], op0=ALU.add, op1=ALU.mult))
                if c == 0:
                    dve.wait_ge(bkt_t, 1)
                    nc.vector.tensor_copy(bucket_bias[:, :], bank[5][0:8, 0:384]).then_inc(bkt_done, 1)
                if c == 3:
                    dve.wait_ge(p_hi, 1)
                    nc.vector.tensor_tensor(whole(plo), bank[6][:, :], whole(phi).bitcast(F32),
                                            ALU.subtract).then_inc(p_lo, 1)
            c0, _, b0 = STAGES["gates"]
            for g in range(2):
                ahead(c0 + g)
                dve.wait_ge(chunk_done, c0 + g + 5)
                for n in range(4):
                    for m in range(2):
                        dst = (rg, ig)[g][:, n, m * S:(m + 1) * S]
                        ins = nc.vector.tensor_scalar(
                            dst, bank[(b0 + 4 * g + n) % 4][:, m * S:(m + 1) * S],
                            col("gate_b", DT * g + 2 * n + m), None, ALU.add)
                    ins.then_inc(banks_read, 1)
            for n in range(4):
                dve.wait_ge(a_ready, 2 * n + 2)
                link(nc.vector.tensor_tensor(xg[:, n % 2, :], av[:, n, :], av[:, n, :], ALU.mult))
                nc.vector.scalar_tensor_tensor(out=rg[:, n, :], in0=xg[:, n % 2, :], scalar=1.0,
                                               in1=rg[:, n, :], op0=ALU.add, op1=ALU.mult)\
                    .then_inc(m2_ready, 1)
                dve.wait_ge(m2_ready, n + 1)
            for n in range(4):
                dve.wait_ge(ig_ready, n + 1)
                last = mark(nc.vector.tensor_tensor(ig[:, n, :], ig[:, n, :], rc[:, n, :], ALU.mult))
            dve.wait_ge(dve_own, last)
            for n in range(4):
                dve.wait_ge(mult_ready, n + 1)
                link(nc.vector.tensor_tensor(rg[:, n, :], rg[:, n, :], ig[:, n, :], ALU.mult))
                for m in range(2):
                    cols = slice(m * S, (m + 1) * S)
                    ins = nc.vector.tensor_tensor_scan(ig[:, n, cols], av[:, n, cols], rg[:, n, cols],
                                                       0.0, ALU.mult, ALU.add)
                link(ins)
                nc.vector.scalar_tensor_tensor(out=rc[:, n, :], in0=gel[:, n, :], scalar=0.5,
                                               in1=ig[:, n, :], op0=ALU.mult, op1=ALU.mult)\
                    .then_inc(y_ready, 1)
                if n:
                    dve.wait_ge(y_hi, n)
                    nc.vector.tensor_tensor(pair(ylo, n - 1), rc[:, n - 1, :],
                                            pair(yhi, n - 1).bitcast(F32), ALU.subtract).then_inc(y_lo, 1)
            dve.wait_ge(y_ready, 4)
            dve.wait_ge(y_hi, 4)
            nc.vector.tensor_tensor(pair(ylo, 3), rc[:, 3, :], pair(yhi, 3).bitcast(F32),
                                    ALU.subtract).then_inc(y_lo, 1)

            c0l, _, b0l = STAGES["lru_out"]

            def lru_residual(j):
                ahead(c0l + j)
                dve.wait_ge(chunk_done, c0l + j + 5)
                for m in range(2):
                    cols = slice(m * S, (m + 1) * S)
                    ins = nc.vector.scalar_tensor_tensor(
                        out=h[:, j, cols], in0=bank[(b0l + j) % 4][:, cols],
                        scalar=col("b_out", 2 * j + m), in1=h[:, j, cols], op0=ALU.add, op1=ALU.add)
                ins.then_inc(banks_read, 1)
                read(b0l + j)

            norm(1, 1, COL["ffn_norm"], lru_residual)

            def ffn(layer):
                n = 1 + 2 * layer
                norm_factor(n)
                c0, _, b0 = STAGES[f"ffn_in{layer}"]

                def gated(i, c, q, par_q):
                    split(i, c0 + c + AHEAD)
                    evacuate(i, c0 + c, b0 + c, tg[:, par_q, :])
                    split(i, c0 + c + 1 + AHEAD)
                    dve.wait_ge(sig_ready, at(i, 2, FFN_PAIRS * layer + q + 1))
                    dve.wait_ge(banks_read, at(i, 4, b0 + c + 5))
                    nc.vector.tensor_tensor(tg[:, par_q, :], tg[:, par_q, :], sg[:, par_q, :], ALU.mult)\
                        .then_inc(silu_ready, 1)
                    evacuate(i, c0 + c + 1, b0 + c + 1, tu[:, par_q, :])
                    dve.wait_ge(banks_read, at(i, 4, b0 + c + 6))
                    dve.wait_ge(silu_ready, at(i, 2, FFN_PAIRS * layer + q + 1))
                    nc.vector.tensor_tensor(tu[:, par_q, :], tg[:, par_q, :], tu[:, par_q, :], ALU.mult)\
                        .then_inc(act_ready, 1)
                    dve.wait_ge(act_ready, at(i, 2, FFN_PAIRS * layer + q + 1))
                    dve.wait_ge(g_hi, at(i, 2, FFN_PAIRS * layer + q + 1))
                    dst, hi = (glo[:, q, :], ghi[:, q, :]) if i is None else \
                        (glo[:, i * 2 + q, :], ghi[:, i * 2 + q, :])
                    nc.vector.tensor_tensor(dst, tu[:, par_q, :], hi.bitcast(F32), ALU.subtract)\
                        .then_inc(g_lo, 1)
                    dve.wait_ge(g_lo, at(i, 2, FFN_PAIRS * layer + q + 1))

                gated(None, 0, 0, 0)
                with dve.Fori(0, 5) as i:
                    for j in range(2):
                        gated(i, 2 + 2 * j, 1 + j, (1 + j) % 2)
                c0 = STAGES[f"ffn_out{layer}"][0]
                split(None, c0 + AHEAD)
                with dve.Fori(0, 2) as i:
                    for j in range(4):
                        split(i, c0 + 1 + j + AHEAD)
                for c in (9, 10):
                    split(None, c0 + c + AHEAD)
                dve.wait_ge(chunk_done, c0 + 10 + 5)

            def ffn_residual(layer):
                def update(j):
                    nc.vector.tensor_tensor(h[:, j, :], bank[4 + j][:, :], h[:, j, :], ALU.add)\
                        .then_inc(acc_read, 1)
                    dve.wait_ge(acc_read, 4 * layer + j + 1)
                return update

            ffn(0)
            norm(2, 2, COL["mix_norm"] + DT, ffn_residual(0))
            norm_factor(2)

            c0, _, b0 = STAGES["qkv"]

            def masked_logits(g):
                for n in range(4):
                    dve.wait_ge(z_mm, 4 * g + n + 1)
                    nc.vector.tensor_tensor(zz[:, n, :], bank[4 + n][:, 0:384], cst("causal", 384), ALU.add)\
                        .then_inc(z_read, 1)

            def neg_log_fail(g):
                dve.wait_ge(l_ready, g + 1)
                dve.wait_ge(z_read, 4 * g + 4)
                nc.vector.scalar_tensor_tensor(out=whole(nl), in0=whole(zz), scalar=0.0, in1=whole(ee),
                                               op0=ALU.max, op1=ALU.add).then_inc(nl_ready, 1)

            def exponents(g):
                dve.wait_ge(nl_ready, g + 1)
                for n in range(4):
                    dve.wait_ge(s_mm, 4 * g + n + 1)
                    ins = nc.vector.tensor_tensor(zz[:, n, :], zz[:, n, :], bank[4 + n][:, 0:384], ALU.add)
                ins.then_inc(arg_ready, 1)

            def outputs(g):
                dve.wait_ge(o_hi, g + 1)
                nc.vector.tensor_tensor(olo[:, g, :], bank[4][:, :], ohi[:, g, :].bitcast(F32),
                                        ALU.subtract).then_inc(o_lo, 1)

            for g in range(GROUPS):
                for q in range(3):
                    c, b = c0 + 3 * g + q, b0 + 3 * g + q
                    ahead(c)
                    if g and q == 1:
                        neg_log_fail(g - 1)
                    if g and q == 2:
                        exponents(g - 1)
                    if q == 0:
                        dve.wait_ge(chunk_done, c + 5)
                        nc.vector.scalar_tensor_tensor(out=whole(qa[:, g % 2]), in0=bank[b % 4][:, :],
                                                       scalar=0.125, in1=rs[:, :], op0=ALU.mult,
                                                       op1=ALU.mult).then_inc(banks_read, 1)
                    if q == 1:
                        evacuate(None, c, b, whole(ka[:, g % 2]))
                    if q == 2:
                        if g == 0:
                            token_factors(0)
                        dve.wait_ge(chunk_done, c + 5)
                        for m in range(2):
                            ins = nc.vector.tensor_scalar(va[:, g % 2, m, :], bank[b % 4][:, m * S:(m + 1) * S],
                                                          rs_tok[:, m:m + 1], None, ALU.mult)
                        ins.then_inc(banks_read, 1)
                    if q == 0 and g >= 2:
                        outputs(g - 2)
                    if g and q == 0:
                        if g >= 2:
                            dve.wait_ge(w_ready, g - 1)
                        masked_logits(g - 1)
            outputs(GROUPS - 2)
            dve.wait_ge(w_ready, GROUPS - 1)
            masked_logits(GROUPS - 1)
            neg_log_fail(GROUPS - 1)
            exponents(GROUPS - 1)
            outputs(GROUPS - 1)

            c0a, _, b0a = STAGES["attn_out"]

            def attn_residual(j):
                ahead(c0a + j)
                dve.wait_ge(chunk_done, c0a + j + 5)
                nc.vector.tensor_tensor(h[:, j, :], bank[(b0a + j) % 4][:, :], h[:, j, :], ALU.add)\
                    .then_inc(banks_read, 1)
                read(b0a + j)

            norm(3, 3, COL["ffn_norm"] + DT, attn_residual)
            ffn(1)
            for j in range(4):
                ffn_residual(1)(j)
                if j:
                    norm_sum(4, j - 1)
            norm_sum(4, 3)
            for n in range(4):
                dve.wait_ge(bias_mm, n + 1)
                nc.vector.tensor_copy(pair(bias, n), bank[4 + n][:, :]).then_inc(bias_read, 1)
            norm_factor(4)

            def final_norm(j):
                for m in range(2):
                    cols = slice(m * S, (m + 1) * S)
                    ins = nc.vector.scalar_tensor_tensor(
                        out=h[:, j, cols], in0=h[:, j, cols], scalar=col("final_norm", 2 * j + m),
                        in1=rs[:, 0:S], op0=ALU.mult, op1=ALU.mult)
                link(ins)

            norm(5, 4, COL["norm_gain"], final_norm)
            norm_factor(5)

            c0, _, b0 = STAGES["mix_in"]

            def silu(c, tensor, j, k):
                dve.wait_ge(gate_sig, k)
                link(nc.vector.tensor_tensor(tensor[:, j, :], tensor[:, j, :], xg[:, c % 2, :], ALU.mult))

            def token_values(c, dst, c_cols):
                dve.wait_ge(chunk_done, c0 + c + 5)
                for m in range(2):
                    ins = nc.vector.tensor_scalar(dst[:, m, c_cols:c_cols + S],
                                                  bank[(b0 + c) % 4][:, m * S:(m + 1) * S],
                                                  rs_tok[:, m:m + 1], None, ALU.mult)
                ins.then_inc(banks_read, 1)

            def head_norm(kind):
                src, den, gain = ((mq, e_even, q_gain), (mk, qe, col("k_gain")))[kind]
                dve.wait_ge(msd, 2 * kind + 2)
                link(nc.vector.reciprocal(den[:, :], den[:, :]))
                nc.vector.scalar_tensor_tensor(out=whole(src), in0=whole(src), scalar=gain,
                                               in1=den[:, :], op0=ALU.mult, op1=ALU.mult)\
                    .then_inc(mn_ready, 1)

            def moba_max(g):
                for n in range(4):
                    dve.wait_ge(sc_mm, 4 * g + n + 1)
                    for m, (s0, s1, o0) in enumerate(((0, S, 0), (S, 384, P))):
                        k = 2 * n + m
                        ins = nc.vector.tensor_tensor_reduce(
                            out=pp_[:, n, s0:s1], in0=bank[4 + n][:, s0:s1],
                            in1=bias[:, 4 * g + n, o0:S], scale=1.0, scalar=3.0 * MASKED,
                            op0=ALU.add, op1=ALU.max, accum_out=mx[:, k:k + 1])
                link(ins)
                nc.vector.tensor_scalar(nmx, mx, -1.0, None, ALU.mult).then_inc(nm_ready, 1)

            def moba_scale(g):
                dve.wait_ge(p_exp, 8 * (g + 1))
                link(nc.vector.reciprocal(rsm, sm))
                for n in range(4):
                    for m, (s0, s1) in enumerate(((0, S), (S, 384))):
                        ins = nc.vector.tensor_scalar(pp_[:, n, s0:s1], pp_[:, n, s0:s1],
                                                      rsm[:, 2 * n + m:2 * n + m + 1], None, ALU.mult)
                    ins.then_inc(p_ready, 1)

            def moba_out(g):
                dve.wait_ge(mpv_mm, g + 1)
                nc.vector.tensor_copy(ya[:, g, :], bank[4][:, :]).then_inc(mpv_read, 1)

            def decay_start():
                nc.vector.tensor_scalar(qe[:, :], whole(fb), -1.0, EXP_CLIP, ALU.mult, ALU.min)\
                    .then_inc(f_in, 1)

            def decay_sum():
                dve.wait_ge(f_ready, 1)
                nc.vector.memset(ones[:, :], 1.0)
                link(nc.vector.scalar_tensor_tensor(out=ke[:, :], in0=whole(fb), scalar=0.0,
                                                    in1=e_even[:, :], op0=ALU.min, op1=ALU.subtract))
                link(nc.vector.tensor_tensor(ke[:, :], ke[:, :], qe[:, :], ALU.add))
                for n in range(HGRN_HEADS):
                    ins = nc.vector.tensor_tensor_scan(cum[:, n * S:(n + 1) * S], ones[:, :], ke[:, n * S:(n + 1) * S],
                                                       0.0, ALU.mult, ALU.add)
                link(ins)
                dve.wait_ge(k_sig, 1)
                for n in range(HGRN_HEADS):
                    k = whole(kb)[:, n * S:(n + 1) * S]
                    ins = nc.vector.tensor_scalar(k, k, omlb[:, n:n + 1], None, ALU.mult)
                link(ins)
                nc.vector.memset(whole(score), 0.0).then_inc(lv_ready, 1)
                dve.wait_ge(lv_ready, 1)

            def level_start(j):
                m = LEVELS[j]
                if j >= 3:
                    dve.wait_ge(lv_ready, j - 1)
                e = (e_even, e_odd)[j % 2]
                v = cum[:, :].rearrange("p (b t) -> p b t", t=2 * m)
                mid = v[:, :, m - 1:m].broadcast_to([P, 1024 // (2 * m), 2 * m])
                nc.vector.tensor_tensor(e[:, :].rearrange("p (b t) -> p b t", t=2 * m), v, mid,
                                        ALU.subtract).then_inc(lv_sub, 1)

            def level_factors(j):
                e = (e_even, e_odd)[j % 2]
                dve.wait_ge(lv_exp, j)
                if j >= 2:
                    dve.wait_ge(lv_mm, j)
                if LEVELS[j] == P:
                    def half(x, a):
                        return x.rearrange("p (h a n) -> p h a n", a=2, n=P)[:, :, a, :]
                    pairs = [(half(qe[:, :], 1), half(whole(qb), 1), half(e[:, :], 1)),
                             (half(ke[:, :], 0), half(whole(kb), 0), half(e[:, :], 0))]
                else:
                    pairs = [(qe[:, :], whole(qb), e[:, :]), (ke[:, :], whole(kb), e[:, :])]
                for dst, x, y in pairs:
                    ins = nc.vector.tensor_tensor(dst, x, y, ALU.mult)
                ins.then_inc(lv_ready, 1)

            def level_read(j):
                dve.wait_ge(lv_mm, j + 1)
                pair0 = 4 + 2 * (j % 2)
                if LEVELS[j] == P:
                    nc.vector.tensor_copy(whole(cross), bank[pair0][:, :]).then_inc(lv_read, 1)
                    return
                mask = cst("levels", 1024)[:, j * P:(j + 1) * P].bitcast(U32)\
                    .rearrange("p (o n) -> p o n", o=1).broadcast_to([P, 4, P])
                if j:
                    dve.wait_ge(lv_read, j)
                for n in range(2):
                    ins = nc.vector.copy_predicated(score[:, 4 * n:4 * n + 4, :], mask,
                                                    bank[pair0 + n][:, :].rearrange("p (u n) -> p u n", n=P))
                ins.then_inc(lv_read, 1)

            for c in range(24):
                ahead(c0 + c)
                b = b0 + c
                if c == 2:
                    token_factors(1)
                if c == 4:
                    head_norm(0)
                if c == 6:
                    head_norm(1)
                if c == 7:
                    moba_max(0)
                if c == 8:
                    moba_scale(0)
                if c == 10:
                    moba_out(0)
                if c == 11:
                    moba_max(1)
                if c == 12:
                    moba_scale(1)
                if c == 14:
                    moba_out(1)
                if c == 15:
                    decay_sum()
                if c < 2:
                    evacuate(None, c0 + c, b, pair(mq, c))
                elif c < 4:
                    evacuate(None, c0 + c, b, pair(mk, c - 2))
                elif c < 6:
                    token_values(c, mv, (c - 4) * S)
                elif c < 8:
                    evacuate(None, c0 + c, b, fb[:, c - 6, :])
                elif c < 10:
                    evacuate(None, c0 + c, b, qb[:, c - 8, :])
                    read(b)
                    silu(c, qb, c - 8, c - 7)
                elif c < 12:
                    token_values(c, vb, (c - 10) * S)
                elif c < 14:
                    evacuate(None, c0 + c, b, ag[:, c - 12, :])
                    read(b)
                    silu(c, ag, c - 12, c - 9)
                elif c < 16:
                    evacuate(None, c0 + c, b, bg[:, c - 14, :])
                    read(b)
                    silu(c, bg, c - 14, c - 9)
                elif c < 20:
                    evacuate(None, c0 + c, b, ga[:, c - 16, :])
                else:
                    evacuate(None, c0 + c, b, gb[:, c - 20, :])
                if c == 14:
                    dve.wait_ge(mpv_read, 2)
                    for n in range(2):
                        ins = nc.vector.tensor_tensor(ya[:, n, :], ya[:, n, :], ag[:, n, :], ALU.mult)
                        ins.then_inc(ya_ready, 1)
                    for n in range(2):
                        dve.wait_ge(ya_ready, n + 1)
                        dve.wait_ge(ya_hi, n + 1)
                        nc.vector.tensor_tensor(pair(yalo, n), ya[:, n, :], pair(yahi, n).bitcast(F32),
                                                ALU.subtract).then_inc(ya_lo, 1)
                    decay_start()
                if c == 15:
                    level_start(1)
                j = c - 15
                if j >= 1:
                    level_read(j - 1)
                if j >= 0 and j + 2 < len(LEVELS):
                    level_start(j + 2)
                if j >= 0 and j + 1 < len(LEVELS):
                    level_factors(j + 1)
            level_read(len(LEVELS) - 1)

            ahead(STAGES["up_a"][0])
            dve.wait_ge(yo_sd, 1)
            link(nc.vector.reciprocal(qe[:, :], qe[:, :]))
            for n in range(HGRN_HEADS):
                cols = slice(n * S, (n + 1) * S)
                ins = nc.vector.scalar_tensor_tensor(
                    out=ke[:, cols], in0=bank[4 + n // 2][:, n % 2 * S:(n % 2 + 1) * S],
                    scalar=col("hgrn_gain", n), in1=qe[:, cols], op0=ALU.mult, op1=ALU.mult)
            ins.then_inc(yo_read, 1)
            dve.wait_ge(yo_read, 1)
            for n in range(2):
                cols = slice(n * PAIR, (n + 1) * PAIR)
                nc.vector.tensor_tensor(ke[:, cols], ke[:, cols], bg[:, n, :], ALU.mult).then_inc(yb_ready, 1)
            for n in range(2):
                cols = slice(n * PAIR, (n + 1) * PAIR)
                dve.wait_ge(yb_ready, n + 1)
                dve.wait_ge(yb_hi, n + 1)
                nc.vector.tensor_tensor(pair(yblo, n), ke[:, cols], pair(ybhi, n).bitcast(F32),
                                        ALU.subtract).then_inc(yb_lo, 1)
            c0, _, b0 = STAGES["up_a"]
            for c in range(2):
                if c:
                    ahead(c0 + c)
                dve.wait_ge(chunk_done, c0 + c + 5)
                for n in (2 * c, 2 * c + 1):
                    dve.wait_ge(gate_sig, 6 + n + 1)
                    nc.vector.tensor_tensor(ga[:, n, :], bank[(b0 + n) % 4][:, :], ga[:, n, :], ALU.mult)\
                        .then_inc(banks_read, 1)
            c0, _, b0 = STAGES["up_b"]
            for c in range(2):
                ahead(c0 + c)
                dve.wait_ge(chunk_done, c0 + c + 5)
                for n in (2 * c, 2 * c + 1):
                    dve.wait_ge(gate_sig, 10 + n + 1)
                    nc.vector.tensor_tensor(gb[:, n, :], bank[(b0 + n) % 4][:, :], gb[:, n, :], ALU.mult)\
                        .then_inc(banks_read, 1)
                    read(b0 + n)
                    nc.vector.tensor_tensor(ga[:, n, :], ga[:, n, :], gb[:, n, :], ALU.add)\
                        .then_inc(m_ready, 1)
                for n in (2 * c, 2 * c + 1):
                    dve.wait_ge(m_ready, n + 1)
                    dve.wait_ge(m_hi, n + 1)
                    nc.vector.tensor_tensor(pair(mlo, n), ga[:, n, :], pair(mhi, n).bitcast(F32),
                                            ALU.subtract).then_inc(m_lo, 1)
            c0, _, b0 = STAGES["out2"]
            for c in range(4):
                ahead(c0 + c)
                dve.wait_ge(chunk_done, c0 + c + 5)
                nc.vector.tensor_tensor(h[:, c, :], bank[(b0 + c) % 4][:, :], h[:, c, :], ALU.add)\
                    .then_inc(banks_read, 1)
                read(b0 + c)
                dve.sem_inc(xg_ready, 1)
                dve.wait_ge(x_hi, 20 + c + 1)
                nc.vector.tensor_tensor(pair(xlo, c), h[:, c, :], pair(xhi, c).bitcast(F32),
                                        ALU.subtract).then_inc(x_lo, 1)
            c0, _, b0 = STAGES["ple"]
            ahead(c0)
            dve.wait_ge(chunk_done, c0 + 5)
            for n in range(4):
                nc.vector.tensor_copy(ple[:, n, :], bank[(b0 + n) % 4][:, :]).then_inc(banks_read, 1)
            read(b0 + 3)
            c0, _, b0 = STAGES["ple_gate"]
            for c in range(4):
                ahead(c0 + c)
                dve.wait_ge(chunk_done, c0 + c + 5)
                if c >= 2:
                    dve.wait_ge(fin_ready, c - 1)
                nc.vector.tensor_copy(xg[:, c % 2, :], bank[(b0 + c) % 4][:, :]).then_inc(banks_read, 1)
                read(b0 + c)
                dve.sem_inc(ple_in, 1)
                dve.wait_ge(ple_sig, c + 1)
                link(nc.vector.tensor_tensor(xg[:, c % 2, :], xg[:, c % 2, :], ple[:, c, :], ALU.mult))
                nc.vector.tensor_tensor(h[:, c, :], h[:, c, :], xg[:, c % 2, :], ALU.add)\
                    .then_inc(fin_ready, 1)


def constants():
    import numpy as np

    c = np.zeros((P, N_CONST), np.float32)

    def put(name, value, off=0):
        value = np.asarray(value, np.float32)
        c[:value.shape[0], CONST[name] + off:CONST[name] + off + value.shape[1]] = value

    k, q = np.arange(P)[:, None], np.arange(P)[None, :]
    put("ident", k == q)
    put("anti", k + q == P - 1)
    put("suffix", -1.0 * (k >= q))
    put("neg", -np.ones((P, P)))
    put("mean_d", np.full((P, P), 1.0 / D))
    put("mean_head", (k // 64 == q // 64) / 64.0)
    put("mean_v", np.full((P, P), 1.0 / P))
    for off in (0, S):
        put("causal", np.where(k < q, 0.0, MASKED), off)
    put("levels", k == q)
    for n, m in enumerate(LEVELS[1:-1]):
        put("levels", (k // (2 * m) == q // (2 * m)) & (k // m % 2 == 0) & (q // m % 2 == 1), (n + 1) * P)
    dist = 255 - np.arange(384)
    far = 16 + (np.log(np.maximum(dist, 16) / 16.0) / np.log(2048 / 16.0) * 16).astype(np.int64)
    bucket = np.where(dist < 0, 32, np.where(dist < 16, dist, np.minimum(far, 31)))
    put("bucket", np.arange(33)[:, None] == bucket[None, :])
    return c


_INS = ["x", "mix_norm", "ffn_norm", "final_norm", "lru_w_in", "lru_b_in", "lru_conv_w", "lru_conv_b",
        "lru_gate_w", "lru_gate_b", "lru_lambda", "lru_w_out", "lru_b_out", "attn_w_qkv", "attn_w_o",
        "ffn_w_in", "ffn_w_out", "p_2", "norm_gain_2", "w_in_2", "q_norm_gain_2", "k_norm_gain_2",
        "rel_bias_2", "hgrn_lb_logits_2", "hgrn_out_gain_2", "w_up_a_2", "w_up_b_2", "w_out_2",
        "w_ple_2", "w_ple_gate_2"]


def kernel(**inputs):
    import numpy as _np
    import concourse.bacc as _bacc
    from concourse import mybir as _mybir
    from concourse.bass_utils import run_bass_kernel_spmd as _run

    nc = _bacc.Bacc("TRN2", target_bir_lowering=False, num_devices=1)
    arrays, aps = {}, {}
    given = {name: _np.ascontiguousarray(inputs[name]) for name in _INS}
    given["consts"] = constants()
    for name, a in given.items():
        arrays[f"in_{name}"] = a
        aps[name] = nc.dram_tensor(f"in_{name}", a.shape, _mybir.dt.from_np(a.dtype),
                                   kind="ExternalInput").ap()
    out = nc.dram_tensor("out_0", (1, S, D), _mybir.dt.float32, kind="ExternalOutput").ap()
    build(nc, aps, out)
    r = _run(nc, [arrays], core_ids=[0])
    return r.results[0]["out_0"]
```

```python
from contextlib import ExitStack

import concourse.bass as bass
from concourse import mybir

F32 = mybir.dt.float32
F32R = mybir.dt.float32r
U32 = mybir.dt.uint32
ALU = mybir.AluOpType
ACT = mybir.ActivationFunctionType

P = 128
S = 256
D = 1024
DT = D // P
FF = 2816
PAIR = 2 * S
CHUNK = 2048
HALF = CHUNK // 2
RAWS = 2
RING = 4
AHEAD = 3
EPS = 1e-6
MASKED = -1e30
LRU_C = 8.0
GELU_IN, GELU_CUBE = 0.7978845608028654, 0.044715
EXP_CLIP = 30.0
FFN_PAIRS = FF // S
GROUPS = 4
HGRN_HEADS = 4
LEVELS = (0, 64, 32, 16, 8, 4, 2, 1, 128)

STAGES = {}
_c = _b = 0
for _name, _n, _banks in (
    ("rec_a", 3, 1), ("gates_a", 1, 4), ("rec_b", 1, 1), ("branch_a", 1, 1), ("gates_b", 1, 4),
    ("branch_b", 3, 1), ("lru_out", 4, 1),
    ("ffn_in0", 22, 1), ("ffn_out0", 11, 0), ("qkv", 12, 1), ("attn_out", 4, 1),
    ("ffn_in1", 22, 1), ("ffn_out1", 11, 0), ("mix_in", 24, 1), ("up_a", 2, 2), ("up_b", 2, 2),
    ("out2", 4, 1), ("ple", 1, 4), ("ple_gate", 4, 1),
):
    STAGES[_name] = (_c, _n, _b)
    _c += _n
    _b += _n * _banks
CHUNKS = _c

ROWS_A = (("mix_norm", 16), ("ffn_norm", 16), ("final_norm", 8), ("b_in", 16), ("conv_w", 32),
          ("conv_b", 8), ("gate_b", 16))
ROWS_B = (("lam", 8), ("b_out", 8), ("norm_gain", 8), ("lb", 4), ("hgrn_gain", 4), ("q_gain", 1),
          ("k_gain", 1))
COL = {}
_r = 0
for _name, _n in ROWS_A + ROWS_B:
    COL[_name] = _r
    _r += _n
N_A = sum(n for _, n in ROWS_A)
N_B = sum(n for _, n in ROWS_B)

CONST = {}
_r = 0
for _name, _n in (("ident", 128), ("anti", 128), ("suffix", 128), ("neg", 128), ("mean_d", 128),
                  ("mean_head", 128), ("mean_v", 128), ("causal", 384), ("levels", 8 * 128),
                  ("bucket", 384)):
    CONST[_name] = _r
    _r += _n
N_CONST = _r

MIX_ORDER = (0, 1, 2, 3, 4, 5, 10, 11, 8, 9, 12, 13, 6, 7, 14, 15, 16, 17, 18, 19, 20, 21, 22, 23)


def at(i, step, base):
    return base if i is None else i * step + base


def build(nc, t, out):
    ctx = ExitStack()
    with ctx:
        def sb(name, shape, dt=F32):
            return ctx.enter_context(nc.sbuf_tensor(name, shape, dt))

        def sem(name):
            return ctx.enter_context(nc.semaphore(name))

        raw = sb("raw", [P, RAWS, CHUNK])
        whi = sb("whi", [P, RING, CHUNK], F32R)
        wlo = sb("wlo", [P, RING, CHUNK], F32R)
        const = sb("const", [P, N_CONST])
        h = sb("h", [P, DT // 2, PAIR])
        xhi = sb("xhi", [P, DT, S], F32R)
        xlo = sb("xlo", [P, DT, S], F32R)
        xg = sb("xg", [P, 2, PAIR])
        ssum = sb("ssum", [P, PAIR])
        sq = sb("sq", [P, 2, PAIR])
        rs = sb("rs", [P, PAIR])
        rs_tok = sb("rs_tok", [P, 2])
        par = sb("par", [P, N_A + N_B])
        small = sb("small", [P, 104])

        base = (nc.sbuf_base + 63) // 64 * 64
        arena = sb("arena", [P, 80 * 256])

        def over(name, kb, shape, dt=F32):
            return nc.alloc_sbuf_tensor_at("a_" + name, shape, dt, offset=base + int(kb * 1024))

        x_tok = over("x_tok", 0, [P, 2, D])
        prow = over("prow", 17, [P, 2, P])
        bucket_bias = over("bucket_bias", 65, [8, 384])
        recp = over("recp", 8, [P, DT, S + 3])
        rc = over("rc", 17, [P, 4, PAIR])
        rchi = over("rchi", 25, [P, DT, S], F32R)
        rclo = over("rclo", 33, [P, DT, S], F32R)
        gel = over("gel", 41, [P, 4, PAIR])
        rg = over("rg", 49, [P, 4, PAIR])
        ig = over("ig", 57, [P, 4, PAIR])
        gsq = over("gsq", 25, [P, 2, PAIR])
        av = over("av_lru", 8, [P, 4, PAIR])
        yhi = over("yhi", 65, [P, DT, S], F32R)
        ylo = over("ylo", 0, [P, DT, S], F32R)
        p_tok = over("p_tok", 74, [P, 2, S])
        phi = over("phi", 76, [P, 2, S], F32R)
        plo = over("plo", 78, [P, 2, S], F32R)
        ghi = over("ghi", 0, [P, FFN_PAIRS, PAIR], F32R)
        glo = over("glo", 22, [P, FFN_PAIRS, PAIR], F32R)
        tg = over("tg", 44, [P, 2, PAIR])
        sg = over("sg", 48, [P, 2, PAIR])
        tu = over("tu", 52, [P, 2, PAIR])
        qa = over("qa", 0, [P, 2, 2, S])
        ka = over("ka", 4, [P, 2, 2, S])
        va = over("va", 8, [P, 2, 2, S])
        zz = over("zz", 12, [P, 4, 384])
        ee = over("ee", 18, [P, 4, 384])
        nl = over("nl", 24, [P, 4, 384])
        ww = over("ww", 30, [P, 4, 384])
        ohi = over("ohi", 36, [P, 4, PAIR], F32R)
        olo = over("olo", 44, [P, 4, PAIR], F32R)
        fb = over("fb", 0, [P, 2, PAIR])
        score = over("score", 0, [P, HGRN_HEADS * 2, P])
        qb = over("qb", 4, [P, 2, PAIR])
        kb = over("kb", 8, [P, 2, PAIR])
        cum = over("cum", 12, [P, 1024])
        vb = over("vb", 16, [P, 2, 512])
        cross = over("cross", 20, [P, HGRN_HEADS, P])
        mq = over("mq", 22, [P, 4, S])
        mk = over("mk", 26, [P, 4, S])
        mv = over("mv", 30, [P, 2, 512])
        e_odd = over("e_odd", 30, [P, 1024])
        e_even = over("e_even", 34, [P, 1024])
        qe = over("qe", 38, [P, 1024])
        ke = over("ke", 42, [P, 1024])
        pp_ = over("probs", 34, [P, 4, 384])
        pt = over("probs_t", 40, [P, 4, 384])
        ag = over("ag", 46, [P, 2, PAIR])
        lf = over("log_f", 66, [P, 1024])
        lf_b = over("log_f_b", 70, [P, 1024])
        ones = over("ones", 74, [P, S])
        bg = over("bg", 50, [P, 2, PAIR])
        ga = over("ga", 22, [P, 4, PAIR])
        bias = over("bias", 54, [P, 8, S])
        gb = over("gb", 54, [P, 4, PAIR])
        bias_rev = over("bias_rev", 62, [P, 8, S])
        ya = over("ya", 62, [P, 2, PAIR])
        yahi = over("yahi", 66, [P, 4, S], F32R)
        yalo = over("yalo", 70, [P, 4, S], F32R)
        ybhi = over("ybhi", 4, [P, 4, S], F32R)
        yblo = over("yblo", 8, [P, 4, S], F32R)
        mhi = over("mhi", 12, [P, DT, S], F32R)
        mlo = over("mlo", 34, [P, DT, S], F32R)
        ple = over("ple", 42, [P, 4, PAIR])
        y_tok = over("y_tok", 0, [P, 2, D])

        bank = [ctx.enter_context(nc.psum_tensor(f"bank{n}", [P, PAIR], F32)) for n in range(8)]
        bias_dram = nc.dram_tensor("bias_scratch", (8, 384), F32, kind="Internal").ap()

        def cst(name, n=128):
            return const[:, CONST[name]:CONST[name] + n]

        ident = cst("ident")
        c8, nc8, lbv, omlb = small[:, 0:8], small[:, 8:16], small[:, 16:20], small[:, 20:24]
        sp_a, sp_b = small[:, 24:32], small[:, 32:40]
        lb_a, lb_b = small[:, 40:44], small[:, 44:48]
        eps = small[:, 48:49]
        q_gain = small[:, 49:50]
        relb = small[0:33, 84:92]
        conv_bias = small[:, 92:100]
        mx, nmx, sm, rsm = (small[:, 52 + 8 * n:60 + 8 * n] for n in range(4))

        s_ident, s_x, s_par, s_const, s_p, s_relb = map(
            sem, ("ident_in", "x_in", "par_in", "const_in", "p_in", "relb_in"))
        raw_full = [sem(f"raw_full{n}") for n in range(RAWS)]
        hi_done, lo_dve, lo_pool = map(sem, ("hi_done", "lo_dve", "lo_pool"))
        chunk_done = sem("chunk_done")
        banks_read = sem("banks_read")
        par_t, par_done, relb_pad, bkt_t, bkt_done, bkt_out, bias_in, p_t, p_hi, p_lo = map(
            sem, ("par_t", "par_done", "relb_pad", "bkt_t", "bkt_done", "bkt_out", "bias_in", "p_t", "p_hi",
                  "p_lo"))
        xg_ready, x_hi, x_lo, sq_ready, ss_acc, ss_done, mean_ready, sd_ready, rs_ready = map(
            sem, ("xg_ready", "x_hi", "x_lo", "sq_ready", "ss_acc", "ss_done", "mean_ready",
                  "sd_ready", "rs_ready"))
        rst_ready, rst_read = map(sem, ("rst_ready", "rst_read"))
        sp_abs, rc_ready, rc_hi, rc_lo, br_z, br_sq, br_cube, br_in, br_tanh = map(
            sem, ("sp_abs", "rc_ready", "rc_hi", "rc_lo", "br_z", "br_sq", "br_cube", "br_in", "br_tanh"))
        gate_mm, a_ready, m2_ready, ig_ready, ix_ready, mult_ready, y_ready, y_hi, y_lo = map(
            sem, ("gate_mm", "a_ready", "m2_ready", "ig_ready", "ix_ready", "mult_ready", "y_ready",
                  "y_hi", "y_lo"))
        sig_ready, silu_ready, act_ready, g_hi, g_lo, acc_read = map(
            sem, ("sig_ready", "silu_ready", "act_ready", "g_hi", "g_lo", "acc_read"))
        z_mm, z_read, l_ready, nl_ready, s_mm, arg_ready, w_ready, pv_mm, o_hi, o_lo = map(
            sem, ("z_mm", "z_read", "l_ready", "nl_ready", "s_mm", "arg_ready", "w_ready",
                  "pv_mm", "o_hi", "o_lo"))
        bias_mm, bias_read, msq, mss, msd, mn_ready = map(
            sem, ("bias_mm", "bias_read", "msq", "mss", "msd", "mn_ready"))
        sc_mm, sc_read, nm_ready, p_exp, p_ready, pt_mm, pt_read, mpv_mm, mpv_read = map(
            sem, ("sc_mm", "sc_read", "nm_ready", "p_exp", "p_ready", "pt_mm", "pt_read",
                  "mpv_mm", "mpv_read"))
        gate_sig, ya_ready, ya_hi, ya_lo = map(sem, ("gate_sig", "ya_ready", "ya_hi", "ya_lo"))
        f_in, f_ready, k_sig, lv_sub, lv_exp, lv_ready, lv_mm, lv_read = map(
            sem, ("f_in", "f_ready", "k_sig", "lv_sub", "lv_exp", "lv_ready", "lv_mm", "lv_read"))
        yo_mm, yo_sq, yo_mean, yo_sd, yo_read, yb_ready, yb_hi, yb_lo = map(
            sem, ("yo_mm", "yo_sq", "yo_mean", "yo_sd", "yo_read", "yb_ready", "yb_hi", "yb_lo"))
        m_ready, m_hi, m_lo, ple_in, ple_sig, fin_ready, y_t, y_read, y_out = map(
            sem, ("m_ready", "m_hi", "m_lo", "ple_in", "ple_sig", "fin_ready", "y_t", "y_read",
                  "y_out"))
        dve_own, act_own = sem("dve_own"), sem("act_own")

        w_in = t["lru_w_in"][0].rearrange("(k p) (c n) -> c p k n", p=P, n=S)
        w_gate = [t["lru_gate_w"][0][:, 2 * n:2 * n + 2].rearrange("g n (k p) d -> p g (n k) d", p=P)
                  for n in range(2)]
        w_lru_out = t["lru_w_out"][0].rearrange("(k p) (c n) -> c p k n", p=P, n=S)
        w_ffn_in = t["ffn_w_in"].rearrange("l (k p) (u c n) -> l u c p k n", p=P, u=2, n=S)
        w_ffn_out = t["ffn_w_out"].rearrange("l (c k p) n -> l c p k n", p=P, k=2)
        w_qkv = t["attn_w_qkv"][0].rearrange("(k p) (q c n) -> q c p k n", p=P, q=3, n=S)
        w_o = t["attn_w_o"][0].rearrange("(k p) (c n) -> c p k n", p=P, n=S)
        w_mix = t["w_in_2"][0].rearrange("(k p) (c n) -> c p k n", p=P, n=S)
        w_up = {n: t[n][0].rearrange("(k p) (c n) -> c p k n", p=P, n=512)
                for n in ("w_up_a_2", "w_up_b_2")}
        w_out2 = t["w_out_2"][0].rearrange("(k p) (c n) -> c p k n", p=P, n=S)
        w_ple = t["w_ple_2"][0].rearrange("(k p) n -> p k n", p=P)
        w_pg = t["w_ple_gate_2"][0].rearrange("(k p) (c n) -> c p k n", p=P, n=S)

        block = ctx.enter_context(nc.Block())

        @block.sync
        def _(sp):
            def load(i, c, src):
                slot = c % RAWS
                if i is not None or c >= RAWS:
                    sp.wait_ge(lo_dve, at(i, 4, c - RAWS + 1))
                    sp.wait_ge(lo_pool, at(i, 4, c - RAWS + 1))
                n = src.shape[-1]
                if len(src.shape) == 4:
                    for g in range(2):
                        sp.dma_start(raw[:, slot, g * HALF:(g + 1) * HALF].rearrange("p (k n) -> p k n", n=n),
                                     src[:, g]).then_inc(raw_full[slot], 16)
                    return
                sp.dma_start(raw[:, slot, :].rearrange("p (k n) -> p k n", n=n), src)\
                    .then_inc(raw_full[slot], 16)

            def stage(name, src):
                c0, n, _ = STAGES[name]
                for c in range(n):
                    load(None, c0 + c, src(c))

            def ffn(layer):
                c0 = STAGES[f"ffn_in{layer}"][0]
                for c in range(2):
                    load(None, c0 + c, w_ffn_in[layer, c % 2, 0])
                with sp.Fori(0, 5) as i:
                    for j in range(4):
                        load(i, c0 + 2 + j, w_ffn_in[layer, j % 2, i * 2 + (1 + j // 2)])
                c0 = STAGES[f"ffn_out{layer}"][0]
                load(None, c0, w_ffn_out[layer, 0])
                with sp.Fori(0, 2) as i:
                    for j in range(4):
                        load(i, c0 + 1 + j, w_ffn_out[layer, i * 4 + (1 + j)])
                for c in (9, 10):
                    load(None, c0 + c, w_ffn_out[layer, c])

            sp.dma_start(ident, t["consts"][:, 0:128]).then_inc(s_ident, 16)
            sp.dma_start(x_tok[:, :, :], t["x"][0].rearrange("(a p) d -> p a d", p=P)).then_inc(s_x, 16)
            rows = (
                (0, "mix_norm", t["mix_norm"].rearrange("l (t p) -> (l t) p", p=P)),
                (0, "ffn_norm", t["ffn_norm"].rearrange("l (t p) -> (l t) p", p=P)),
                (0, "final_norm", t["final_norm"].rearrange("(t p) -> t p", p=P)),
                (0, "b_in", t["lru_b_in"][0].rearrange("(t p) -> t p", p=P)),
                (0, "conv_w", t["lru_conv_w"][0].rearrange("j (t p) -> (j t) p", p=P)),
                (0, "conv_b", t["lru_conv_b"][0].rearrange("(t p) -> t p", p=P)),
                (0, "gate_b", t["lru_gate_b"][0].rearrange("g (t p) -> (g t) p", p=P)),
                (1, "lam", t["lru_lambda"][0].rearrange("(t p) -> t p", p=P)),
                (1, "b_out", t["lru_b_out"][0].rearrange("(t p) -> t p", p=P)),
                (1, "norm_gain", t["norm_gain_2"][0].rearrange("(t p) -> t p", p=P)),
                (1, "lb", t["hgrn_lb_logits_2"][0].rearrange("(t p) -> t p", p=P)),
                (1, "hgrn_gain", t["hgrn_out_gain_2"][0].rearrange("(t p) -> t p", p=P)),
            )
            for tile, name, src in rows:
                r0 = COL[name] - tile * N_A
                sp.dma_start(prow[r0:r0 + src.shape[0], tile, :], src).then_inc(s_par, 16)
            for name in ("q_gain", "k_gain"):
                r0 = COL[name] - N_A
                for half in range(2):
                    sp.dma_start(prow[r0:r0 + 1, 1, 64 * half:64 * half + 64],
                                 t[name[0] + "_norm_gain_2"]).then_inc(s_par, 16)
            stage("rec_a", lambda c: w_in[4 + c])
            stage("gates_a", lambda c: w_gate[0])
            stage("rec_b", lambda c: w_in[7])
            stage("branch_a", lambda c: w_in[0])
            stage("gates_b", lambda c: w_gate[1])
            stage("branch_b", lambda c: w_in[1 + c])
            stage("lru_out", lambda c: w_lru_out[c])
            ffn(0)
            stage("qkv", lambda c: w_qkv[c % 3, c // 3])
            stage("attn_out", lambda c: w_o[c])
            ffn(1)
            stage("mix_in", lambda c: w_mix[MIX_ORDER[c]])
            stage("up_a", lambda c: w_up["w_up_a_2"][c])
            stage("up_b", lambda c: w_up["w_up_b_2"][c])
            stage("out2", lambda c: w_out2[c])
            stage("ple", lambda c: w_ple)
            stage("ple_gate", lambda c: w_pg[c])
            out_v = out[0].rearrange("(a p) d -> p a d", p=P)
            for j in range(4):
                sp.wait_ge(y_read, j + 1)
                sp.dma_start(out_v[:, :, j * S:(j + 1) * S], y_tok[:, :, j * S:(j + 1) * S])\
                    .then_inc(y_out, 16)
            sp.wait_ge(y_out, 64)

        @block.gpsimd
        def _(pool):
            def lo(i, c):
                pool.wait_ge(hi_done, at(i, 4, c + 1))
                nc.gpsimd.tensor_tensor(
                    wlo[:, c % RING, HALF:], raw[:, c % RAWS, HALF:],
                    whi[:, c % RING, HALF:].bitcast(F32), ALU.subtract).then_inc(lo_pool, 1)

            def branch_square(c):
                pool.wait_ge(br_z, c + 1)
                nc.gpsimd.tensor_tensor(gsq[:, c % 2, :], gel[:, c, :], gel[:, c, :], ALU.mult)\
                    .then_inc(br_sq, 1)

            def branch_cube(c):
                pool.wait_ge(br_cube, c + 1)
                nc.gpsimd.tensor_tensor(gsq[:, c % 2, :], gsq[:, c % 2, :], gel[:, c, :], ALU.mult)\
                    .then_inc(br_in, 1)

            def gated_input(n):
                pool.wait_ge(ig_ready, n + 1)
                nc.gpsimd.tensor_tensor(ig[:, n, :], ig[:, n, :], rc[:, n, :], ALU.mult)\
                    .then_inc(ix_ready, 1)

            for c in range(12):
                lo(None, c)
                if c == 8:
                    gated_input(0)
                    gated_input(1)
                    branch_square(0)
                if c == 9:
                    branch_cube(0)
                if c == 10:
                    branch_square(1)
                    branch_cube(1)
                    gated_input(2)
                    gated_input(3)
            with pool.Fori(3, CHUNKS // 4) as i:
                for j in range(4):
                    lo(i, j)
            for c in range(CHUNKS // 4 * 4, CHUNKS):
                lo(None, c)

        @block.tensor
        def _(pe):
            def chunk_ready(i, c):
                pe.wait_ge(hi_done, at(i, 4, c + 1))
                pe.wait_ge(lo_dve, at(i, 4, c + 1))
                pe.wait_ge(lo_pool, at(i, 4, c + 1))

            def product(dst, slot, w0, hi, lo, start, stop, shared=False):
                wh, wl = whi[:, slot, w0:w0 + P], wlo[:, slot, w0:w0 + P]
                nc.tensor.matmul(dst, wh, hi, start=start, stop=False, skip_group_check=shared)
                nc.tensor.matmul(dst, wh, lo, start=False, stop=False, skip_group_check=shared)
                return nc.tensor.matmul(dst, wl, hi, start=False, stop=stop, skip_group_check=shared)

            def product_tok(dst, slot, w0, hi, lo, start, stop):
                wh, wl = whi[:, slot, w0:w0 + S], wlo[:, slot, w0:w0 + S]
                nc.tensor.matmul(dst, hi, wh, start=start, stop=False)
                nc.tensor.matmul(dst, lo, wh, start=False, stop=False)
                return nc.tensor.matmul(dst, hi, wl, start=False, stop=stop)

            def columns_first(c, b, hi, lo, ready, count, k_tiles=DT, cols=S):
                chunk_ready(None, c)
                for q in range(cols // S):
                    pe.wait_ge(banks_read, b + q + 1)
                for k in range(k_tiles):
                    if k % 2 == 0:
                        pe.wait_ge(ready, count + k // 2 + 1)
                    for q in range(cols // S):
                        for m in range(2):
                            last = product(bank[(b + q) % 4][:, m * S:(m + 1) * S], c % RING,
                                           k * cols + q * S + m * P, hi[:, k, :], lo[:, k, :],
                                           k == 0 and m == 0, k == k_tiles - 1, True)
                last.then_inc(chunk_done, 1)

            def columns(i, c, b, hi, lo, k_tiles=DT, cols=S, tok=False):
                chunk_ready(i, c)
                for q in range(cols // S):
                    pe.wait_ge(banks_read, at(i, 4, b + q + 1))
                    dst = bank[(b + q) % 4]
                    for m in range(2):
                        for k in range(k_tiles):
                            ends = dict(start=k == 0, stop=k == k_tiles - 1)
                            d = dst[:, m * S:(m + 1) * S]
                            if tok:
                                last = product_tok(d, c % RING, k * cols, hi[:, k, m * P:(m + 1) * P],
                                                   lo[:, k, m * P:(m + 1) * P], **ends)
                            else:
                                last = product(d, c % RING, k * cols + q * S + m * P, hi[:, k, :],
                                               lo[:, k, :], **ends)
                last.then_inc(chunk_done, 1)

            def statistics(n):
                pe.wait_ge(ss_done, n + 1)
                nc.tensor.matmul(bank[7][:, 0:S], cst("mean_d"), ssum[:, 0:S], start=True, stop=False)
                nc.tensor.matmul(bank[7][:, 0:S], cst("mean_d"), ssum[:, S:], start=False, stop=True)\
                    .then_inc(mean_ready, 1)

            def token_factors(n, k):
                pe.wait_ge(rs_ready, n + 1)
                for m in range(2):
                    last = nc.tensor.matmul(bank[7][:, m:m + 1], rs[0:1, m * P:(m + 1) * P],
                                            ident[0:1, 0:1], start=True, stop=True)
                last.then_inc(rst_ready, 1)

            pe.wait_ge(s_ident, 16)
            pe.wait_ge(s_x, 16)
            for j in range(4):
                for m in range(2):
                    for a in range(2):
                        f0 = (2 * j + m) * P
                        last = nc.tensor.transpose(bank[j][:, m * S + a * P:m * S + (a + 1) * P],
                                                   x_tok[:, a, f0:f0 + P], ident)
                last.then_inc(chunk_done, 1)
            pe.wait_ge(s_par, 16 * 16)
            nc.tensor.transpose(bank[4][:, 0:N_A], prow[0:N_A, 0, :], ident[0:N_A, 0:N_A])
            nc.tensor.transpose(bank[4][:, N_A:N_A + N_B], prow[0:N_B, 1, :], ident[0:N_B, 0:N_B])\
                .then_inc(par_t, 1)

            pe.wait_ge(s_const, 16)
            def table_and_p():
                pe.wait_ge(s_relb, 16)
                pe.wait_ge(relb_pad, 1)
                nc.tensor.matmul(bank[5][0:8, 0:384], relb,
                                 const[0:33, CONST["bucket"]:CONST["bucket"] + 384],
                                 start=True, stop=True).then_inc(bkt_t, 1)
                pe.wait_ge(s_p, 16)
                for m in range(2):
                    for a in range(2):
                        last = nc.tensor.transpose(bank[6][:, m * S + a * P:m * S + (a + 1) * P],
                                                   p_tok[:, a, m * P:(m + 1) * P], ident)
                last.then_inc(p_t, 1)

            def gates(name, n0):
                c, _, b0 = STAGES[name]
                chunk_ready(None, c)
                for q in range(4):
                    n = n0 + q % 2
                    if q < 2:
                        pe.wait_ge(rc_lo, n + 1)
                    pe.wait_ge(banks_read, b0 + q + 1)
                    for m in range(2):
                        for k in range(2):
                            last = product(bank[(b0 + q) % 4][:, m * S:(m + 1) * S], c % RING,
                                           (2 * q + k) * S + m * P, rchi[:, 2 * n + k, :],
                                           rclo[:, 2 * n + k, :], k == 0, k == 1)
                    last.then_inc(gate_mm if q < 3 else chunk_done, 1)

            c0, _, b0 = STAGES["rec_a"]
            columns_first(c0, b0, xhi, xlo, x_lo, 0)
            statistics(0)
            columns(None, c0 + 1, b0 + 1, xhi, xlo)
            table_and_p()
            columns(None, c0 + 2, b0 + 2, xhi, xlo)
            gates("gates_a", 0)
            for name in ("rec_b", "branch_a"):
                columns(None, STAGES[name][0], STAGES[name][2], xhi, xlo)
            gates("gates_b", 2)
            c0, _, b0 = STAGES["branch_b"]
            for c in range(3):
                columns(None, c0 + c, b0 + c, xhi, xlo)
            c0, _, b0 = STAGES["lru_out"]
            columns_first(c0, b0, yhi, ylo, y_lo, 0)
            for c in range(1, 4):
                columns(None, c0 + c, b0 + c, yhi, ylo)

            def ffn(layer):
                c0, _, b0 = STAGES[f"ffn_in{layer}"]
                n = 1 + 2 * layer
                columns_first(c0, b0, xhi, xlo, x_lo, 4 * n)
                statistics(n)
                columns(None, c0 + 1, b0 + 1, xhi, xlo)
                with pe.Fori(0, 5) as i:
                    for j in range(2, 6):
                        columns(i, c0 + j, b0 + j, xhi, xlo)
                c0 = STAGES[f"ffn_out{layer}"][0]

                def rows(i, c, hi, lo, first, final):
                    chunk_ready(i, c0 + c)
                    for m in range(DT):
                        for k in range(2):
                            last = product(bank[4 + m // 2][:, m % 2 * S:(m % 2 + 1) * S],
                                           (c0 + c) % RING, k * D + m * P, hi(k), lo(k),
                                           first and k == 0 and m % 2 == 0, final and k == 1, True)
                    last.then_inc(chunk_done, 1)

                def rows_at(c):
                    pe.wait_ge(g_lo, FFN_PAIRS * layer + c + 1)
                    rows(None, c, lambda k: ghi[:, c, k * S:(k + 1) * S],
                         lambda k: glo[:, c, k * S:(k + 1) * S], c == 0, c == FFN_PAIRS - 1)

                pe.wait_ge(sd_ready, n + 1)
                rows_at(0)
                with pe.Fori(0, 2) as i:
                    for j in range(1, 5):
                        pe.wait_ge(g_lo, at(i, 4, FFN_PAIRS * layer + j + 1))
                        rows(i, j, lambda k: ghi[:, i * 4 + j, k * S:(k + 1) * S],
                             lambda k: glo[:, i * 4 + j, k * S:(k + 1) * S], False, False)
                rows_at(9)
                rows_at(10)

            pe.wait_ge(p_lo, 1)
            pe.wait_ge(bkt_done, 1)
            ffn(0)

            c0, _, b0 = STAGES["qkv"]

            def logits(g):
                pe.wait_ge(banks_read, b0 + 3 * g + 2 + 4)
                if g:
                    pe.wait_ge(o_lo, g)
                for n in range(4):
                    r0, f = 64 * (n % 2), n // 2
                    if g == 0 and n == 3:
                        pe.wait_ge(rst_read, 1)
                    q = qa[r0:r0 + 64, g % 2, f, :]
                    k = ka[r0:r0 + 64, g % 2, f, :]
                    nc.tensor.matmul(bank[4 + n][:, 0:S], k[:, 0:P], q, start=True, stop=True)
                    nc.tensor.matmul(bank[4 + n][:, S:384], k[:, P:S], q[:, P:S], start=True, stop=True)\
                        .then_inc(z_mm, 1)

            def suffixes(g):
                pe.wait_ge(nl_ready, g + 1)
                for n in range(4):
                    pe.wait_ge(z_read, 4 * g + n + 1)
                    nc.tensor.matmul(bank[4 + n][:, 0:S], cst("suffix"), nl[:, n, 0:S],
                                     start=True, stop=False)
                    nc.tensor.matmul(bank[4 + n][:, P:S], cst("neg"), nl[:, n, S:384],
                                     start=False, stop=True)
                    nc.tensor.matmul(bank[4 + n][:, S:384], cst("suffix"), nl[:, n, S:384],
                                     start=True, stop=True).then_inc(s_mm, 1)

            def weighted_values(g):
                pe.wait_ge(w_ready, g + 1)
                pe.wait_ge(banks_read, b0 + 3 * g + 3 + 4)
                for n in range(4):
                    r0, f = 64 * (n % 2), n // 2
                    dst = bank[4][r0:r0 + 64, f * S:(f + 1) * S]
                    v = va[:, g % 2, :, 64 * n:64 * n + 64]
                    nc.tensor.matmul(dst, v[:, 0, :], ww[:, n, 0:S], start=True, stop=False)
                    last = nc.tensor.matmul(dst[:, P:S], v[:, 1, :], ww[:, n, S:384],
                                            start=False, stop=True)
                last.then_inc(pv_mm, 1)

            for g in range(GROUPS):
                for q in range(3):
                    if g == q == 0:
                        columns_first(c0, b0, xhi, xlo, x_lo, 8)
                    else:
                        columns(None, c0 + 3 * g + q, b0 + 3 * g + q, xhi, xlo, tok=q == 2)
                    if g == 0 and q == 0:
                        statistics(2)
                    if g == 0 and q == 1:
                        pe.wait_ge(sd_ready, 3)
                        token_factors(2, 0)
                    if g:
                        (logits, suffixes, weighted_values)[q](g - 1)
            for step in (logits, suffixes, weighted_values):
                step(GROUPS - 1)
            c0, _, b0 = STAGES["attn_out"]
            o_h = ohi[:, :, :].rearrange("p a (b n) -> p (a b) n", n=S)
            o_l = olo[:, :, :].rearrange("p a (b n) -> p (a b) n", n=S)
            columns_first(c0, b0, o_h, o_l, o_lo, 0)
            for c in range(1, 4):
                columns(None, c0 + c, b0 + c, o_h, o_l)
            ffn(1)

            pe.wait_ge(bias_in, 16)
            for n in range(4):
                pe.wait_ge(acc_read, 4 + n + 1)
                nc.tensor.matmul(bank[4 + n][:, :], cst("anti"),
                                 bias_rev[:, 2 * n:2 * n + 2, :].rearrange("p a n -> p (a n)"),
                                 start=True, stop=True).then_inc(bias_mm, 1)
            pe.wait_ge(bias_read, 4)
            statistics(4)

            c0, _, b0 = STAGES["mix_in"]

            def head_squares(kind):
                pe.wait_ge(msq, kind + 1)
                src = (e_even, qe)[kind]
                if kind == 1:
                    pe.wait_ge(rst_read, 2)
                for n in range(2):
                    last = nc.tensor.matmul(bank[4 + 2 * kind + n][:, :], cst("mean_head"),
                                            src[:, n * PAIR:(n + 1) * PAIR], start=True, stop=True)
                last.then_inc(mss, 1)

            def moba_scores(g):
                pe.wait_ge(mn_ready, 2)
                if g:
                    pe.wait_ge(mpv_read, g)
                for n in range(4):
                    r0, f = 64 * (n % 2), 2 * g + n // 2
                    q, k = mq[r0:r0 + 64, f, :], mk[r0:r0 + 64, f, :]
                    nc.tensor.matmul(bank[4 + n][:, 0:S], q[:, P:S], k, start=True, stop=True)
                    nc.tensor.matmul(bank[4 + n][:, S:384], q[:, 0:P], k[:, 0:P], start=True, stop=True)\
                        .then_inc(sc_mm, 1)

            def moba_transposes(g):
                for n in range(4):
                    pe.wait_ge(p_ready, 4 * g + n + 1)
                    for d0, s0 in ((0, S), (P, 0), (S, P)):
                        last = nc.tensor.transpose(bank[4 + n][:, d0:d0 + P], pp_[:, n, s0:s0 + P], ident)
                    last.then_inc(pt_mm, 1)

            def moba_values(g):
                for n in range(4):
                    pe.wait_ge(pt_read, 4 * g + n + 1)
                pe.wait_ge(banks_read, b0 + 6 + 4)
                for n in range(4):
                    r0, f = 64 * (n % 2), n // 2
                    hd = 4 * g + n
                    dst = bank[4][r0:r0 + 64, f * S:(f + 1) * S]
                    nc.tensor.matmul(dst, mv[:, 0, 64 * hd:64 * hd + 64], pt[:, n, 0:S],
                                     start=True, stop=False)
                    last = nc.tensor.matmul(dst[:, P:S], mv[:, 1, 64 * hd:64 * hd + 64],
                                            pt[:, n, S:384], start=False, stop=True)
                last.then_inc(mpv_mm, 1)

            def level(j):
                pe.wait_ge(lv_ready, j + 1)
                pair = 4 + 2 * (j % 2)
                if j >= 2:
                    pe.wait_ge(lv_read, j - 1)
                else:
                    pe.wait_ge(mpv_read, 2)
                q, k = (qb[:, :, :].rearrange("p a n -> p (a n)"),
                        kb[:, :, :].rearrange("p a n -> p (a n)")) if j == 0 else (qe, ke)
                for n in range(HGRN_HEADS):
                    if LEVELS[j] == P:
                        last = nc.tensor.matmul(bank[pair][:, n * P:(n + 1) * P],
                                                k[:, n * S:n * S + P], q[:, n * S + P:(n + 1) * S],
                                                start=True, stop=True)
                        continue
                    for a in range(2):
                        u = 2 * n + a
                        last = nc.tensor.matmul(bank[pair + u // 4][:, u % 4 * P:(u % 4 + 1) * P],
                                                k[:, u * P:(u + 1) * P], q[:, u * P:(u + 1) * P],
                                                start=True, stop=True)
                last.then_inc(lv_mm, 1)

            plan = {
                0: [lambda: statistics(5)],
                1: [lambda: (pe.wait_ge(sd_ready, 6), token_factors(5, 1))],
                2: [lambda: head_squares(0)],
                4: [lambda: head_squares(1)],
                6: [lambda: moba_scores(0)],
                8: [lambda: moba_transposes(0)],
                9: [lambda: moba_values(0)],
                10: [lambda: moba_scores(1)],
                12: [lambda: moba_transposes(1)],
                13: [lambda: moba_values(1)],
            }
            for j in range(len(LEVELS)):
                plan[14 + j] = [lambda j=j: level(j)]
            for c in range(24):
                if c == 0:
                    columns_first(c0, b0, xhi, xlo, x_lo, 16)
                else:
                    columns(None, c0 + c, b0 + c, xhi, xlo, tok=c in (4, 5, 10, 11))
                for todo in plan.get(c, ()):
                    todo()

            def hgrn_outputs():
                pe.wait_ge(lv_read, len(LEVELS))
                for n in range(HGRN_HEADS):
                    dst = bank[4 + n // 2][:, n % 2 * S:(n % 2 + 1) * S]
                    v0, v1 = vb[:, 0, n * P:(n + 1) * P], vb[:, 1, n * P:(n + 1) * P]
                    nc.tensor.matmul(dst[:, 0:P], v0, score[:, 2 * n, :], start=True, stop=True)
                    nc.tensor.matmul(dst[:, P:S], v0, cross[:, n, :], start=True, stop=False)
                    last = nc.tensor.matmul(dst[:, P:S], v1, score[:, 2 * n + 1, :],
                                            start=False, stop=True)
                last.then_inc(yo_mm, 1)

            def hgrn_squares():
                pe.wait_ge(yo_sq, 1)
                for n in range(2):
                    last = nc.tensor.matmul(bank[6 + n][:, :], cst("mean_v"),
                                            e_even[:, n * PAIR:(n + 1) * PAIR], start=True, stop=True)
                last.then_inc(yo_mean, 1)

            hgrn_outputs()
            pe.wait_ge(ya_lo, 2)
            c0, _, b0 = STAGES["up_a"]
            columns(None, c0, b0, yahi, yalo, k_tiles=4, cols=512)
            hgrn_squares()
            columns(None, c0 + 1, b0 + 2, yahi, yalo, k_tiles=4, cols=512)
            c0, _, b0 = STAGES["up_b"]
            columns_first(c0, b0, ybhi, yblo, yb_lo, 0, k_tiles=4, cols=512)
            columns(None, c0 + 1, b0 + 2, ybhi, yblo, k_tiles=4, cols=512)
            c0, _, b0 = STAGES["out2"]
            columns_first(c0, b0, mhi, mlo, m_lo, 0)
            for c in range(1, 4):
                columns(None, c0 + c, b0 + c, mhi, mlo)
            c0, _, b0 = STAGES["ple"]
            columns(None, c0, b0, phi, plo, k_tiles=2, cols=D)
            c0, _, b0 = STAGES["ple_gate"]

            def to_tokens(j):
                pe.wait_ge(fin_ready, j + 1)
                if j == 0:
                    pe.wait_ge(yo_read, 1)
                for a in range(2):
                    for m in range(2):
                        last = nc.tensor.transpose(
                            bank[4 + j][:, a * S + m * P:a * S + (m + 1) * P],
                            h[:, j, m * S + a * P:m * S + (a + 1) * P], ident)
                last.then_inc(y_t, 1)

            columns_first(c0, b0, xhi, xlo, x_lo, 20)
            for c in range(1, 4):
                columns(None, c0 + c, b0 + c, xhi, xlo)
                to_tokens(c - 1)
            to_tokens(3)

        @block.scalar
        def _(act):
            own = [0]

            def link(ins):
                own[0] += 1
                ins.then_inc(act_own, 1)
                act.wait_ge(act_own, own[0])

            def split(i, c):
                gate_chunks = sum(g <= c and g % RAWS == c % RAWS for g in
                                  (STAGES["gates_a"][0], STAGES["gates_b"][0]))
                act.wait_ge(raw_full[c % RAWS], at(i, 32, 16 * (c // RAWS + 1 + gate_chunks)))
                act.wait_ge(chunk_done, at(i, 4, c + 1))
                nc.scalar.activation(whi[:, c % RING, :], raw[:, c % RAWS, :], ACT.Copy)\
                    .then_inc(hi_done, 1)

            def ahead(c):
                if c + AHEAD < CHUNKS:
                    split(None, c + AHEAD)

            def pair(tensor, j):
                return tensor[:, 2 * j:2 * j + 2, :].rearrange("p a n -> p (a n)")

            def norm_square(n, j):
                if j == 0:
                    if n:
                        act.wait_ge(mean_ready, n)
                    dst = ssum[:, :]
                else:
                    if 3 * n + (j == 3):
                        act.wait_ge(ss_acc, 3 * n + (j == 3))
                    if n and j == 2:
                        act.wait_ge(rs_ready, n)
                    dst = sq[:, j % 2, :]
                nc.scalar.activation(dst, h[:, j, :], ACT.Square).then_inc(sq_ready, 1)

            def norm_pair(n, xn, j):
                act.wait_ge(xg_ready, 4 * xn + j + 1)
                nc.scalar.activation(pair(xhi, j), xg[:, j % 2, :], ACT.Copy).then_inc(x_hi, 1)
                norm_square(n, j)

            def norm_root(n):
                act.wait_ge(mean_ready, n + 1)
                nc.scalar.activation(sq[:, 0, 0:S], bank[7][:, 0:S], ACT.Sqrt, bias=eps)\
                    .then_inc(sd_ready, 1)

            act.dma_start(const[:, 128:], t["consts"][:, 128:]).then_inc(s_const, 16)
            act.dma_start(small[0:32, 84:92], t["rel_bias_2"]).then_inc(s_relb, 16)
            act.dma_start(p_tok[:, :, :], t["p_2"][0, 0].rearrange("(a p) d -> p a d", p=P))\
                .then_inc(s_p, 16)
            for j in range(4):
                norm_pair(0, 0, j)
            for c in range(AHEAD):
                split(None, c)
            norm_root(0)
            lam = par[:, COL["lam"]:COL["lam"] + 8]
            act.wait_ge(par_done, 1)
            link(nc.scalar.activation(sp_a, lam, ACT.Abs))
            link(nc.scalar.activation(sp_a, sp_a, ACT.Exp, scale=-1.0))
            link(nc.scalar.activation(sp_a, sp_a, ACT.Ln, bias=1.0))
            nc.scalar.activation(lb_b, lb_a, ACT.Exp).then_inc(sp_abs, 1)

            def rec_hi(j):
                act.wait_ge(rc_ready, j + 1)
                nc.scalar.activation(pair(rchi, j), rc[:, j, :], ACT.Copy).then_inc(rc_hi, 1)

            def gate_sigmoids(name, n0):
                c, _, b0 = STAGES[name]
                act.wait_ge(banks_read, b0 - 1 + 5)
                for q in range(4):
                    if q < 3:
                        act.wait_ge(gate_mm, 3 * (n0 // 2) + q + 1)
                    else:
                        act.wait_ge(chunk_done, c + 5)
                    n = n0 + q % 2
                    for m in range(2):
                        cols = slice(m * S, (m + 1) * S)
                        f = COL["gate_b"] + DT * (q // 2) + 2 * n + m
                        ins = nc.scalar.activation((rg, ig)[q // 2][:, n, cols],
                                                   bank[(b0 + q) % 4][:, cols], ACT.Sigmoid,
                                                   bias=par[:, f:f + 1])
                    ins.then_inc(banks_read, 1)
                act.wait_ge(banks_read, b0 + 3 + 5)
                act.sem_inc(ig_ready, 2)

            def gate_decay(n0):
                for f in range(2 * n0, 2 * n0 + 4):
                    cols = slice(f % 2 * S, (f % 2 + 1) * S)
                    nc.scalar.activation(av[:, f // 2, cols], rg[:, f // 2, cols], ACT.Exp,
                                         scale=nc8[:, f:f + 1]).then_inc(a_ready, 1)
                for f in range(2 * n0, 2 * n0 + 4):
                    cols = slice(f % 2 * S, (f % 2 + 1) * S)
                    if f == 2 * n0:
                        act.wait_ge(a_ready, 4 * n0 + 4)
                    nc.scalar.activation(rg[:, f // 2, cols], rg[:, f // 2, cols], ACT.Tanh,
                                         scale=c8[:, f:f + 1]).then_inc(a_ready, 1)

            def gate_root(n0):
                for n in (n0, n0 + 1):
                    act.wait_ge(m2_ready, n + 1)
                    nc.scalar.activation(rg[:, n, :], rg[:, n, :], ACT.Sqrt).then_inc(mult_ready, 1)

            def branch_square(c):
                act.wait_ge(br_z, c + 1)
                nc.scalar.activation(gsq[:, c % 2, :], gel[:, c, :], ACT.Square).then_inc(br_sq, 1)

            def branch_tanh(c):
                act.wait_ge(br_in, c + 1)
                nc.scalar.activation(gsq[:, c % 2, :], gsq[:, c % 2, :], ACT.Tanh, scale=GELU_IN)\
                    .then_inc(br_tanh, 1)

            def y_hi_of(n):
                act.wait_ge(y_ready, n + 1)
                nc.scalar.activation(pair(yhi, n), rc[:, n, :], ACT.Copy).then_inc(y_hi, 1)

            c0 = STAGES["rec_a"][0]
            ahead(c0)
            ahead(c0 + 1)
            rec_hi(0)
            ahead(c0 + 2)
            rec_hi(1)
            act.wait_ge(p_t, 1)
            nc.scalar.activation(phi[:, :, :].rearrange("p a n -> p (a n)"), bank[6][:, :],
                                 ACT.Copy).then_inc(p_hi, 1)
            ahead(STAGES["gates_a"][0])
            rec_hi(2)
            act.wait_ge(bkt_done, 1)
            act.dma_start(bias_dram, bucket_bias[:, :]).then_inc(bkt_out, 16)
            gate_sigmoids("gates_a", 0)
            ahead(STAGES["rec_b"][0])
            gate_decay(0)
            ahead(STAGES["branch_a"][0])
            rec_hi(3)
            gate_root(0)
            ahead(STAGES["gates_b"][0])
            gate_sigmoids("gates_b", 2)
            c0 = STAGES["branch_b"][0]
            ahead(c0)
            gate_decay(2)
            ahead(c0 + 1)
            branch_tanh(0)
            gate_root(2)
            branch_square(2)
            ahead(c0 + 2)
            branch_tanh(1)
            act.wait_ge(bkt_out, 16)
            branch_tanh(2)
            y_hi_of(0)
            y_hi_of(1)
            branch_square(3)
            branch_tanh(3)
            y_hi_of(2)
            y_hi_of(3)
            c0 = STAGES["lru_out"][0]
            for c in range(4):
                ahead(c0 + c)
                norm_pair(1, 1, c)

            def ffn(layer):
                n = 1 + 2 * layer
                norm_root(n)
                c0, _, b0 = STAGES[f"ffn_in{layer}"]

                def gated(i, c, q, par_q):
                    split(i, c0 + c + AHEAD)
                    act.wait_ge(banks_read, at(i, 4, b0 + c + 5))
                    nc.scalar.activation(sg[:, par_q, :], tg[:, par_q, :], ACT.Sigmoid)\
                        .then_inc(sig_ready, 1)
                    split(i, c0 + c + 1 + AHEAD)
                    act.wait_ge(act_ready, at(i, 2, FFN_PAIRS * layer + q + 1))
                    dst = ghi[:, q, :] if i is None else ghi[:, i * 2 + q, :]
                    nc.scalar.activation(dst, tu[:, par_q, :], ACT.Copy).then_inc(g_hi, 1)

                gated(None, 0, 0, 0)
                with act.Fori(0, 5) as i:
                    for j in range(2):
                        gated(i, 2 + 2 * j, 1 + j, (1 + j) % 2)
                c0 = STAGES[f"ffn_out{layer}"][0]
                split(None, c0 + AHEAD)
                with act.Fori(0, 2) as i:
                    for j in range(4):
                        split(i, c0 + 1 + j + AHEAD)
                for c in (9, 10):
                    split(None, c0 + c + AHEAD)

            ffn(0)
            for j in range(4):
                norm_pair(2, 2, j)
            norm_root(2)

            c0, _, b0 = STAGES["qkv"]

            def whole(tensor):
                return tensor[:, :, :].rearrange("p a n -> p (a n)")

            def log_terms(g):
                act.wait_ge(z_read, 4 * g + 4)
                link(nc.scalar.activation(whole(ee), whole(zz), ACT.Abs))
                link(nc.scalar.activation(whole(ee), whole(ee), ACT.Exp, scale=-1.0))
                nc.scalar.activation(whole(ee), whole(ee), ACT.Ln, bias=1.0).then_inc(l_ready, 1)

            def weights(g):
                act.wait_ge(arg_ready, g + 1)
                nc.scalar.activation(whole(ww), whole(zz), ACT.Exp).then_inc(w_ready, 1)

            def outputs(g):
                act.wait_ge(pv_mm, g + 1)
                nc.scalar.activation(ohi[:, g, :], bank[4][:, :], ACT.Copy).then_inc(o_hi, 1)

            for g in range(GROUPS):
                for q in range(3):
                    ahead(c0 + 3 * g + q)
                    if q == 0 and g >= 2:
                        outputs(g - 2)
                    if q == 0 and g >= 1:
                        log_terms(g - 1)
                    if q == 2 and g >= 1:
                        weights(g - 1)
            outputs(GROUPS - 2)
            log_terms(GROUPS - 1)
            weights(GROUPS - 1)
            outputs(GROUPS - 1)
            act.wait_ge(bkt_out, 16)
            src = bass.AP(bias_dram.tensor, 0, [[1, P], [384, 8], [1, S]])
            act.dma_start(bias_rev[:, :, :], src).then_inc(bias_in, 16)
            c0 = STAGES["attn_out"][0]
            for c in range(4):
                ahead(c0 + c)
                norm_pair(3, 3, c)
            ffn(1)
            for j in range(4):
                act.wait_ge(acc_read, 4 + j + 1)
                norm_square(4, j)
            norm_root(4)
            for j in range(4):
                norm_pair(5, 4, j)
            norm_root(5)

            c0, _, b0 = STAGES["mix_in"]

            def sigmoid_to_tmp(c, src):
                act.wait_ge(banks_read, b0 + c + 5)
                nc.scalar.activation(xg[:, c % 2, :], src, ACT.Sigmoid).then_inc(gate_sig, 1)

            def head_square(kind):
                act.wait_ge(banks_read, b0 + 2 * kind + 2 + 4)
                src, dst = ((mq, e_even), (mk, qe))[kind]
                nc.scalar.activation(dst[:, :], whole(src), ACT.Square).then_inc(msq, 1)

            def head_root(kind):
                act.wait_ge(mss, kind + 1)
                dst = (e_even, qe)[kind]
                for n in range(2):
                    ins = nc.scalar.activation(dst[:, n * PAIR:(n + 1) * PAIR],
                                               bank[4 + 2 * kind + n][:, :], ACT.Ln, bias=eps)
                link(ins)
                nc.scalar.activation(dst[:, :], dst[:, :], ACT.Exp, scale=-0.5).then_inc(msd, 1)

            def moba_exp(g):
                act.wait_ge(nm_ready, g + 1)
                for n in range(4):
                    for m, (s0, s1) in enumerate(((0, S), (S, 384))):
                        col = 2 * n + m
                        ins = nc.scalar.activation(pp_[:, n, s0:s1], pp_[:, n, s0:s1], ACT.Exp,
                                                   bias=nmx[:, col:col + 1],
                                                   accum_out=sm[:, col:col + 1])
                        ins.then_inc(p_exp, 1)

            def moba_copies(g):
                for n in range(4):
                    act.wait_ge(pt_mm, 4 * g + n + 1)
                    nc.scalar.activation(pt[:, n, :], bank[4 + n][:, 0:384], ACT.Copy)\
                        .then_inc(pt_read, 1)

            def decay_exp():
                act.wait_ge(f_in, 1)
                link(nc.scalar.activation(lf[:, :], whole(fb), ACT.Abs))
                nc.scalar.activation(lf[:, :], lf[:, :], ACT.Exp, scale=-1.0)
                link(nc.scalar.activation(lf_b[:, :], lf_b[:, :], ACT.Exp))

            def decay_ln():
                for n in range(HGRN_HEADS):
                    nc.scalar.activation(lf_b[:, n * S:(n + 1) * S], lf_b[:, n * S:(n + 1) * S], ACT.Ln,
                                         scale=lbv[:, n:n + 1], bias=1.0)
                nc.scalar.activation(lf[:, :], lf[:, :], ACT.Ln, bias=1.0).then_inc(f_ready, 1)

            def level(j):
                e = (e_even, e_odd)[j % 2]
                act.wait_ge(lv_sub, j)
                link(nc.scalar.activation(e[:, :], e[:, :], ACT.Abs))
                nc.scalar.activation(e[:, :], e[:, :], ACT.Exp, scale=-1.0).then_inc(lv_exp, 1)

            def split_out(n, ready, src, dst, done):
                act.wait_ge(ready, n + 1)
                nc.scalar.activation(dst, src, ACT.Copy).then_inc(done, 1)

            def gate(tensor, c, j):
                act.wait_ge(banks_read, b0 + c + 5)
                nc.scalar.activation(tensor[:, j, :], tensor[:, j, :], ACT.Sigmoid).then_inc(gate_sig, 1)

            for c in range(24):
                ahead(c0 + c)
                if c == 1:
                    head_square(0)
                if c == 3:
                    head_root(0)
                    head_square(1)
                if c == 5:
                    head_root(1)
                if c == 7:
                    moba_exp(0)
                if c == 8:
                    decay_exp()
                if c == 9:
                    moba_copies(0)
                    decay_ln()
                if c == 10:
                    nc.scalar.activation(whole(kb), whole(fb), ACT.Sigmoid, scale=-1.0).then_inc(k_sig, 1)
                    sigmoid_to_tmp(8, qb[:, 0, :])
                    sigmoid_to_tmp(9, qb[:, 1, :])
                if c == 11:
                    moba_exp(1)
                if c == 13:
                    moba_copies(1)
                if c == 14:
                    sigmoid_to_tmp(12, ag[:, 0, :])
                    sigmoid_to_tmp(13, ag[:, 1, :])
                    for n in range(2):
                        split_out(n, ya_ready, ya[:, n, :], pair(yahi, n), ya_hi)
                if c >= 14 and c - 13 < len(LEVELS):
                    level(c - 13)
                if c == 22:
                    sigmoid_to_tmp(14, bg[:, 0, :])
                    sigmoid_to_tmp(15, bg[:, 1, :])
                    for n in range(4):
                        gate(ga, 16 + n, n)
                if c == 23:
                    for n in range(4):
                        gate(gb, 20 + n, n)
            act.wait_ge(yo_mm, 1)
            for n in range(2):
                ins = nc.scalar.activation(e_even[:, n * PAIR:(n + 1) * PAIR], bank[4 + n][:, :], ACT.Square)
            ins.then_inc(yo_sq, 1)
            ahead(STAGES["up_a"][0])
            act.wait_ge(yo_mean, 1)
            for n in range(2):
                ins = nc.scalar.activation(qe[:, n * PAIR:(n + 1) * PAIR], bank[6 + n][:, :],
                                           ACT.Ln, bias=eps)
            link(ins)
            nc.scalar.activation(qe[:, :], qe[:, :], ACT.Exp, scale=-0.5).then_inc(yo_sd, 1)
            ahead(STAGES["up_a"][0] + 1)
            for n in range(2):
                split_out(n, yb_ready, ke[:, n * PAIR:(n + 1) * PAIR], pair(ybhi, n), yb_hi)
            for c in range(2):
                ahead(STAGES["up_b"][0] + c)
                for n in (2 * c, 2 * c + 1):
                    split_out(n, m_ready, ga[:, n, :], pair(mhi, n), m_hi)
            for c in range(4):
                ahead(STAGES["out2"][0] + c)
                split_out(20 + c, xg_ready, h[:, c, :], pair(xhi, c), x_hi)
            ahead(STAGES["ple"][0])
            for c in range(4):
                ahead(STAGES["ple_gate"][0] + c)
                act.wait_ge(ple_in, c + 1)
                nc.scalar.activation(xg[:, c % 2, :], xg[:, c % 2, :], ACT.Sigmoid).then_inc(ple_sig, 1)
            for j in range(4):
                act.wait_ge(y_t, j + 1)
                nc.scalar.activation(y_tok[:, :, j * S:(j + 1) * S],
                                     bank[4 + j][:, :].rearrange("p (a n) -> p a n", a=2),
                                     ACT.Copy).then_inc(y_read, 1)

        @block.vector
        def _(dve):
            own = [0]

            def mark(ins):
                own[0] += 1
                ins.then_inc(dve_own, 1)
                return own[0]

            def link(ins):
                dve.wait_ge(dve_own, mark(ins))

            def split(i, c):
                dve.wait_ge(hi_done, at(i, 4, c + 1))
                nc.vector.tensor_tensor(wlo[:, c % RING, :HALF], raw[:, c % RAWS, :HALF],
                                        whi[:, c % RING, :HALF].bitcast(F32), ALU.subtract)\
                    .then_inc(lo_dve, 1)

            def ahead(c):
                if c + AHEAD < CHUNKS:
                    split(None, c + AHEAD)

            def pair(tensor, j):
                return tensor[:, 2 * j:2 * j + 2, :].rearrange("p a n -> p (a n)")

            def whole(tensor):
                return tensor[:, :, :].rearrange("p a n -> p (a n)")

            def col(name, n=0):
                return par[:, COL[name] + n:COL[name] + n + 1]

            def norm_gain(n, xn, j, gain):
                if 4 * xn + j >= 2:
                    dve.wait_ge(x_lo, 4 * xn + j - 1)
                    dve.wait_ge(x_hi, 4 * xn + j - 1)
                for m in range(2):
                    ins = nc.vector.tensor_scalar(xg[:, j % 2, m * S:(m + 1) * S],
                                                  h[:, j, m * S:(m + 1) * S],
                                                  par[:, gain + 2 * j + m:gain + 2 * j + m + 1], None,
                                                  ALU.mult)
                ins.then_inc(xg_ready, 1)

            def norm_lo(xn, j):
                dve.wait_ge(x_hi, 4 * xn + j + 1)
                nc.vector.tensor_tensor(pair(xlo, j), xg[:, j % 2, :], pair(xhi, j).bitcast(F32),
                                        ALU.subtract).then_inc(x_lo, 1)

            def norm_sum(n, j):
                dve.wait_ge(sq_ready, 4 * n + j + 1)
                if j:
                    if j > 1:
                        dve.wait_ge(ss_acc, 3 * n + j - 1)
                    nc.vector.tensor_tensor(ssum[:, :], ssum[:, :], sq[:, j % 2, :], ALU.add)\
                        .then_inc(ss_acc, 1)
                    if j == 3:
                        dve.wait_ge(ss_acc, 3 * n + 3)
                        dve.sem_inc(ss_done, 1)

            def norm_factor(n):
                dve.wait_ge(sd_ready, n + 1)
                link(nc.vector.reciprocal(rs[:, 0:S], sq[:, 0, 0:S]))
                nc.vector.tensor_copy(rs[:, S:], rs[:, 0:S]).then_inc(rs_ready, 1)
                dve.wait_ge(rs_ready, n + 1)

            def token_factors(k):
                dve.wait_ge(rst_ready, k + 1)
                nc.vector.tensor_copy(rs_tok[:, :], bank[7][:, 0:2]).then_inc(rst_read, 1)
                dve.wait_ge(rst_read, k + 1)

            def norm(n, xn, gain, update):
                for j in range(4):
                    update(j)
                    norm_gain(n, xn, j, gain)
                    if j:
                        norm_lo(xn, j - 1)
                        norm_sum(n, j - 1)
                norm_lo(xn, 3)
                norm_sum(n, 3)

            def evacuate(i, c, b, dst, op=None):
                dve.wait_ge(chunk_done, at(i, 4, c + 5))
                nc.vector.tensor_tensor(dst, bank[b % 4][:, :], rs[:, :], ALU.mult)\
                    .then_inc(banks_read, 1)

            def read(b):
                dve.wait_ge(banks_read, b + 5)

            nc.vector.memset(eps, EPS)
            for j in range(4):
                dve.wait_ge(chunk_done, j + 1)
                nc.vector.tensor_copy(h[:, j, :], bank[j][:, :]).then_inc(banks_read, 1)
            dve.wait_ge(par_t, 1)
            link(nc.vector.tensor_copy(par[:, :], bank[4][:, 0:N_A + N_B]))
            link(nc.vector.tensor_tensor(lb_a, par[:, COL["lb"]:COL["lb"] + 4],
                                         par[:, COL["lb"]:COL["lb"] + 4], ALU.subtract))
            nc.vector.memset(small[32:33, 84:92], MASKED).then_inc(relb_pad, 1)
            nc.vector.tensor_scalar(q_gain, col("q_gain"), 0.125, None, ALU.mult).then_inc(par_done, 1)
            dve.wait_ge(par_done, 1)
            norm(0, 0, COL["mix_norm"], lambda j: dve.wait_ge(banks_read, j + 1))
            for c in range(AHEAD):
                split(None, c)
            norm_factor(0)
            lam = par[:, COL["lam"]:COL["lam"] + 8]
            dve.wait_ge(sp_abs, 1)
            link(nc.vector.tensor_scalar(sp_b, lam, -1.0, 0.0, ALU.mult, ALU.max))
            link(nc.vector.tensor_tensor(sp_b, sp_b, sp_a, ALU.add))
            nc.vector.tensor_scalar(c8, sp_b, LRU_C, None, ALU.mult)
            link(nc.vector.tensor_scalar(nc8, sp_b, -LRU_C, None, ALU.mult))
            link(nc.vector.reciprocal(lb_a, lb_b))
            link(nc.vector.tensor_tensor(lb_a, lb_a, lb_b, ALU.mult))
            link(nc.vector.tensor_tensor(lbv, lb_a, lb_a, ALU.subtract))
            link(nc.vector.tensor_scalar(omlb, lbv, -1.0, 1.0, ALU.mult, ALU.add))

            b_rec = par[:, COL["b_in"] + DT:COL["b_in"] + 2 * DT]
            nc.vector.tensor_scalar(recp[:, :, 0:3],
                                    b_rec.rearrange("p (f o) -> p f o", o=1).broadcast_to([P, DT, 3]),
                                    -1.0, None, ALU.mult)
            taps = [par[:, COL["conv_w"] + n * DT:COL["conv_w"] + (n + 1) * DT] for n in range(4)]
            link(nc.vector.tensor_tensor(conv_bias, taps[0], taps[1], ALU.add))
            link(nc.vector.tensor_tensor(conv_bias, conv_bias, taps[2], ALU.add))
            link(nc.vector.tensor_tensor(conv_bias, conv_bias, taps[3], ALU.add))
            link(nc.vector.tensor_tensor(conv_bias, conv_bias, b_rec, ALU.mult))
            link(nc.vector.tensor_tensor(conv_bias, conv_bias, par[:, COL["conv_b"]:COL["conv_b"] + DT],
                                         ALU.add))

            def recurrent(name, c, j):
                c0, _, b0 = STAGES[name]
                dve.wait_ge(banks_read, b0 + c - 1 + 5)
                dve.wait_ge(chunk_done, c0 + c + 5)
                nc.vector.tensor_tensor(recp[:, 2 * j:2 * j + 2, 3:],
                                        bank[(b0 + c) % 4][:, :].rearrange("p (a n) -> p a n", a=2),
                                        rs[:, :].rearrange("p (a n) -> p a n", a=2), ALU.mult)\
                    .then_inc(banks_read, 1)
                read(b0 + c)

            def convolve(j):
                for tap in (3, 2, 1, 0):
                    marks = []
                    for m in range(2):
                        f = 2 * j + m
                        dst = rc[:, j, m * S:(m + 1) * S]
                        w = col("conv_w", tap * DT + f)
                        if tap == 3:
                            marks.append(mark(nc.vector.tensor_scalar(
                                dst, recp[:, f, tap:tap + S], w, conv_bias[:, f:f + 1], ALU.mult,
                                ALU.add)))
                        else:
                            dve.wait_ge(dve_own, before[m])
                            ins = nc.vector.scalar_tensor_tensor(
                                out=dst, in0=recp[:, f, tap:tap + S], scalar=w, in1=dst,
                                op0=ALU.mult, op1=ALU.add)
                            if tap == 0 and m == 1:
                                ins.then_inc(rc_ready, 1)
                            else:
                                marks.append(mark(ins))
                    before = marks

            def conv_lo(j):
                dve.wait_ge(rc_ready, j + 1)
                dve.wait_ge(rc_hi, j + 1)
                nc.vector.tensor_tensor(pair(rclo, j), rc[:, j, :], pair(rchi, j).bitcast(F32),
                                        ALU.subtract).then_inc(rc_lo, 1)

            def branch(name, c, j):
                c0, _, b0 = STAGES[name]
                dve.wait_ge(banks_read, b0 + c - 1 + 5)
                evacuate(None, c0 + c, b0 + c, gel[:, j, :])
                read(b0 + c)
                for m in range(2):
                    z = gel[:, j, m * S:(m + 1) * S]
                    ins = nc.vector.tensor_scalar(z, z, col("b_in", 2 * j + m), None, ALU.add)
                ins.then_inc(br_z, 1)

            def branch_poly(j):
                dve.wait_ge(br_sq, j + 1)
                nc.vector.tensor_scalar(gsq[:, j % 2, :], gsq[:, j % 2, :], GELU_CUBE, 1.0,
                                        ALU.mult, ALU.add).then_inc(br_cube, 1)

            def branch_cube(j):
                dve.wait_ge(br_cube, j + 1)
                nc.vector.tensor_tensor(gsq[:, j % 2, :], gsq[:, j % 2, :], gel[:, j, :], ALU.mult)\
                    .then_inc(br_in, 1)

            def branch_gelu(j):
                dve.wait_ge(br_tanh, j + 1)
                link(nc.vector.scalar_tensor_tensor(out=gel[:, j, :], in0=gsq[:, j % 2, :], scalar=1.0,
                                                    in1=gel[:, j, :], op0=ALU.add, op1=ALU.mult))

            def one_less_a2(n):
                dve.wait_ge(a_ready, 8 * (n // 2) + 6 + 2 * (n % 2))
                link(nc.vector.tensor_tensor(xg[:, n % 2, :], av[:, n, :], av[:, n, :], ALU.mult))
                nc.vector.scalar_tensor_tensor(out=rg[:, n, :], in0=xg[:, n % 2, :], scalar=1.0,
                                               in1=rg[:, n, :], op0=ALU.add, op1=ALU.mult)\
                    .then_inc(m2_ready, 1)
                dve.wait_ge(m2_ready, n + 1)

            def scan(n):
                dve.wait_ge(ix_ready, n + 1)
                dve.wait_ge(mult_ready, n + 1)
                link(nc.vector.tensor_tensor(rg[:, n, :], rg[:, n, :], ig[:, n, :], ALU.mult))
                for m in range(2):
                    cols = slice(m * S, (m + 1) * S)
                    ins = nc.vector.tensor_tensor_scan(ig[:, n, cols], av[:, n, cols], rg[:, n, cols],
                                                       0.0, ALU.mult, ALU.add)
                link(ins)

            def output(n):
                nc.vector.scalar_tensor_tensor(out=rc[:, n, :], in0=gel[:, n, :], scalar=0.5,
                                               in1=ig[:, n, :], op0=ALU.mult, op1=ALU.mult)\
                    .then_inc(y_ready, 1)

            def output_lo(n):
                dve.wait_ge(y_ready, n + 1)
                dve.wait_ge(y_hi, n + 1)
                nc.vector.tensor_tensor(pair(ylo, n), rc[:, n, :], pair(yhi, n).bitcast(F32),
                                        ALU.subtract).then_inc(y_lo, 1)

            c0 = STAGES["rec_a"][0]
            for c in range(3):
                ahead(c0 + c)
                if c:
                    conv_lo(c - 1)
                recurrent("rec_a", c, c)
                convolve(c)
                if c == 1:
                    dve.wait_ge(bkt_t, 1)
                    nc.vector.tensor_copy(bucket_bias[:, :], bank[5][0:8, 0:384]).then_inc(bkt_done, 1)
            ahead(STAGES["gates_a"][0])
            conv_lo(2)
            dve.wait_ge(p_hi, 1)
            nc.vector.tensor_tensor(whole(plo), bank[6][:, :], whole(phi).bitcast(F32),
                                    ALU.subtract).then_inc(p_lo, 1)
            ahead(STAGES["rec_b"][0])
            recurrent("rec_b", 0, 3)
            convolve(3)
            ahead(STAGES["branch_a"][0])
            conv_lo(3)
            one_less_a2(0)
            one_less_a2(1)
            branch("branch_a", 0, 0)
            ahead(STAGES["gates_b"][0])
            branch_poly(0)
            scan(0)
            scan(1)
            c0 = STAGES["branch_b"][0]
            ahead(c0)
            branch("branch_b", 0, 1)
            ahead(c0 + 1)
            branch_poly(1)
            branch_gelu(0)
            output(0)
            one_less_a2(2)
            one_less_a2(3)
            branch("branch_b", 1, 2)
            ahead(c0 + 2)
            branch_poly(2)
            branch_gelu(1)
            output(1)
            branch_cube(2)
            output_lo(0)
            scan(2)
            scan(3)
            branch_gelu(2)
            output(2)
            branch("branch_b", 2, 3)
            output_lo(1)
            branch_poly(3)
            branch_cube(3)
            output_lo(2)
            branch_gelu(3)
            output(3)
            output_lo(3)

            c0l, _, b0l = STAGES["lru_out"]

            def lru_residual(j):
                ahead(c0l + j)
                dve.wait_ge(chunk_done, c0l + j + 5)
                for m in range(2):
                    cols = slice(m * S, (m + 1) * S)
                    ins = nc.vector.scalar_tensor_tensor(
                        out=h[:, j, cols], in0=bank[(b0l + j) % 4][:, cols],
                        scalar=col("b_out", 2 * j + m), in1=h[:, j, cols], op0=ALU.add, op1=ALU.add)
                ins.then_inc(banks_read, 1)
                read(b0l + j)

            norm(1, 1, COL["ffn_norm"], lru_residual)

            def ffn(layer):
                n = 1 + 2 * layer
                norm_factor(n)
                c0, _, b0 = STAGES[f"ffn_in{layer}"]

                def gated(i, c, q, par_q):
                    split(i, c0 + c + AHEAD)
                    evacuate(i, c0 + c, b0 + c, tg[:, par_q, :])
                    split(i, c0 + c + 1 + AHEAD)
                    dve.wait_ge(sig_ready, at(i, 2, FFN_PAIRS * layer + q + 1))
                    dve.wait_ge(banks_read, at(i, 4, b0 + c + 5))
                    nc.vector.tensor_tensor(tg[:, par_q, :], tg[:, par_q, :], sg[:, par_q, :], ALU.mult)\
                        .then_inc(silu_ready, 1)
                    evacuate(i, c0 + c + 1, b0 + c + 1, tu[:, par_q, :])
                    dve.wait_ge(banks_read, at(i, 4, b0 + c + 6))
                    dve.wait_ge(silu_ready, at(i, 2, FFN_PAIRS * layer + q + 1))
                    nc.vector.tensor_tensor(tu[:, par_q, :], tg[:, par_q, :], tu[:, par_q, :], ALU.mult)\
                        .then_inc(act_ready, 1)
                    dve.wait_ge(act_ready, at(i, 2, FFN_PAIRS * layer + q + 1))
                    dve.wait_ge(g_hi, at(i, 2, FFN_PAIRS * layer + q + 1))
                    dst, hi = (glo[:, q, :], ghi[:, q, :]) if i is None else \
                        (glo[:, i * 2 + q, :], ghi[:, i * 2 + q, :])
                    nc.vector.tensor_tensor(dst, tu[:, par_q, :], hi.bitcast(F32), ALU.subtract)\
                        .then_inc(g_lo, 1)
                    dve.wait_ge(g_lo, at(i, 2, FFN_PAIRS * layer + q + 1))

                gated(None, 0, 0, 0)
                with dve.Fori(0, 5) as i:
                    for j in range(2):
                        gated(i, 2 + 2 * j, 1 + j, (1 + j) % 2)
                c0 = STAGES[f"ffn_out{layer}"][0]
                split(None, c0 + AHEAD)
                with dve.Fori(0, 2) as i:
                    for j in range(4):
                        split(i, c0 + 1 + j + AHEAD)
                for c in (9, 10):
                    split(None, c0 + c + AHEAD)
                dve.wait_ge(chunk_done, c0 + 10 + 5)

            def ffn_residual(layer):
                def update(j):
                    nc.vector.tensor_tensor(h[:, j, :], bank[4 + j][:, :], h[:, j, :], ALU.add)\
                        .then_inc(acc_read, 1)
                    dve.wait_ge(acc_read, 4 * layer + j + 1)
                return update

            ffn(0)
            norm(2, 2, COL["mix_norm"] + DT, ffn_residual(0))
            norm_factor(2)

            c0, _, b0 = STAGES["qkv"]

            def masked_logits(g):
                for n in range(4):
                    dve.wait_ge(z_mm, 4 * g + n + 1)
                    nc.vector.tensor_tensor(zz[:, n, :], bank[4 + n][:, 0:384], cst("causal", 384), ALU.add)\
                        .then_inc(z_read, 1)

            def neg_log_fail(g):
                dve.wait_ge(l_ready, g + 1)
                dve.wait_ge(z_read, 4 * g + 4)
                nc.vector.scalar_tensor_tensor(out=whole(nl), in0=whole(zz), scalar=0.0, in1=whole(ee),
                                               op0=ALU.max, op1=ALU.add).then_inc(nl_ready, 1)

            def exponents(g):
                dve.wait_ge(nl_ready, g + 1)
                for n in range(4):
                    dve.wait_ge(s_mm, 4 * g + n + 1)
                    ins = nc.vector.tensor_tensor(zz[:, n, :], zz[:, n, :], bank[4 + n][:, 0:384], ALU.add)
                ins.then_inc(arg_ready, 1)

            def outputs(g):
                dve.wait_ge(o_hi, g + 1)
                nc.vector.tensor_tensor(olo[:, g, :], bank[4][:, :], ohi[:, g, :].bitcast(F32),
                                        ALU.subtract).then_inc(o_lo, 1)

            for g in range(GROUPS):
                for q in range(3):
                    c, b = c0 + 3 * g + q, b0 + 3 * g + q
                    ahead(c)
                    if g and q == 1:
                        neg_log_fail(g - 1)
                    if g and q == 2:
                        exponents(g - 1)
                    if q == 0:
                        dve.wait_ge(chunk_done, c + 5)
                        nc.vector.scalar_tensor_tensor(out=whole(qa[:, g % 2]), in0=bank[b % 4][:, :],
                                                       scalar=0.125, in1=rs[:, :], op0=ALU.mult,
                                                       op1=ALU.mult).then_inc(banks_read, 1)
                    if q == 1:
                        evacuate(None, c, b, whole(ka[:, g % 2]))
                    if q == 2:
                        if g == 0:
                            token_factors(0)
                        dve.wait_ge(chunk_done, c + 5)
                        for m in range(2):
                            ins = nc.vector.tensor_scalar(va[:, g % 2, m, :], bank[b % 4][:, m * S:(m + 1) * S],
                                                          rs_tok[:, m:m + 1], None, ALU.mult)
                        ins.then_inc(banks_read, 1)
                    if q == 0 and g >= 2:
                        outputs(g - 2)
                    if g and q == 0:
                        if g >= 2:
                            dve.wait_ge(w_ready, g - 1)
                        masked_logits(g - 1)
            outputs(GROUPS - 2)
            dve.wait_ge(w_ready, GROUPS - 1)
            masked_logits(GROUPS - 1)
            neg_log_fail(GROUPS - 1)
            exponents(GROUPS - 1)
            outputs(GROUPS - 1)

            c0a, _, b0a = STAGES["attn_out"]

            def attn_residual(j):
                ahead(c0a + j)
                dve.wait_ge(chunk_done, c0a + j + 5)
                nc.vector.tensor_tensor(h[:, j, :], bank[(b0a + j) % 4][:, :], h[:, j, :], ALU.add)\
                    .then_inc(banks_read, 1)
                read(b0a + j)

            norm(3, 3, COL["ffn_norm"] + DT, attn_residual)
            ffn(1)
            for j in range(4):
                ffn_residual(1)(j)
                if j:
                    norm_sum(4, j - 1)
            norm_sum(4, 3)
            for n in range(4):
                dve.wait_ge(bias_mm, n + 1)
                nc.vector.tensor_copy(pair(bias, n), bank[4 + n][:, :]).then_inc(bias_read, 1)
            norm_factor(4)

            def final_norm(j):
                for m in range(2):
                    cols = slice(m * S, (m + 1) * S)
                    ins = nc.vector.scalar_tensor_tensor(
                        out=h[:, j, cols], in0=h[:, j, cols], scalar=col("final_norm", 2 * j + m),
                        in1=rs[:, 0:S], op0=ALU.mult, op1=ALU.mult)
                link(ins)

            norm(5, 4, COL["norm_gain"], final_norm)
            norm_factor(5)

            c0, _, b0 = STAGES["mix_in"]

            def silu(c, tensor, j, k):
                dve.wait_ge(gate_sig, k)
                link(nc.vector.tensor_tensor(tensor[:, j, :], tensor[:, j, :], xg[:, c % 2, :], ALU.mult))

            def token_values(c, dst, c_cols):
                dve.wait_ge(chunk_done, c0 + c + 5)
                for m in range(2):
                    ins = nc.vector.tensor_scalar(dst[:, m, c_cols:c_cols + S],
                                                  bank[(b0 + c) % 4][:, m * S:(m + 1) * S],
                                                  rs_tok[:, m:m + 1], None, ALU.mult)
                ins.then_inc(banks_read, 1)

            def head_norm(kind):
                src, den, gain = ((mq, e_even, q_gain), (mk, qe, col("k_gain")))[kind]
                dve.wait_ge(msd, kind + 1)
                nc.vector.scalar_tensor_tensor(out=whole(src), in0=whole(src), scalar=gain,
                                               in1=den[:, :], op0=ALU.mult, op1=ALU.mult)\
                    .then_inc(mn_ready, 1)

            def moba_max(g):
                for n in range(4):
                    dve.wait_ge(sc_mm, 4 * g + n + 1)
                    for m, (s0, s1, o0) in enumerate(((0, S, 0), (S, 384, P))):
                        k = 2 * n + m
                        ins = nc.vector.tensor_tensor_reduce(
                            out=pp_[:, n, s0:s1], in0=bank[4 + n][:, s0:s1],
                            in1=bias[:, 4 * g + n, o0:S], scale=1.0, scalar=3.0 * MASKED,
                            op0=ALU.add, op1=ALU.max, accum_out=mx[:, k:k + 1])
                link(ins)
                nc.vector.tensor_scalar(nmx, mx, -1.0, None, ALU.mult).then_inc(nm_ready, 1)

            def moba_scale(g):
                dve.wait_ge(p_exp, 8 * (g + 1))
                link(nc.vector.reciprocal(rsm, sm))
                for n in range(4):
                    for m, (s0, s1) in enumerate(((0, S), (S, 384))):
                        ins = nc.vector.tensor_scalar(pp_[:, n, s0:s1], pp_[:, n, s0:s1],
                                                      rsm[:, 2 * n + m:2 * n + m + 1], None, ALU.mult)
                    ins.then_inc(p_ready, 1)

            def moba_out(g):
                dve.wait_ge(mpv_mm, g + 1)
                nc.vector.tensor_copy(ya[:, g, :], bank[4][:, :]).then_inc(mpv_read, 1)

            def decay_start():
                nc.vector.tensor_scalar(lf_b[:, :], whole(fb), -1.0, EXP_CLIP, ALU.mult, ALU.min)\
                    .then_inc(f_in, 1)

            def decay_sum():
                dve.wait_ge(f_ready, 1)
                nc.vector.memset(ones[:, :], 1.0)
                link(nc.vector.scalar_tensor_tensor(out=lf[:, :], in0=whole(fb), scalar=0.0,
                                                    in1=lf[:, :], op0=ALU.min, op1=ALU.subtract))
                link(nc.vector.tensor_tensor(lf[:, :], lf[:, :], lf_b[:, :], ALU.add))
                for n in range(HGRN_HEADS):
                    ins = nc.vector.tensor_tensor_scan(cum[:, n * S:(n + 1) * S], ones[:, :],
                                                       lf[:, n * S:(n + 1) * S], 0.0, ALU.mult, ALU.add)
                link(ins)

            def decay_keys():
                dve.wait_ge(k_sig, 1)
                for n in range(HGRN_HEADS):
                    k = whole(kb)[:, n * S:(n + 1) * S]
                    ins = nc.vector.tensor_scalar(k, k, omlb[:, n:n + 1], None, ALU.mult)
                link(ins)
                nc.vector.memset(whole(score), 0.0).then_inc(lv_ready, 1)
                dve.wait_ge(lv_ready, 1)

            def level_start(j):
                m = LEVELS[j]
                if j >= 3:
                    dve.wait_ge(lv_ready, j - 1)
                e = (e_even, e_odd)[j % 2]
                v = cum[:, :].rearrange("p (b t) -> p b t", t=2 * m)
                mid = v[:, :, m - 1:m].broadcast_to([P, 1024 // (2 * m), 2 * m])
                nc.vector.tensor_tensor(e[:, :].rearrange("p (b t) -> p b t", t=2 * m), v, mid,
                                        ALU.subtract).then_inc(lv_sub, 1)

            def level_factors(j):
                e = (e_even, e_odd)[j % 2]
                dve.wait_ge(lv_exp, j)
                if j >= 2:
                    dve.wait_ge(lv_mm, j)
                if LEVELS[j] == P:
                    def half(x, a):
                        return x.rearrange("p (h a n) -> p h a n", a=2, n=P)[:, :, a, :]
                    pairs = [(half(qe[:, :], 1), half(whole(qb), 1), half(e[:, :], 1)),
                             (half(ke[:, :], 0), half(whole(kb), 0), half(e[:, :], 0))]
                else:
                    pairs = [(qe[:, :], whole(qb), e[:, :]), (ke[:, :], whole(kb), e[:, :])]
                for dst, x, y in pairs:
                    ins = nc.vector.tensor_tensor(dst, x, y, ALU.mult)
                ins.then_inc(lv_ready, 1)

            def level_read(j):
                dve.wait_ge(lv_mm, j + 1)
                pair0 = 4 + 2 * (j % 2)
                if LEVELS[j] == P:
                    nc.vector.tensor_copy(whole(cross), bank[pair0][:, :]).then_inc(lv_read, 1)
                    return
                mask = cst("levels", 1024)[:, j * P:(j + 1) * P].bitcast(U32)\
                    .rearrange("p (o n) -> p o n", o=1).broadcast_to([P, 4, P])
                if j:
                    dve.wait_ge(lv_read, j)
                for n in range(2):
                    ins = nc.vector.copy_predicated(score[:, 4 * n:4 * n + 4, :], mask,
                                                    bank[pair0 + n][:, :].rearrange("p (u n) -> p u n", n=P))
                ins.then_inc(lv_read, 1)

            for c in range(24):
                ahead(c0 + c)
                b = b0 + c
                if c == 2:
                    token_factors(1)
                if c == 4:
                    head_norm(0)
                if c == 6:
                    head_norm(1)
                if c == 7:
                    moba_max(0)
                if c == 8:
                    read(b0 + 7)
                    decay_start()
                    moba_scale(0)
                if c == 10:
                    moba_out(0)
                    decay_sum()
                if c == 11:
                    moba_max(1)
                    silu(8, qb, 0, 1)
                    silu(9, qb, 1, 2)
                if c == 12:
                    moba_scale(1)
                    decay_keys()
                if c == 14:
                    moba_out(1)
                j = c - 14
                if j >= 1:
                    level_read(j - 1)
                    if j + 2 < len(LEVELS):
                        level_start(j + 2)
                    if j + 1 < len(LEVELS):
                        level_factors(j + 1)
                if c < 2:
                    evacuate(None, c0 + c, b, pair(mq, c))
                elif c < 4:
                    evacuate(None, c0 + c, b, pair(mk, c - 2))
                elif c < 6:
                    token_values(c, mv, (c - 4) * S)
                elif c < 8:
                    evacuate(None, c0 + c, b, fb[:, c - 6, :])
                elif c < 10:
                    evacuate(None, c0 + c, b, qb[:, c - 8, :])
                elif c < 12:
                    token_values(c, vb, (c - 10) * S)
                elif c < 14:
                    evacuate(None, c0 + c, b, ag[:, c - 12, :])
                elif c < 16:
                    evacuate(None, c0 + c, b, bg[:, c - 14, :])
                elif c < 20:
                    evacuate(None, c0 + c, b, ga[:, c - 16, :])
                else:
                    evacuate(None, c0 + c, b, gb[:, c - 20, :])
                if c == 14:
                    level_start(1)
                    level_start(2)
                    silu(12, ag, 0, 3)
                    silu(13, ag, 1, 4)
                    dve.wait_ge(mpv_read, 2)
                    for n in range(2):
                        ins = nc.vector.tensor_tensor(ya[:, n, :], ya[:, n, :], ag[:, n, :], ALU.mult)
                        ins.then_inc(ya_ready, 1)
                    for n in range(2):
                        dve.wait_ge(ya_ready, n + 1)
                        dve.wait_ge(ya_hi, n + 1)
                        nc.vector.tensor_tensor(pair(yalo, n), ya[:, n, :], pair(yahi, n).bitcast(F32),
                                                ALU.subtract).then_inc(ya_lo, 1)
                    level_factors(1)
                if c == 23:
                    silu(14, bg, 0, 5)
                    silu(15, bg, 1, 6)

            ahead(STAGES["up_a"][0])
            dve.wait_ge(yo_sd, 1)
            for n in range(HGRN_HEADS):
                cols = slice(n * S, (n + 1) * S)
                ins = nc.vector.scalar_tensor_tensor(
                    out=ke[:, cols], in0=bank[4 + n // 2][:, n % 2 * S:(n % 2 + 1) * S],
                    scalar=col("hgrn_gain", n), in1=qe[:, cols], op0=ALU.mult, op1=ALU.mult)
            ins.then_inc(yo_read, 1)
            dve.wait_ge(yo_read, 1)
            for n in range(2):
                cols = slice(n * PAIR, (n + 1) * PAIR)
                nc.vector.tensor_tensor(ke[:, cols], ke[:, cols], bg[:, n, :], ALU.mult).then_inc(yb_ready, 1)
            for n in range(2):
                cols = slice(n * PAIR, (n + 1) * PAIR)
                dve.wait_ge(yb_ready, n + 1)
                dve.wait_ge(yb_hi, n + 1)
                nc.vector.tensor_tensor(pair(yblo, n), ke[:, cols], pair(ybhi, n).bitcast(F32),
                                        ALU.subtract).then_inc(yb_lo, 1)
            c0, _, b0 = STAGES["up_a"]
            for c in range(2):
                if c:
                    ahead(c0 + c)
                dve.wait_ge(chunk_done, c0 + c + 5)
                for n in (2 * c, 2 * c + 1):
                    dve.wait_ge(gate_sig, 6 + n + 1)
                    nc.vector.tensor_tensor(ga[:, n, :], bank[(b0 + n) % 4][:, :], ga[:, n, :], ALU.mult)\
                        .then_inc(banks_read, 1)
            c0, _, b0 = STAGES["up_b"]
            for c in range(2):
                ahead(c0 + c)
                dve.wait_ge(chunk_done, c0 + c + 5)
                for n in (2 * c, 2 * c + 1):
                    dve.wait_ge(gate_sig, 10 + n + 1)
                    nc.vector.tensor_tensor(gb[:, n, :], bank[(b0 + n) % 4][:, :], gb[:, n, :], ALU.mult)\
                        .then_inc(banks_read, 1)
                    read(b0 + n)
                    nc.vector.tensor_tensor(ga[:, n, :], ga[:, n, :], gb[:, n, :], ALU.add)\
                        .then_inc(m_ready, 1)
                for n in (2 * c, 2 * c + 1):
                    dve.wait_ge(m_ready, n + 1)
                    dve.wait_ge(m_hi, n + 1)
                    nc.vector.tensor_tensor(pair(mlo, n), ga[:, n, :], pair(mhi, n).bitcast(F32),
                                            ALU.subtract).then_inc(m_lo, 1)
            c0, _, b0 = STAGES["out2"]
            for c in range(4):
                ahead(c0 + c)
                dve.wait_ge(chunk_done, c0 + c + 5)
                nc.vector.tensor_tensor(h[:, c, :], bank[(b0 + c) % 4][:, :], h[:, c, :], ALU.add)\
                    .then_inc(banks_read, 1)
                read(b0 + c)
                dve.sem_inc(xg_ready, 1)
                dve.wait_ge(x_hi, 20 + c + 1)
                nc.vector.tensor_tensor(pair(xlo, c), h[:, c, :], pair(xhi, c).bitcast(F32),
                                        ALU.subtract).then_inc(x_lo, 1)
            c0, _, b0 = STAGES["ple"]
            ahead(c0)
            dve.wait_ge(chunk_done, c0 + 5)
            for n in range(4):
                nc.vector.tensor_copy(ple[:, n, :], bank[(b0 + n) % 4][:, :]).then_inc(banks_read, 1)
            read(b0 + 3)
            c0, _, b0 = STAGES["ple_gate"]
            for c in range(4):
                ahead(c0 + c)
                dve.wait_ge(chunk_done, c0 + c + 5)
                if c >= 2:
                    dve.wait_ge(fin_ready, c - 1)
                nc.vector.tensor_copy(xg[:, c % 2, :], bank[(b0 + c) % 4][:, :]).then_inc(banks_read, 1)
                read(b0 + c)
                dve.sem_inc(ple_in, 1)
                dve.wait_ge(ple_sig, c + 1)
                link(nc.vector.tensor_tensor(xg[:, c % 2, :], xg[:, c % 2, :], ple[:, c, :], ALU.mult))
                nc.vector.tensor_tensor(h[:, c, :], h[:, c, :], xg[:, c % 2, :], ALU.add)\
                    .then_inc(fin_ready, 1)


def constants():
    import numpy as np

    c = np.zeros((P, N_CONST), np.float32)

    def put(name, value, off=0):
        value = np.asarray(value, np.float32)
        c[:value.shape[0], CONST[name] + off:CONST[name] + off + value.shape[1]] = value

    k, q = np.arange(P)[:, None], np.arange(P)[None, :]
    put("ident", k == q)
    put("anti", k + q == P - 1)
    put("suffix", -1.0 * (k >= q))
    put("neg", -np.ones((P, P)))
    put("mean_d", np.full((P, P), 1.0 / D))
    put("mean_head", (k // 64 == q // 64) / 64.0)
    put("mean_v", np.full((P, P), 1.0 / P))
    for off in (0, S):
        put("causal", np.where(k < q, 0.0, MASKED), off)
    put("levels", k == q)
    for n, m in enumerate(LEVELS[1:-1]):
        put("levels", (k // (2 * m) == q // (2 * m)) & (k // m % 2 == 0) & (q // m % 2 == 1), (n + 1) * P)
    dist = 255 - np.arange(384)
    far = 16 + (np.log(np.maximum(dist, 16) / 16.0) / np.log(2048 / 16.0) * 16).astype(np.int64)
    bucket = np.where(dist < 0, 32, np.where(dist < 16, dist, np.minimum(far, 31)))
    put("bucket", np.arange(33)[:, None] == bucket[None, :])
    return c


_INS = ["x", "mix_norm", "ffn_norm", "final_norm", "lru_w_in", "lru_b_in", "lru_conv_w", "lru_conv_b",
        "lru_gate_w", "lru_gate_b", "lru_lambda", "lru_w_out", "lru_b_out", "attn_w_qkv", "attn_w_o",
        "ffn_w_in", "ffn_w_out", "p_2", "norm_gain_2", "w_in_2", "q_norm_gain_2", "k_norm_gain_2",
        "rel_bias_2", "hgrn_lb_logits_2", "hgrn_out_gain_2", "w_up_a_2", "w_up_b_2", "w_out_2",
        "w_ple_2", "w_ple_gate_2"]


def kernel(**inputs):
    import numpy as _np
    import concourse.bacc as _bacc
    from concourse import mybir as _mybir
    from concourse.bass_utils import run_bass_kernel_spmd as _run

    nc = _bacc.Bacc("TRN2", target_bir_lowering=False, num_devices=1)
    arrays, aps = {}, {}
    given = {name: _np.ascontiguousarray(inputs[name]) for name in _INS}
    given["consts"] = constants()
    for name, a in given.items():
        arrays[f"in_{name}"] = a
        aps[name] = nc.dram_tensor(f"in_{name}", a.shape, _mybir.dt.from_np(a.dtype),
                                   kind="ExternalInput").ap()
    out = nc.dram_tensor("out_0", (1, S, D), _mybir.dt.float32, kind="ExternalOutput").ap()
    build(nc, aps, out)
    r = _run(nc, [arrays], core_ids=[0])
    return r.results[0]["out_0"]
```

```python
from contextlib import ExitStack

import concourse.bass as bass
from concourse import mybir

F32 = mybir.dt.float32
F32R = mybir.dt.float32r
U32 = mybir.dt.uint32
ALU = mybir.AluOpType
ACT = mybir.ActivationFunctionType

P = 128
S = 256
D = 1024
DT = D // P
FF = 2816
PAIR = 2 * S
CHUNK = 2048
HALF = CHUNK // 2
RAWS = 2
RING = 4
AHEAD = 3
EPS = 1e-6
MASKED = -1e30
LRU_C = 8.0
GELU_IN, GELU_CUBE = 0.7978845608028654, 0.044715
EXP_CLIP = 30.0
FFN_PAIRS = FF // S
GROUPS = 4
HGRN_HEADS = 4
HEAD_ORDER = (1, 2, 3, 0)
LEVELS = (0, 64, 32, 16, 8, 4, 2, 1, 128)

STAGES = {}
_c = _b = 0
for _name, _n, _banks in (
    ("rec_a", 3, 1), ("gates_a", 1, 4), ("rec_b", 1, 1), ("branch_a", 1, 1), ("gates_b", 1, 4),
    ("branch_b", 3, 1), ("lru_out", 4, 1),
    ("ffn_in0", 22, 1), ("ffn_out0", 11, 0), ("qkv", 12, 1), ("attn_out", 4, 1),
    ("ffn_in1", 22, 1), ("ffn_out1", 11, 0), ("mix_in", 24, 1), ("up_a", 2, 2), ("up_b", 2, 2),
    ("out2", 4, 1), ("ple", 1, 4), ("ple_gate", 4, 1),
):
    STAGES[_name] = (_c, _n, _b)
    _c += _n
    _b += _n * _banks
CHUNKS = _c

ROWS_A = (("mix_norm", 16), ("ffn_norm", 16), ("final_norm", 8), ("b_in", 16), ("conv_w", 32),
          ("conv_b", 8), ("gate_b", 16))
ROWS_B = (("lam", 8), ("b_out", 8), ("norm_gain", 8), ("lb", 4), ("hgrn_gain", 4), ("q_gain", 1),
          ("k_gain", 1))
COL = {}
_r = 0
for _name, _n in ROWS_A + ROWS_B:
    COL[_name] = _r
    _r += _n
N_A = sum(n for _, n in ROWS_A)
N_B = sum(n for _, n in ROWS_B)

CONST = {}
_r = 0
for _name, _n in (("ident", 128), ("mean_d", 128), ("anti", 128), ("suffix", 128), ("neg", 128),
                  ("mean_head", 128), ("mean_v", 128), ("causal", 384), ("levels", 8 * 128),
                  ("bucket", 384)):
    CONST[_name] = _r
    _r += _n
N_CONST = _r

MIX_ORDER = (0, 1, 2, 3, 4, 5, 10, 11, 8, 9, 12, 13, 6, 7, 14, 15, 16, 17, 18, 19, 20, 21, 22, 23)


def at(i, step, base):
    return base if i is None else i * step + base


def build(nc, t, out):
    ctx = ExitStack()
    with ctx:
        def sb(name, shape, dt=F32):
            return ctx.enter_context(nc.sbuf_tensor(name, shape, dt))

        def sem(name):
            return ctx.enter_context(nc.semaphore(name))

        raw = sb("raw", [P, RAWS, CHUNK])
        whi = sb("whi", [P, RING, CHUNK], F32R)
        wlo = sb("wlo", [P, RING, CHUNK], F32R)
        const = sb("const", [P, N_CONST])
        h = sb("h", [P, DT // 2, PAIR])
        xhi = sb("xhi", [P, DT, S], F32R)
        xlo = sb("xlo", [P, DT, S], F32R)
        xg = sb("xg", [P, 2, PAIR])
        ssum = sb("ssum", [P, PAIR])
        sq = sb("sq", [P, 2, PAIR])
        rs = sb("rs", [P, PAIR])
        rs_tok = sb("rs_tok", [P, 2])
        par = sb("par", [P, N_A + N_B])
        small = sb("small", [P, 104])

        base = (nc.sbuf_base + 63) // 64 * 64
        arena = sb("arena", [P, 80 * 256])

        def over(name, kb, shape, dt=F32):
            return nc.alloc_sbuf_tensor_at("a_" + name, shape, dt, offset=base + int(kb * 1024))

        x_tok = over("x_tok", 0, [P, 2, D])
        prow = over("prow", 17, [P, 2, P])
        bucket_bias = over("bucket_bias", 65, [8, 384])
        recp = over("recp", 8, [P, DT, S + 3])
        rc = over("rc", 17, [P, 4, PAIR])
        rchi = over("rchi", 25, [P, DT, S], F32R)
        rclo = over("rclo", 33, [P, DT, S], F32R)
        gel = over("gel", 41, [P, 4, PAIR])
        rg = over("rg", 49, [P, 4, PAIR])
        ig = over("ig", 57, [P, 4, PAIR])
        gsq = over("gsq", 25, [P, 2, PAIR])
        av = over("av_lru", 8, [P, 4, PAIR])
        yhi = over("yhi", 65, [P, DT, S], F32R)
        ylo = over("ylo", 0, [P, DT, S], F32R)
        p_tok = over("p_tok", 74, [P, 2, S])
        phi = over("phi", 76, [P, 2, S], F32R)
        plo = over("plo", 78, [P, 2, S], F32R)
        ghi = over("ghi", 0, [P, FFN_PAIRS, PAIR], F32R)
        glo = over("glo", 22, [P, FFN_PAIRS, PAIR], F32R)
        tg = over("tg", 44, [P, 2, PAIR])
        sg = over("sg", 48, [P, 2, PAIR])
        tu = over("tu", 70, [P, 2, PAIR])
        qa = over("qa", 0, [P, 2, 2, S])
        ka = over("ka", 4, [P, 2, 2, S])
        va = over("va", 8, [P, 2, 2, S])
        zz = over("zz", 12, [P, 4, 384])
        ee = over("ee", 18, [P, 4, 384])
        nlhi = over("nlhi", 24, [P, 4, 384], F32R)
        nllo = over("nllo", 52, [P, 4, 384], F32R)
        suffix_r = over("suffix_r", 58, [P, 2 * P], F32R)
        ww = over("ww", 30, [P, 4, 384])
        ohi = over("ohi", 36, [P, 4, PAIR], F32R)
        olo = over("olo", 44, [P, 4, PAIR], F32R)
        fb = over("fb", 0, [P, 2, PAIR])
        score = over("score", 0, [P, HGRN_HEADS * 2, P])
        qb = over("qb", 4, [P, 2, PAIR])
        kb = over("kb", 8, [P, 2, PAIR])
        cum = over("cum", 12, [P, 1024])
        vb = over("vb", 16, [P, 2, 512])
        cross = over("cross", 20, [P, HGRN_HEADS, P])
        mq = over("mq", 22, [P, 4, S])
        mk = over("mk", 26, [P, 4, S])
        mv = over("mv", 30, [P, 2, 512])
        e_odd = over("e_odd", 30, [P, 1024])
        e_even = over("e_even", 34, [P, 1024])
        qe = over("qe", 38, [P, 1024])
        ke = over("ke", 42, [P, 1024])
        pp_ = over("probs", 34, [P, 4, 384])
        pt = over("probs_t", 40, [P, 4, 384])
        ag = over("ag", 46, [P, 2, PAIR])
        lf = over("log_f", 66, [P, 1024])
        lf_b = over("log_f_b", 70, [P, 1024])
        ones = over("ones", 74, [P, S])
        bg = over("bg", 50, [P, 2, PAIR])
        ga = over("ga", 22, [P, 4, PAIR])
        bias = over("bias", 54, [P, 8, S])
        gb = over("gb", 54, [P, 4, PAIR])
        bias_rev = over("bias_rev", 62, [P, 8, S])
        ya = over("ya", 62, [P, 2, PAIR])
        yahi = over("yahi", 66, [P, 4, S], F32R)
        yalo = over("yalo", 70, [P, 4, S], F32R)
        ybhi = over("ybhi", 4, [P, 4, S], F32R)
        yblo = over("yblo", 8, [P, 4, S], F32R)
        mhi = over("mhi", 12, [P, DT, S], F32R)
        mlo = over("mlo", 34, [P, DT, S], F32R)
        ple = over("ple", 42, [P, 4, PAIR])
        y_tok = over("y_tok", 0, [P, 2, D])

        bank = [ctx.enter_context(nc.psum_tensor(f"bank{n}", [P, PAIR], F32)) for n in range(8)]
        bias_dram = nc.dram_tensor("bias_scratch", (8, 384), F32, kind="Internal").ap()

        def cst(name, n=128):
            return const[:, CONST[name]:CONST[name] + n]

        ident = cst("ident")
        c8, nc8, lbv, omlb = small[:, 0:8], small[:, 8:16], small[:, 16:20], small[:, 20:24]
        sp_a, sp_b = small[:, 24:32], small[:, 32:40]
        lb_a, lb_b = small[:, 40:44], small[:, 44:48]
        eps = small[:, 48:49]
        q_gain = small[:, 49:50]
        relb = small[0:33, 84:92]
        conv_bias = small[:, 92:100]
        two_gains = small[:, 92:100]
        mx, nmx, sm, rsm = (small[:, 52 + 8 * n:60 + 8 * n] for n in range(4))

        s_x = [sem(f"x_in{n}") for n in range(2)]
        s_ident, s_gain, s_par, s_const, s_p, s_relb = map(
            sem, ("ident_in", "gain_in", "par_in", "const_in", "p_in", "relb_in"))
        raw_full = [sem(f"raw_full{n}") for n in range(RAWS)]
        hi_done, lo_dve, lo_pool = map(sem, ("hi_done", "lo_dve", "lo_pool"))
        chunk_done = sem("chunk_done")
        banks_read = sem("banks_read")
        gain_t, gain_done, par_t, par_done, relb_pad, bkt_t, bkt_done, bkt_out, bias_in, p_t, p_hi, p_lo = map(
            sem, ("gain_t", "gain_done", "par_t", "par_done", "relb_pad", "bkt_t", "bkt_done", "bkt_out", "bias_in", "p_t", "p_hi",
                  "p_lo"))
        xg_ready, x_hi, x_lo, sq_ready, ss_acc, ss_done, mean_ready, sd_ready, rs_ready = map(
            sem, ("xg_ready", "x_hi", "x_lo", "sq_ready", "ss_acc", "ss_done", "mean_ready",
                  "sd_ready", "rs_ready"))
        ms_ready = sem("ms_ready")
        rst_ready, rst_read = map(sem, ("rst_ready", "rst_read"))
        sp_abs, tap_ready, rc_ready, rc_hi, rc_lo, br_z, br_sq, br_cube, br_in, br_tanh = map(
            sem, ("sp_abs", "tap_ready", "rc_ready", "rc_hi", "rc_lo", "br_z", "br_sq", "br_cube", "br_in", "br_tanh"))
        lru_const, gate_mm, a_ready, m2_ready, ig_ready, ix_ready, mult_ready, y_ready, y_hi, y_lo = map(
            sem, ("lru_const", "gate_mm", "a_ready", "m2_ready", "ig_ready", "ix_ready", "mult_ready", "y_ready",
                  "y_hi", "y_lo"))
        sig_ready, silu_ready, act_ready, g_hi, g_lo, acc_mm, acc_read = map(
            sem, ("sig_ready", "silu_ready", "act_ready", "g_hi", "g_lo", "acc_mm", "acc_read"))
        z_mm, z_read, l_ready, sp_ready, nl_hi, nl_ready, s_mm, arg_ready, w_ready, pv_mm, o_hi, o_lo = map(
            sem, ("z_mm", "z_read", "l_ready", "sp_ready", "nl_hi", "nl_ready", "s_mm", "arg_ready", "w_ready",
                  "pv_mm", "o_hi", "o_lo"))
        bias_mm, bias_read, msq, mss, msd, mn_ready = map(
            sem, ("bias_mm", "bias_read", "msq", "mss", "msd", "mn_ready"))
        sc_mm, sc_read, nm_ready, p_exp, p_ready, pt_mm, pt_read, mpv_mm, mpv_read = map(
            sem, ("sc_mm", "sc_read", "nm_ready", "p_exp", "p_ready", "pt_mm", "pt_read",
                  "mpv_mm", "mpv_read"))
        gate_sig, ya_ready, ya_hi, ya_lo = map(sem, ("gate_sig", "ya_ready", "ya_hi", "ya_lo"))
        f_in, f_ready, k_sig, lv_sub, lv_exp, lv_ready, lv_mm, lv_read = map(
            sem, ("f_in", "f_ready", "k_sig", "lv_sub", "lv_exp", "lv_ready", "lv_mm", "lv_read"))
        yo_mm, yo_sq, yo_mean, yo_sd, yo_read, yb_ready, yb_hi, yb_lo = map(
            sem, ("yo_mm", "yo_sq", "yo_mean", "yo_sd", "yo_read", "yb_ready", "yb_hi", "yb_lo"))
        m_ready, m_hi, m_lo, fin_ready, y_t, y_read, y_out = map(
            sem, ("m_ready", "m_hi", "m_lo", "fin_ready", "y_t", "y_read",
                  "y_out"))
        dve_own, act_own = sem("dve_own"), sem("act_own")

        w_in = t["lru_w_in"][0].rearrange("(k p) (c n) -> c p k n", p=P, n=S)
        w_gate = [t["lru_gate_w"][0][:, 2 * n:2 * n + 2].rearrange("g n (k p) d -> p g (n k) d", p=P)
                  for n in range(2)]
        w_lru_out = t["lru_w_out"][0].rearrange("(k p) (c n) -> c p k n", p=P, n=S)
        w_ffn_in = t["ffn_w_in"].rearrange("l (k p) (u c n) -> l u c p k n", p=P, u=2, n=S)
        w_ffn_out = t["ffn_w_out"].rearrange("l (c k p) n -> l c p k n", p=P, k=2)
        w_qkv = t["attn_w_qkv"][0].rearrange("(k p) (q c n) -> q c p k n", p=P, q=3, n=S)
        w_o = t["attn_w_o"][0].rearrange("(k p) (c n) -> c p k n", p=P, n=S)
        w_mix = t["w_in_2"][0].rearrange("(k p) (c n) -> c p k n", p=P, n=S)
        w_up = {n: t[n][0].rearrange("(k p) (c n) -> c p k n", p=P, n=512)
                for n in ("w_up_a_2", "w_up_b_2")}
        w_out2 = t["w_out_2"][0].rearrange("(k p) (c n) -> c p k n", p=P, n=S)
        w_ple = t["w_ple_2"][0].rearrange("(k p) n -> p k n", p=P)
        w_pg = t["w_ple_gate_2"][0].rearrange("(k p) (c n) -> c p k n", p=P, n=S)

        block = ctx.enter_context(nc.Block())

        @block.sync
        def _(sp):
            def load(i, c, src):
                slot = c % RAWS
                if i is not None or c >= RAWS:
                    sp.wait_ge(lo_dve, at(i, 4, c - RAWS + 1))
                    sp.wait_ge(lo_pool, at(i, 4, c - RAWS + 1))
                n = src.shape[-1]
                if len(src.shape) == 4:
                    for g in range(2):
                        sp.dma_start(raw[:, slot, g * HALF:(g + 1) * HALF].rearrange("p (k n) -> p k n", n=n),
                                     src[:, g]).then_inc(raw_full[slot], 16)
                    return
                sp.dma_start(raw[:, slot, :].rearrange("p (k n) -> p k n", n=n), src)\
                    .then_inc(raw_full[slot], 16)

            def stage(name, src, first=0, end=None):
                c0, n, _ = STAGES[name]
                for c in range(first, n if end is None else end):
                    load(None, c0 + c, src(c))

            def ffn(layer):
                c0 = STAGES[f"ffn_in{layer}"][0]
                for c in range(2):
                    load(None, c0 + c, w_ffn_in[layer, c % 2, 0])
                with sp.Fori(0, 5) as i:
                    for j in range(4):
                        load(i, c0 + 2 + j, w_ffn_in[layer, j % 2, i * 2 + (1 + j // 2)])
                c0 = STAGES[f"ffn_out{layer}"][0]
                load(None, c0, w_ffn_out[layer, 0])
                with sp.Fori(0, 2) as i:
                    for j in range(4):
                        load(i, c0 + 1 + j, w_ffn_out[layer, i * 4 + (1 + j)])
                for c in (9, 10):
                    load(None, c0 + c, w_ffn_out[layer, c])

            x_in = t["x"][0].rearrange("(a p) d -> p a d", p=P)
            sp.dma_start(const[:, 0:256], t["consts"][:, 0:256]).then_inc(s_ident, 16)
            sp.dma_start(prow[0:16, 0, :], t["mix_norm"].rearrange("l (t p) -> (l t) p", p=P))\
                .then_inc(s_gain, 16)
            for half in range(2):
                cols = slice(half * D // 2, (half + 1) * D // 2)
                sp.dma_start(x_tok[:, :, cols], x_in[:, :, cols]).then_inc(s_x[half], 16)
            rows = (
                (0, "ffn_norm", t["ffn_norm"].rearrange("l (t p) -> (l t) p", p=P)),
                (0, "final_norm", t["final_norm"].rearrange("(t p) -> t p", p=P)),
                (0, "b_in", t["lru_b_in"][0].rearrange("(t p) -> t p", p=P)),
                (0, "conv_w", t["lru_conv_w"][0].rearrange("j (t p) -> (j t) p", p=P)),
                (0, "conv_b", t["lru_conv_b"][0].rearrange("(t p) -> t p", p=P)),
                (0, "gate_b", t["lru_gate_b"][0].rearrange("g (t p) -> (g t) p", p=P)),
                (1, "lam", t["lru_lambda"][0].rearrange("(t p) -> t p", p=P)),
                (1, "b_out", t["lru_b_out"][0].rearrange("(t p) -> t p", p=P)),
                (1, "norm_gain", t["norm_gain_2"][0].rearrange("(t p) -> t p", p=P)),
                (1, "lb", t["hgrn_lb_logits_2"][0].rearrange("(t p) -> t p", p=P)),
                (1, "hgrn_gain", t["hgrn_out_gain_2"][0].rearrange("(t p) -> t p", p=P)),
            )
            stage("rec_a", lambda c: w_in[4 + c], 0, 2)
            for tile, name, src in rows:
                r0 = COL[name] - tile * N_A
                sp.dma_start(prow[r0:r0 + src.shape[0], tile, :], src).then_inc(s_par, 16)
            for name in ("q_gain", "k_gain"):
                r0 = COL[name] - N_A
                for half in range(2):
                    sp.dma_start(prow[r0:r0 + 1, 1, 64 * half:64 * half + 64],
                                 t[name[0] + "_norm_gain_2"]).then_inc(s_par, 16)
            sp.dma_start(const[:, 256:], t["consts"][:, 256:]).then_inc(s_const, 16)
            sp.dma_start(small[0:32, 84:92], t["rel_bias_2"]).then_inc(s_relb, 16)
            sp.dma_start(p_tok[:, :, :], t["p_2"][0, 0].rearrange("(a p) d -> p a d", p=P))\
                .then_inc(s_p, 16)
            stage("rec_a", lambda c: w_in[4 + c], 2)
            stage("gates_a", lambda c: w_gate[0])
            stage("rec_b", lambda c: w_in[7])
            stage("branch_a", lambda c: w_in[0])
            stage("gates_b", lambda c: w_gate[1])
            stage("branch_b", lambda c: w_in[1 + c])
            stage("lru_out", lambda c: w_lru_out[c])
            ffn(0)
            stage("qkv", lambda c: w_qkv[c % 3, c // 3])
            stage("attn_out", lambda c: w_o[c])
            ffn(1)
            stage("mix_in", lambda c: w_mix[MIX_ORDER[c]])
            stage("up_a", lambda c: w_up["w_up_a_2"][c])
            stage("up_b", lambda c: w_up["w_up_b_2"][c])
            stage("out2", lambda c: w_out2[c])
            stage("ple", lambda c: w_ple)
            stage("ple_gate", lambda c: w_pg[c])
            out_v = out[0].rearrange("(a p) d -> p a d", p=P)
            for j in range(4):
                sp.wait_ge(y_read, j + 1)
                sp.dma_start(out_v[:, :, j * S:(j + 1) * S], y_tok[:, :, j * S:(j + 1) * S])\
                    .then_inc(y_out, 16)
            sp.wait_ge(y_out, 64)

        @block.gpsimd
        def _(pool):
            def lo(i, c):
                pool.wait_ge(hi_done, at(i, 4, c + 1))
                nc.gpsimd.tensor_tensor(
                    wlo[:, c % RING, HALF:], raw[:, c % RAWS, HALF:],
                    whi[:, c % RING, HALF:].bitcast(F32), ALU.subtract).then_inc(lo_pool, 1)

            def branch_square(c):
                pool.wait_ge(br_z, c + 1)
                nc.gpsimd.tensor_tensor(gsq[:, c % 2, :], gel[:, c, :], gel[:, c, :], ALU.mult)\
                    .then_inc(br_sq, 1)

            def branch_cube(c):
                pool.wait_ge(br_cube, c + 1)
                nc.gpsimd.tensor_tensor(gsq[:, c % 2, :], gsq[:, c % 2, :], gel[:, c, :], ALU.mult)\
                    .then_inc(br_in, 1)

            def gated_input(n):
                pool.wait_ge(ig_ready, n + 1)
                nc.gpsimd.tensor_tensor(ig[:, n, :], ig[:, n, :], rc[:, n, :], ALU.mult)\
                    .then_inc(ix_ready, 1)

            def norm_sums(n, pairs):
                for j in pairs:
                    pool.wait_ge(sq_ready, 4 * n + j + 1)
                    if j > 1:
                        pool.wait_ge(ss_acc, 3 * n + j - 1)
                    nc.gpsimd.tensor_tensor(ssum[:, :], ssum[:, :], sq[:, j % 2, :], ALU.add)\
                        .then_inc(ss_acc, 1)
                    if j == 3:
                        pool.wait_ge(ss_acc, 3 * n + 3)
                        pool.sem_inc(ss_done, 1)

            done = [0]

            def to(end):
                first = (done[0] + 3) // 4
                if end // 4 - first >= 2:
                    for c in range(done[0], 4 * first):
                        lo(None, c)
                    with pool.Fori(first, end // 4) as i:
                        for j in range(4):
                            lo(i, j)
                    done[0] = end // 4 * 4
                for c in range(done[0], end):
                    lo(None, c)
                done[0] = end

            to(1)
            norm_sums(0, (1, 2, 3))
            to(8)
            gated_input(0)
            gated_input(1)
            to(9)
            branch_square(0)
            to(10)
            branch_cube(0)
            to(11)
            gated_input(2)
            gated_input(3)
            branch_square(1)
            to(12)
            branch_cube(1)
            nxt = STAGES["lru_out"][0] + AHEAD
            to(nxt + 2)
            norm_sums(1, (1, 2))
            to(nxt + 3)
            norm_sums(1, (3,))
            to(STAGES["qkv"][0] + AHEAD - 1)
            norm_sums(2, (1, 2, 3))
            nxt = STAGES["attn_out"][0] + AHEAD
            to(nxt + 2)
            norm_sums(3, (1, 2))
            to(nxt + 3)
            norm_sums(3, (3,))
            to(STAGES["mix_in"][0] + AHEAD - 1)
            norm_sums(4, (1, 2, 3))
            to(STAGES["mix_in"][0] + AHEAD + 1)
            norm_sums(5, (1, 2, 3))
            to(CHUNKS)

        @block.tensor
        def _(pe):
            def chunk_ready(i, c):
                pe.wait_ge(hi_done, at(i, 4, c + 1))
                pe.wait_ge(lo_dve, at(i, 4, c + 1))
                pe.wait_ge(lo_pool, at(i, 4, c + 1))

            def product(dst, slot, w0, hi, lo, start, stop, shared=False):
                wh, wl = whi[:, slot, w0:w0 + P], wlo[:, slot, w0:w0 + P]
                nc.tensor.matmul(dst, wh, hi, start=start, stop=False, skip_group_check=shared)
                nc.tensor.matmul(dst, wh, lo, start=False, stop=False, skip_group_check=shared)
                return nc.tensor.matmul(dst, wl, hi, start=False, stop=stop, skip_group_check=shared)

            def product_tok(dst, slot, w0, hi, lo, start, stop):
                wh, wl = whi[:, slot, w0:w0 + S], wlo[:, slot, w0:w0 + S]
                nc.tensor.matmul(dst, hi, wh, start=start, stop=False)
                nc.tensor.matmul(dst, lo, wh, start=False, stop=False)
                return nc.tensor.matmul(dst, hi, wl, start=False, stop=stop)

            def columns_part(c, b, hi, lo, k0, k1, ready, count, k_tiles=DT, cols=S):
                if k0 == 0:
                    chunk_ready(None, c)
                    for q in range(cols // S):
                        pe.wait_ge(banks_read, b + q + 1)
                for k in range(k0, k1):
                    if k % 2 == 0:
                        pe.wait_ge(ready, count + k // 2 + 1)
                    for q in range(cols // S):
                        for m in range(2):
                            last = product(bank[(b + q) % 4][:, m * S:(m + 1) * S], c % RING,
                                           k * cols + q * S + m * P, hi[:, k, :], lo[:, k, :],
                                           k == 0 and m == 0, k == k_tiles - 1, True)
                if k1 == k_tiles:
                    last.then_inc(chunk_done, 1)

            def columns_first(c, b, hi, lo, ready, count, k_tiles=DT, cols=S):
                columns_part(c, b, hi, lo, 0, k_tiles, ready, count, k_tiles, cols)

            def columns(i, c, b, hi, lo, k_tiles=DT, cols=S, tok=False):
                chunk_ready(i, c)
                for q in range(cols // S):
                    pe.wait_ge(banks_read, at(i, 4, b + q + 1))
                    dst = bank[(b + q) % 4]
                    for m in range(2):
                        for k in range(k_tiles):
                            ends = dict(start=k == 0, stop=k == k_tiles - 1)
                            d = dst[:, m * S:(m + 1) * S]
                            if tok:
                                last = product_tok(d, c % RING, k * cols, hi[:, k, m * P:(m + 1) * P],
                                                   lo[:, k, m * P:(m + 1) * P], **ends)
                            else:
                                last = product(d, c % RING, k * cols + q * S + m * P, hi[:, k, :],
                                               lo[:, k, :], **ends)
                last.then_inc(chunk_done, 1)

            def statistics(n):
                pe.wait_ge(ss_done, n + 1)
                nc.tensor.matmul(bank[7][:, 0:S], cst("mean_d"), ssum[:, 0:S], start=True, stop=False)
                nc.tensor.matmul(bank[7][:, 0:S], cst("mean_d"), ssum[:, S:], start=False, stop=True)\
                    .then_inc(mean_ready, 1)

            def token_factors(n, k):
                pe.wait_ge(rs_ready, n + 1)
                for m in range(2):
                    last = nc.tensor.matmul(bank[7][:, m:m + 1], rs[0:1, m * P:(m + 1) * P],
                                            ident[0:1, 0:1], start=True, stop=True)
                last.then_inc(rst_ready, 1)

            pe.wait_ge(s_ident, 16)
            pe.wait_ge(s_gain, 16)
            nc.tensor.transpose(bank[4][:, 0:16], prow[0:16, 0, :], ident[0:16, 0:16]).then_inc(gain_t, 1)
            for j in range(4):
                pe.wait_ge(s_x[j // 2], 16)
                for m in range(2):
                    for a in range(2):
                        f0 = (2 * j + m) * P
                        last = nc.tensor.transpose(bank[j][:, m * S + a * P:m * S + (a + 1) * P],
                                                   x_tok[:, a, f0:f0 + P], ident)
                last.then_inc(chunk_done, 1)

            def parameters():
                pe.wait_ge(s_par, 16 * 15)
                nc.tensor.transpose(bank[6][:, 0:N_A], prow[0:N_A, 0, :], ident[0:N_A, 0:N_A])
                nc.tensor.transpose(bank[6][:, N_A:N_A + N_B], prow[0:N_B, 1, :], ident[0:N_B, 0:N_B])\
                    .then_inc(par_t, 1)

            def table_and_p():
                pe.wait_ge(s_const, 16)
                pe.wait_ge(s_relb, 16)
                pe.wait_ge(relb_pad, 1)
                nc.tensor.matmul(bank[5][0:8, 0:384], relb,
                                 const[0:33, CONST["bucket"]:CONST["bucket"] + 384],
                                 start=True, stop=True).then_inc(bkt_t, 1)
                pe.wait_ge(s_p, 16)
                for m in range(2):
                    for a in range(2):
                        last = nc.tensor.transpose(bank[6][:, m * S + a * P:m * S + (a + 1) * P],
                                                   p_tok[:, a, m * P:(m + 1) * P], ident)
                last.then_inc(p_t, 1)

            def gates(name, n0):
                c, _, b0 = STAGES[name]
                chunk_ready(None, c)
                for q in range(4):
                    n = n0 + q % 2
                    if q < 2:
                        pe.wait_ge(rc_lo, n + 1)
                    pe.wait_ge(banks_read, b0 + q + 1)
                    for m in range(2):
                        for k in range(2):
                            last = product(bank[(b0 + q) % 4][:, m * S:(m + 1) * S], c % RING,
                                           (2 * q + k) * S + m * P, rchi[:, 2 * n + k, :],
                                           rclo[:, 2 * n + k, :], k == 0, k == 1)
                    last.then_inc(gate_mm if q < 3 else chunk_done, 1)

            c0, _, b0 = STAGES["rec_a"]
            columns_first(c0, b0, xhi, xlo, x_lo, 0)
            statistics(0)
            parameters()
            columns(None, c0 + 1, b0 + 1, xhi, xlo)
            table_and_p()
            columns(None, c0 + 2, b0 + 2, xhi, xlo)
            gates("gates_a", 0)
            for name in ("rec_b", "branch_a"):
                columns(None, STAGES[name][0], STAGES[name][2], xhi, xlo)
            gates("gates_b", 2)
            c0, _, b0 = STAGES["branch_b"]
            for c in range(3):
                columns(None, c0 + c, b0 + c, xhi, xlo)
            c0, _, b0 = STAGES["lru_out"]
            for k0 in range(0, DT, 2):
                for c in range(3):
                    columns_part(c0 + c, b0 + c, yhi, ylo, k0, k0 + 2, y_lo, 0)
            columns(None, c0 + 3, b0 + 3, yhi, ylo)

            def relative_bias():
                pe.wait_ge(bias_in, 16)
                for n in range(4):
                    if n == 3:
                        pe.wait_ge(sd_ready, 4)
                    nc.tensor.matmul(bank[4 + n][:, :], cst("anti"),
                                     bias_rev[:, 2 * n:2 * n + 2, :].rearrange("p a n -> p (a n)"),
                                     start=True, stop=True).then_inc(bias_mm, 1)

            def ffn(layer):
                c0, _, b0 = STAGES[f"ffn_in{layer}"]
                n = 1 + 2 * layer
                columns_first(c0, b0, xhi, xlo, x_lo, 4 * n)
                columns(None, c0 + 1, b0 + 1, xhi, xlo)
                statistics(n)
                if layer:
                    relative_bias()
                with pe.Fori(0, 5) as i:
                    for j in range(2, 6):
                        columns(i, c0 + j, b0 + j, xhi, xlo)
                c0 = STAGES[f"ffn_out{layer}"][0]

                def rows(i, c, hi, lo, first, final):
                    chunk_ready(i, c0 + c)
                    for m in range(DT):
                        for k in range(2):
                            last = product(bank[4 + m // 2][:, m % 2 * S:(m % 2 + 1) * S],
                                           (c0 + c) % RING, k * D + m * P, hi(k), lo(k),
                                           first and k == 0 and m % 2 == 0, final and k == 1, True)
                        if final and m in (1, 3, 5):
                            last.then_inc(acc_mm, 1)
                    last.then_inc(chunk_done, 1)

                def rows_at(c):
                    pe.wait_ge(g_lo, FFN_PAIRS * layer + c + 1)
                    rows(None, c, lambda k: ghi[:, c, k * S:(k + 1) * S],
                         lambda k: glo[:, c, k * S:(k + 1) * S], c == 0, c == FFN_PAIRS - 1)

                pe.wait_ge(sd_ready, n + 1)
                if layer:
                    pe.wait_ge(bias_read, 4)
                rows_at(0)
                with pe.Fori(0, 2) as i:
                    for j in range(1, 5):
                        pe.wait_ge(g_lo, at(i, 4, FFN_PAIRS * layer + j + 1))
                        rows(i, j, lambda k: ghi[:, i * 4 + j, k * S:(k + 1) * S],
                             lambda k: glo[:, i * 4 + j, k * S:(k + 1) * S], False, False)
                rows_at(9)
                rows_at(10)

            pe.wait_ge(p_lo, 1)
            pe.wait_ge(bkt_done, 1)
            ffn(0)

            c0, _, b0 = STAGES["qkv"]

            def logits(g):
                pe.wait_ge(banks_read, b0 + 3 * g + 1 + 5)
                for n in HEAD_ORDER:
                    r0, f = 64 * (n % 2), n // 2
                    if g == 0 and n == 3:
                        pe.wait_ge(rst_read, 1)
                    if g and n == 0:
                        pe.wait_ge(o_lo, g)
                    q = qa[r0:r0 + 64, g % 2, f, :]
                    k = ka[r0:r0 + 64, g % 2, f, :]
                    nc.tensor.matmul(bank[4 + n][:, 0:S], k[:, 0:P], q, start=True, stop=True)
                    nc.tensor.matmul(bank[4 + n][:, S:384], k[:, P:S], q[:, P:S], start=True, stop=True)\
                        .then_inc(z_mm, 1)

            def suffixes(g):
                pe.wait_ge(z_read, 4 * g + 4)
                for n in range(4):
                    pe.wait_ge(nl_ready, 4 * g + n + 1)
                    first, last, neg = bank[4 + n][:, 0:S], bank[4 + n][:, S:384], suffix_r[:, P:]
                    tri = suffix_r[:, 0:P]
                    nc.tensor.matmul(first, tri, nlhi[:, n, 0:S], start=True, stop=False)
                    nc.tensor.matmul(first, tri, nllo[:, n, 0:S], start=False, stop=False)
                    nc.tensor.matmul(first[:, P:S], neg, nlhi[:, n, S:384], start=False, stop=False)
                    nc.tensor.matmul(first[:, P:S], neg, nllo[:, n, S:384], start=False, stop=True)
                    nc.tensor.matmul(last, tri, nlhi[:, n, S:384], start=True, stop=False)
                    nc.tensor.matmul(last, tri, nllo[:, n, S:384], start=False, stop=True)\
                        .then_inc(s_mm, 1)

            def weighted_values(g):
                pe.wait_ge(banks_read, b0 + 3 * g + 2 + 5)
                for n in range(4):
                    pe.wait_ge(w_ready, 4 * g + n + 1)
                    r0, f = 64 * (n % 2), n // 2
                    dst = bank[4][r0:r0 + 64, f * S:(f + 1) * S]
                    v = va[:, g % 2, :, 64 * n:64 * n + 64]
                    nc.tensor.matmul(dst, v[:, 0, :], ww[:, n, 0:S], start=True, stop=False)
                    last = nc.tensor.matmul(dst[:, P:S], v[:, 1, :], ww[:, n, S:384],
                                            start=False, stop=True)
                last.then_inc(pv_mm, 1)

            for g in range(GROUPS):
                for q in range(3):
                    if g == q == 0:
                        columns_first(c0, b0, xhi, xlo, x_lo, 8)
                        statistics(2)
                    else:
                        columns(None, c0 + 3 * g + q, b0 + 3 * g + q, xhi, xlo, tok=q == 2)
                    if g == 0 and q == 1:
                        pe.wait_ge(sd_ready, 3)
                        token_factors(2, 0)
                    if g and q == 1:
                        suffixes(g - 1)
                if g:
                    weighted_values(g - 1)
                logits(g)
            c0a, _, b0a = STAGES["attn_out"]
            o_h = ohi[:, :, :].rearrange("p a (b n) -> p (a b) n", n=S)
            o_l = olo[:, :, :].rearrange("p a (b n) -> p (a b) n", n=S)

            def attn_part(c, k0, k1):
                columns_part(c0a + c, b0a + c, o_h, o_l, k0, k1, o_lo, 0)

            for c in range(3):
                attn_part(c, 0, 6)
            suffixes(GROUPS - 1)
            attn_part(3, 0, 4)
            weighted_values(GROUPS - 1)
            attn_part(3, 4, 6)
            for c in range(4):
                attn_part(c, 6, 8)
            ffn(1)

            c0, _, b0 = STAGES["mix_in"]

            def head_squares(kind):
                pe.wait_ge(msq, kind + 1)
                src = (e_even, qe)[kind]
                if kind == 1:
                    pe.wait_ge(rst_read, 2)
                for n in range(2):
                    last = nc.tensor.matmul(bank[4 + 2 * kind + n][:, :], cst("mean_head"),
                                            src[:, n * PAIR:(n + 1) * PAIR], start=True, stop=True)
                last.then_inc(mss, 1)

            def moba_scores(g):
                pe.wait_ge(mn_ready, 2)
                if g:
                    pe.wait_ge(mpv_read, g)
                for n in range(4):
                    r0, f = 64 * (n % 2), 2 * g + n // 2
                    q, k = mq[r0:r0 + 64, f, :], mk[r0:r0 + 64, f, :]
                    nc.tensor.matmul(bank[4 + n][:, 0:S], q[:, P:S], k, start=True, stop=True)
                    nc.tensor.matmul(bank[4 + n][:, S:384], q[:, 0:P], k[:, 0:P], start=True, stop=True)\
                        .then_inc(sc_mm, 1)

            def moba_transposes(g):
                for n in range(4):
                    pe.wait_ge(p_ready, 4 * g + n + 1)
                    for d0, s0 in ((0, S), (P, 0), (S, P)):
                        last = nc.tensor.transpose(bank[4 + n][:, d0:d0 + P], pp_[:, n, s0:s0 + P], ident)
                    last.then_inc(pt_mm, 1)

            def moba_values(g):
                for n in range(4):
                    pe.wait_ge(pt_read, 4 * g + n + 1)
                pe.wait_ge(banks_read, b0 + 6 + 4)
                for n in range(4):
                    r0, f = 64 * (n % 2), n // 2
                    hd = 4 * g + n
                    dst = bank[4][r0:r0 + 64, f * S:(f + 1) * S]
                    nc.tensor.matmul(dst, mv[:, 0, 64 * hd:64 * hd + 64], pt[:, n, 0:S],
                                     start=True, stop=False)
                    last = nc.tensor.matmul(dst[:, P:S], mv[:, 1, 64 * hd:64 * hd + 64],
                                            pt[:, n, S:384], start=False, stop=True)
                last.then_inc(mpv_mm, 1)

            def level(j):
                pe.wait_ge(lv_ready, j + 1)
                pair = 4 + 2 * (j % 2)
                if j >= 2:
                    pe.wait_ge(lv_read, j - 1)
                else:
                    pe.wait_ge(mpv_read, 2)
                q, k = (qb[:, :, :].rearrange("p a n -> p (a n)"),
                        kb[:, :, :].rearrange("p a n -> p (a n)")) if j == 0 else (qe, ke)
                m = LEVELS[j]
                for n in range(HGRN_HEADS):
                    if m == P:
                        last = nc.tensor.matmul(bank[pair][:, n * P:(n + 1) * P],
                                                k[:, n * S:n * S + P], q[:, n * S + P:(n + 1) * S],
                                                start=True, stop=True)
                        continue
                    for a in range(2):
                        u = 2 * n + a
                        dst = bank[pair + u // 4][:, u % 4 * P:(u % 4 + 1) * P]
                        queries = q[:, u * P:(u + 1) * P]
                        if j:
                            dst = dst[:, 0:P // 2]
                            queries = queries.rearrange("p (b t) -> p b t", t=2 * m)[:, :, m:]
                        last = nc.tensor.matmul(dst, k[:, u * P:(u + 1) * P], queries,
                                                start=True, stop=True)
                last.then_inc(lv_mm, 1)

            plan = {
                0: [lambda: statistics(4)],
                1: [lambda: (pe.wait_ge(sd_ready, 5), statistics(5))],
                3: [lambda: (pe.wait_ge(sd_ready, 6), token_factors(5, 1)), lambda: head_squares(0)],
                4: [lambda: head_squares(1)],
                6: [lambda: moba_scores(0)],
                8: [lambda: moba_transposes(0)],
                9: [lambda: moba_values(0)],
                10: [lambda: moba_scores(1)],
                12: [lambda: moba_transposes(1)],
                13: [lambda: moba_values(1)],
            }
            for j in range(len(LEVELS)):
                plan[14 + j] = [lambda j=j: level(j)]
            for c in range(24):
                if c == 0:
                    columns_first(c0, b0, xhi, xlo, x_lo, 16)
                else:
                    columns(None, c0 + c, b0 + c, xhi, xlo, tok=c in (4, 5, 10, 11))
                for todo in plan.get(c, ()):
                    todo()

            def hgrn_outputs():
                pe.wait_ge(lv_read, len(LEVELS))
                for n in range(HGRN_HEADS):
                    dst = bank[4 + n // 2][:, n % 2 * S:(n % 2 + 1) * S]
                    v0, v1 = vb[:, 0, n * P:(n + 1) * P], vb[:, 1, n * P:(n + 1) * P]
                    nc.tensor.matmul(dst[:, 0:P], v0, score[:, 2 * n, :], start=True, stop=True)
                    nc.tensor.matmul(dst[:, P:S], v0, cross[:, n, :], start=True, stop=False)
                    last = nc.tensor.matmul(dst[:, P:S], v1, score[:, 2 * n + 1, :],
                                            start=False, stop=True)
                last.then_inc(yo_mm, 1)

            def hgrn_squares():
                pe.wait_ge(yo_sq, 1)
                for n in range(2):
                    last = nc.tensor.matmul(bank[6 + n][:, :], cst("mean_v"),
                                            e_even[:, n * PAIR:(n + 1) * PAIR], start=True, stop=True)
                last.then_inc(yo_mean, 1)

            hgrn_outputs()
            pe.wait_ge(ya_lo, 2)
            c0, _, b0 = STAGES["up_a"]
            chunk_ready(None, c0)
            for q in range(2):
                pe.wait_ge(banks_read, b0 + q + 1)
                for m in range(2):
                    for k in range(4):
                        last = product(bank[(b0 + q) % 4][:, m * S:(m + 1) * S], c0 % RING,
                                       k * 512 + q * S + m * P, yahi[:, k, :], yalo[:, k, :],
                                       k == 0, k == 3)
                if q == 0:
                    hgrn_squares()
            last.then_inc(chunk_done, 1)
            columns(None, c0 + 1, b0 + 2, yahi, yalo, k_tiles=4, cols=512)
            c0, _, b0 = STAGES["up_b"]
            columns_first(c0, b0, ybhi, yblo, yb_lo, 0, k_tiles=4, cols=512)
            columns(None, c0 + 1, b0 + 2, ybhi, yblo, k_tiles=4, cols=512)
            c0, _, b0 = STAGES["out2"]
            for k0 in (0, 4):
                for c in range(3):
                    columns_part(c0 + c, b0 + c, mhi, mlo, k0, k0 + 4, m_lo, 0)
            columns(None, c0 + 3, b0 + 3, mhi, mlo)
            c0, _, b0 = STAGES["ple"]
            columns(None, c0, b0, phi, plo, k_tiles=2, cols=D)
            c0, _, b0 = STAGES["ple_gate"]

            def to_tokens(j):
                pe.wait_ge(fin_ready, j + 1)
                if j == 0:
                    pe.wait_ge(yo_read, 1)
                for a in range(2):
                    for m in range(2):
                        last = nc.tensor.transpose(
                            bank[4 + j][:, a * S + m * P:a * S + (m + 1) * P],
                            h[:, j, m * S + a * P:m * S + (a + 1) * P], ident)
                last.then_inc(y_t, 1)

            columns_first(c0, b0, xhi, xlo, x_lo, 20)
            for c in range(1, 4):
                columns(None, c0 + c, b0 + c, xhi, xlo)
                to_tokens(c - 1)
            to_tokens(3)

        @block.scalar
        def _(act):
            own = [0]

            def link(ins):
                own[0] += 1
                ins.then_inc(act_own, 1)
                act.wait_ge(act_own, own[0])

            def split(i, c):
                gate_chunks = sum(g <= c and g % RAWS == c % RAWS for g in
                                  (STAGES["gates_a"][0], STAGES["gates_b"][0]))
                act.wait_ge(raw_full[c % RAWS], at(i, 32, 16 * (c // RAWS + 1 + gate_chunks)))
                act.wait_ge(chunk_done, at(i, 4, c + 1))
                nc.scalar.activation(whi[:, c % RING, :], raw[:, c % RAWS, :], ACT.Copy)\
                    .then_inc(hi_done, 1)

            def ahead(c):
                if c + AHEAD < CHUNKS:
                    split(None, c + AHEAD)

            def pair(tensor, j):
                return tensor[:, 2 * j:2 * j + 2, :].rearrange("p a n -> p (a n)")

            def norm_square(n, j):
                if j == 0:
                    if n:
                        act.wait_ge(mean_ready, n)
                    dst = ssum[:, :]
                else:
                    if 3 * n + (j == 3):
                        act.wait_ge(ss_acc, 3 * n + (j == 3))
                    if n and j == 2:
                        act.wait_ge(rs_ready, n)
                    dst = sq[:, j % 2, :]
                if n < 5:
                    nc.scalar.activation(dst, h[:, j, :], ACT.Square).then_inc(sq_ready, 1)
                    return
                for m in range(2):
                    cols = slice(m * S, (m + 1) * S)
                    gain = COL["final_norm"] + 2 * j + m
                    ins = nc.scalar.activation(dst[:, cols], h[:, j, cols], ACT.Square,
                                               scale=par[:, gain:gain + 1])
                ins.then_inc(sq_ready, 1)

            def norm_hi(xn, j):
                act.wait_ge(xg_ready, 4 * xn + j + 1)
                nc.scalar.activation(pair(xhi, j), xg[:, j % 2, :], ACT.Copy).then_inc(x_hi, 1)

            def norm_pair(n, xn, j):
                norm_hi(xn, j)
                norm_square(n, j)

            def norm_root(n):
                act.wait_ge(mean_ready, n + 1)
                nc.scalar.activation(sq[:, 0, 0:S], bank[7][:, 0:S], ACT.Sqrt, bias=eps)\
                    .then_inc(sd_ready, 1)

            def take_x(j):
                act.wait_ge(chunk_done, j + 1)
                nc.scalar.activation(h[:, j, :], bank[j][:, :], ACT.Copy).then_inc(banks_read, 1)

            take_x(0)
            take_x(1)
            norm_hi(0, 0)
            take_x(2)
            norm_hi(0, 1)
            take_x(3)
            split(None, 0)
            norm_hi(0, 2)
            norm_hi(0, 3)
            for j in range(4):
                act.wait_ge(banks_read, j + 1)
                norm_square(0, j)
            for c in range(1, AHEAD):
                split(None, c)
            norm_root(0)

            def rec_hi(j):
                act.wait_ge(rc_ready, j + 1)
                nc.scalar.activation(pair(rchi, j), rc[:, j, :], ACT.Copy).then_inc(rc_hi, 1)

            def gate_sigmoids(name, n0):
                c, _, b0 = STAGES[name]
                act.wait_ge(banks_read, b0 - 1 + 5)
                for q in range(4):
                    if q < 3:
                        act.wait_ge(gate_mm, 3 * (n0 // 2) + q + 1)
                    else:
                        act.wait_ge(chunk_done, c + 5)
                    n = n0 + q % 2
                    for m in range(2):
                        cols = slice(m * S, (m + 1) * S)
                        f = COL["gate_b"] + DT * (q // 2) + 2 * n + m
                        ins = nc.scalar.activation((rg, ig)[q // 2][:, n, cols],
                                                   bank[(b0 + q) % 4][:, cols], ACT.Sigmoid,
                                                   bias=par[:, f:f + 1])
                    ins.then_inc(banks_read, 1)
                act.wait_ge(banks_read, b0 + 3 + 5)
                act.sem_inc(ig_ready, 2)

            def gate_decay(n0):
                act.wait_ge(lru_const, 1)
                for f in range(2 * n0, 2 * n0 + 4):
                    cols = slice(f % 2 * S, (f % 2 + 1) * S)
                    nc.scalar.activation(av[:, f // 2, cols], rg[:, f // 2, cols], ACT.Exp,
                                         scale=nc8[:, f:f + 1]).then_inc(a_ready, 1)
                for f in range(2 * n0, 2 * n0 + 4):
                    cols = slice(f % 2 * S, (f % 2 + 1) * S)
                    if f == 2 * n0:
                        act.wait_ge(a_ready, 4 * n0 + 4)
                    nc.scalar.activation(rg[:, f // 2, cols], rg[:, f // 2, cols], ACT.Tanh,
                                         scale=c8[:, f:f + 1]).then_inc(a_ready, 1)

            def gate_root(n0):
                for n in (n0, n0 + 1):
                    act.wait_ge(m2_ready, n + 1)
                    nc.scalar.activation(rg[:, n, :], rg[:, n, :], ACT.Sqrt).then_inc(mult_ready, 1)

            def branch_square(c):
                act.wait_ge(br_z, c + 1)
                nc.scalar.activation(gsq[:, c % 2, :], gel[:, c, :], ACT.Square).then_inc(br_sq, 1)

            def branch_tanh(c):
                act.wait_ge(br_in, c + 1)
                nc.scalar.activation(gsq[:, c % 2, :], gsq[:, c % 2, :], ACT.Tanh, scale=GELU_IN)\
                    .then_inc(br_tanh, 1)

            def y_hi_of(n):
                act.wait_ge(y_ready, n + 1)
                nc.scalar.activation(pair(yhi, n), rc[:, n, :], ACT.Copy).then_inc(y_hi, 1)

            def last_tap(name, c, j):
                act.wait_ge(banks_read, STAGES[name][2] + c + 5)
                for m in range(2):
                    f = 2 * j + m
                    tap = COL["conv_w"] + 3 * DT + f
                    ins = nc.scalar.activation(rc[:, j, m * S:(m + 1) * S], recp[:, f, 3:3 + S],
                                               ACT.Identity, bias=conv_bias[:, f:f + 1],
                                               scale=par[:, tap:tap + 1])
                ins.then_inc(tap_ready, 1)

            c0 = STAGES["rec_a"][0]
            lam = par[:, COL["lam"]:COL["lam"] + 8]
            act.wait_ge(par_done, 1)
            link(nc.scalar.activation(sp_a, lam, ACT.Abs))
            link(nc.scalar.activation(sp_a, sp_a, ACT.Exp, scale=-1.0))
            nc.scalar.activation(lb_b, lb_a, ACT.Exp)
            nc.scalar.activation(sp_a, sp_a, ACT.Ln, bias=1.0).then_inc(sp_abs, 1)
            ahead(c0)
            last_tap("rec_a", 0, 0)
            last_tap("rec_a", 1, 1)
            rec_hi(0)
            ahead(c0 + 1)
            rec_hi(1)
            ahead(c0 + 2)
            last_tap("rec_a", 2, 2)
            gate_sigmoids("gates_a", 0)
            rec_hi(2)
            ahead(STAGES["gates_a"][0])
            act.wait_ge(bkt_done, 1)
            act.dma_start(bias_dram, bucket_bias[:, :]).then_inc(bkt_out, 16)
            last_tap("rec_b", 0, 3)
            ahead(STAGES["rec_b"][0])
            rec_hi(3)
            gate_decay(0)
            gate_sigmoids("gates_b", 2)
            ahead(STAGES["branch_a"][0])
            ahead(STAGES["gates_b"][0])
            act.wait_ge(p_t, 1)
            nc.scalar.activation(phi[:, :, :].rearrange("p a n -> p (a n)"), bank[6][:, :],
                                 ACT.Copy).then_inc(p_hi, 1)
            gate_root(0)
            c0 = STAGES["branch_b"][0]
            ahead(c0)
            branch_tanh(0)
            gate_decay(2)
            act.wait_ge(bkt_out, 16)
            y_hi_of(0)
            ahead(c0 + 1)
            gate_root(2)
            ahead(c0 + 2)
            branch_square(2)
            branch_tanh(1)
            y_hi_of(1)
            branch_tanh(2)
            ahead(STAGES["lru_out"][0])
            y_hi_of(2)
            branch_square(3)
            branch_tanh(3)
            y_hi_of(3)
            c0 = STAGES["lru_out"][0]
            ahead(c0 + 1)
            for c in range(4):
                norm_pair(1, 1, c)
                if c >= 2:
                    ahead(c0 + c)

            def ffn(layer):
                n = 1 + 2 * layer
                norm_root(n)
                c0, _, b0 = STAGES[f"ffn_in{layer}"]

                def gated(i, c, q, par_q):
                    split(i, c0 + c + AHEAD)
                    act.wait_ge(banks_read, at(i, 4, b0 + c + 5))
                    nc.scalar.activation(sg[:, par_q, :], tg[:, par_q, :], ACT.Sigmoid)\
                        .then_inc(sig_ready, 1)
                    split(i, c0 + c + 1 + AHEAD)
                    act.wait_ge(act_ready, at(i, 2, FFN_PAIRS * layer + q + 1))
                    dst = ghi[:, q, :] if i is None else ghi[:, i * 2 + q, :]
                    nc.scalar.activation(dst, tu[:, par_q, :], ACT.Copy).then_inc(g_hi, 1)

                gated(None, 0, 0, 0)
                if layer:
                    for q in range(4):
                        act.wait_ge(bias_mm, q + 1)
                        nc.scalar.activation(pair(bias, q), bank[4 + q][:, :], ACT.Copy)\
                            .then_inc(bias_read, 1)
                with act.Fori(0, 5) as i:
                    for j in range(2):
                        gated(i, 2 + 2 * j, 1 + j, (1 + j) % 2)
                c0 = STAGES[f"ffn_out{layer}"][0]
                split(None, c0 + AHEAD)
                with act.Fori(0, 2) as i:
                    for j in range(4):
                        split(i, c0 + 1 + j + AHEAD)
                split(None, c0 + 9 + AHEAD)

            ffn(0)
            for j in range(4):
                norm_pair(2, 2, j)
                if j == 3:
                    split(None, STAGES["qkv"][0] + AHEAD - 1)
            norm_root(2)

            c0, _, b0 = STAGES["qkv"]

            def whole(tensor):
                return tensor[:, :, :].rearrange("p a n -> p (a n)")

            def log_terms(g):
                act.wait_ge(z_read, 4 * g + 4)
                link(nc.scalar.activation(whole(ee), whole(zz), ACT.Abs))
                link(nc.scalar.activation(whole(ee), whole(ee), ACT.Exp, scale=-1.0))
                for n in range(2):
                    part = ee[:, 2 * n:2 * n + 2, :].rearrange("p a n -> p (a n)")
                    nc.scalar.activation(part, part, ACT.Ln, bias=1.0).then_inc(l_ready, 1)

            def fail_hi(g):
                for n in range(4):
                    act.wait_ge(sp_ready, 4 * g + n + 1)
                    nc.scalar.activation(nlhi[:, n, :], ee[:, n, :], ACT.Copy).then_inc(nl_hi, 1)

            def weights(g):
                for n in range(4):
                    act.wait_ge(arg_ready, 4 * g + n + 1)
                    nc.scalar.activation(ww[:, n, :], zz[:, n, :], ACT.Exp).then_inc(w_ready, 1)

            def outputs(g):
                act.wait_ge(pv_mm, g + 1)
                nc.scalar.activation(ohi[:, g, :], bank[4][:, :], ACT.Copy).then_inc(o_hi, 1)

            for g in range(GROUPS):
                for q in range(3):
                    ahead(c0 + 3 * g + q)
                    if q == 0 and g >= 2:
                        outputs(g - 2)
                    if q == 0 and g >= 1:
                        log_terms(g - 1)
                        fail_hi(g - 1)
                    if q == 2 and g >= 1:
                        weights(g - 1)
                    if q == g == 0:
                        nc.scalar.activation(suffix_r[:, :],
                                             const[:, CONST["suffix"]:CONST["suffix"] + 2 * P], ACT.Copy)
            ahead(STAGES["attn_out"][0])
            outputs(GROUPS - 2)
            log_terms(GROUPS - 1)
            fail_hi(GROUPS - 1)
            weights(GROUPS - 1)
            outputs(GROUPS - 1)
            act.wait_ge(bkt_out, 16)
            src = bass.AP(bias_dram.tensor, 0, [[1, P], [384, 8], [1, S]])
            act.dma_start(bias_rev[:, :, :], src).then_inc(bias_in, 16)
            c0 = STAGES["attn_out"][0]
            for c in range(4):
                if c == 0:
                    ahead(c0 + 1)
                norm_pair(3, 3, c)
                if c >= 2:
                    ahead(c0 + c)
            ffn(1)
            for j in range(4):
                norm_pair(4, 4, j)
                if j == 3:
                    split(None, STAGES["mix_in"][0] + AHEAD - 1)

            c0, _, b0 = STAGES["mix_in"]

            def sigmoid_to_tmp(c, src):
                act.wait_ge(banks_read, b0 + c + 5)
                nc.scalar.activation(xg[:, c % 2, :], src, ACT.Sigmoid).then_inc(gate_sig, 1)

            def head_square(kind):
                act.wait_ge(banks_read, b0 + 2 * kind + 2 + 4)
                src, dst = ((mq, e_even), (mk, qe))[kind]
                nc.scalar.activation(dst[:, :], whole(src), ACT.Square).then_inc(msq, 1)

            def head_root(kind):
                act.wait_ge(mss, kind + 1)
                dst = (e_even, qe)[kind]
                for n in range(2):
                    ins = nc.scalar.activation(dst[:, n * PAIR:(n + 1) * PAIR],
                                               bank[4 + 2 * kind + n][:, :], ACT.Ln, bias=eps)
                link(ins)
                nc.scalar.activation(dst[:, :], dst[:, :], ACT.Exp, scale=-0.5).then_inc(msd, 1)

            def moba_exp(g):
                act.wait_ge(nm_ready, g + 1)
                for n in range(4):
                    for m, (s0, s1) in enumerate(((0, S), (S, 384))):
                        col = 2 * n + m
                        ins = nc.scalar.activation(pp_[:, n, s0:s1], pp_[:, n, s0:s1], ACT.Exp,
                                                   bias=nmx[:, col:col + 1],
                                                   accum_out=sm[:, col:col + 1])
                        ins.then_inc(p_exp, 1)

            def moba_copies(g):
                for n in range(4):
                    act.wait_ge(pt_mm, 4 * g + n + 1)
                    nc.scalar.activation(pt[:, n, :], bank[4 + n][:, 0:384], ACT.Copy)\
                        .then_inc(pt_read, 1)

            def decay_exp():
                act.wait_ge(f_in, 1)
                link(nc.scalar.activation(lf[:, :], whole(fb), ACT.Abs))
                nc.scalar.activation(lf[:, :], lf[:, :], ACT.Exp, scale=-1.0)
                link(nc.scalar.activation(lf_b[:, :], lf_b[:, :], ACT.Exp))

            def decay_ln():
                for n in range(HGRN_HEADS):
                    nc.scalar.activation(lf_b[:, n * S:(n + 1) * S], lf_b[:, n * S:(n + 1) * S], ACT.Ln,
                                         scale=lbv[:, n:n + 1], bias=1.0)
                nc.scalar.activation(lf[:, :], lf[:, :], ACT.Ln, bias=1.0).then_inc(f_ready, 1)

            def level(j):
                e = (e_even, e_odd)[j % 2]
                act.wait_ge(lv_sub, j)
                link(nc.scalar.activation(e[:, :], e[:, :], ACT.Abs))
                nc.scalar.activation(e[:, :], e[:, :], ACT.Exp, scale=-1.0).then_inc(lv_exp, 1)

            def split_out(n, ready, src, dst, done):
                act.wait_ge(ready, n + 1)
                nc.scalar.activation(dst, src, ACT.Copy).then_inc(done, 1)

            def gate(tensor, c, j):
                act.wait_ge(banks_read, b0 + c + 5)
                nc.scalar.activation(tensor[:, j, :], tensor[:, j, :], ACT.Sigmoid).then_inc(gate_sig, 1)

            for c in range(24):
                ahead(c0 + c)
                if c == 0:
                    norm_root(4)
                    for j in range(4):
                        norm_square(5, j)
                if c == 1:
                    act.wait_ge(ms_ready, 1)
                    nc.scalar.activation(sq[:, 0, 0:S], xg[:, 0, 0:S], ACT.Sqrt, bias=eps)\
                        .then_inc(sd_ready, 1)
                if c == 2:
                    head_square(0)
                if c == 4:
                    head_square(1)
                    head_root(0)
                if c == 5:
                    head_root(1)
                if c == 7:
                    moba_exp(0)
                if c == 8:
                    decay_exp()
                if c == 9:
                    moba_copies(0)
                    decay_ln()
                if c == 10:
                    nc.scalar.activation(whole(kb), whole(fb), ACT.Sigmoid, scale=-1.0).then_inc(k_sig, 1)
                    sigmoid_to_tmp(8, qb[:, 0, :])
                    sigmoid_to_tmp(9, qb[:, 1, :])
                if c == 11:
                    moba_exp(1)
                if c == 13:
                    moba_copies(1)
                if c >= 14 and c - 13 < len(LEVELS):
                    level(c - 13)
                if c == 22:
                    sigmoid_to_tmp(12, ag[:, 0, :])
                    sigmoid_to_tmp(13, ag[:, 1, :])
                    for n in range(4):
                        gate(ga, 16 + n, n)
                if c == 23:
                    for n in range(2):
                        split_out(n, ya_ready, ya[:, n, :], pair(yahi, n), ya_hi)
                    sigmoid_to_tmp(14, bg[:, 0, :])
                    sigmoid_to_tmp(15, bg[:, 1, :])
                    for n in range(4):
                        gate(gb, 20 + n, n)
            act.wait_ge(yo_mm, 1)
            for n in range(2):
                ins = nc.scalar.activation(e_even[:, n * PAIR:(n + 1) * PAIR], bank[4 + n][:, :], ACT.Square)
            ins.then_inc(yo_sq, 1)
            ahead(STAGES["up_a"][0])
            act.wait_ge(yo_mean, 1)
            for n in range(2):
                ins = nc.scalar.activation(qe[:, n * PAIR:(n + 1) * PAIR], bank[6 + n][:, :],
                                           ACT.Ln, bias=eps)
            link(ins)
            for n in range(2):
                cols = slice(n * PAIR, (n + 1) * PAIR)
                nc.scalar.activation(qe[:, cols], qe[:, cols], ACT.Exp, scale=-0.5).then_inc(yo_sd, 1)
            ahead(STAGES["up_a"][0] + 1)
            for n in range(2):
                split_out(n, yb_ready, ke[:, n * PAIR:(n + 1) * PAIR], pair(ybhi, n), yb_hi)
            for c in range(2):
                ahead(STAGES["up_b"][0] + c)
                for n in (2 * c, 2 * c + 1):
                    split_out(n, m_ready, ga[:, n, :], pair(mhi, n), m_hi)
            for c in range(4):
                ahead(STAGES["out2"][0] + c)
                split_out(20 + c, xg_ready, h[:, c, :], pair(xhi, c), x_hi)
            ahead(STAGES["ple"][0])
            for c in range(4):
                ahead(STAGES["ple_gate"][0] + c)
                _, _, b0 = STAGES["ple_gate"]
                act.wait_ge(banks_read, b0 - 1 + 5)
                act.wait_ge(chunk_done, STAGES["ple_gate"][0] + c + 5)
                if c >= 2:
                    act.wait_ge(fin_ready, c - 1)
                nc.scalar.activation(xg[:, c % 2, :], bank[(b0 + c) % 4][:, :], ACT.Sigmoid)\
                    .then_inc(banks_read, 1)
            for j in range(4):
                act.wait_ge(y_t, j + 1)
                nc.scalar.activation(y_tok[:, :, j * S:(j + 1) * S],
                                     bank[4 + j][:, :].rearrange("p (a n) -> p a n", a=2),
                                     ACT.Copy).then_inc(y_read, 1)

        @block.vector
        def _(dve):
            own = [0]

            def mark(ins):
                own[0] += 1
                ins.then_inc(dve_own, 1)
                return own[0]

            def link(ins):
                dve.wait_ge(dve_own, mark(ins))

            def split(i, c):
                dve.wait_ge(hi_done, at(i, 4, c + 1))
                nc.vector.tensor_tensor(wlo[:, c % RING, :HALF], raw[:, c % RAWS, :HALF],
                                        whi[:, c % RING, :HALF].bitcast(F32), ALU.subtract)\
                    .then_inc(lo_dve, 1)

            def ahead(c):
                if c + AHEAD < CHUNKS:
                    split(None, c + AHEAD)

            def pair(tensor, j):
                return tensor[:, 2 * j:2 * j + 2, :].rearrange("p a n -> p (a n)")

            def whole(tensor):
                return tensor[:, :, :].rearrange("p a n -> p (a n)")

            def col(name, n=0):
                return par[:, COL[name] + n:COL[name] + n + 1]

            def norm_gain(xn, j, gain):
                if 4 * xn + j >= 2:
                    dve.wait_ge(x_lo, 4 * xn + j - 1)
                    dve.wait_ge(x_hi, 4 * xn + j - 1)
                for m in range(2):
                    ins = nc.vector.tensor_scalar(xg[:, j % 2, m * S:(m + 1) * S],
                                                  h[:, j, m * S:(m + 1) * S],
                                                  gain[:, 2 * j + m:2 * j + m + 1], None, ALU.mult)
                ins.then_inc(xg_ready, 1)

            def norm_lo(xn, j):
                dve.wait_ge(x_hi, 4 * xn + j + 1)
                nc.vector.tensor_tensor(pair(xlo, j), xg[:, j % 2, :], pair(xhi, j).bitcast(F32),
                                        ALU.subtract).then_inc(x_lo, 1)

            def norm_factor(n):
                dve.wait_ge(sd_ready, n + 1)
                link(nc.vector.reciprocal(rs[:, 0:S], sq[:, 0, 0:S]))
                nc.vector.tensor_copy(rs[:, S:], rs[:, 0:S]).then_inc(rs_ready, 1)
                dve.wait_ge(rs_ready, n + 1)

            def token_factors(k):
                dve.wait_ge(rst_ready, k + 1)
                nc.vector.tensor_copy(rs_tok[:, :], bank[7][:, 0:2]).then_inc(rst_read, 1)
                dve.wait_ge(rst_read, k + 1)

            def gains(name, layer=0):
                return par[:, COL[name] + layer * DT:COL[name] + (layer + 1) * DT]

            def norm(xn, gain, update, splits, paced=True):
                for j in range(4):
                    update(j)
                    norm_gain(xn, j, gain)
                    if paced:
                        norm_lo(xn, j)
                    elif j:
                        norm_lo(xn, j - 1)
                    for c in splits[j]:
                        split(None, c)
                if not paced:
                    norm_lo(xn, 3)

            def evacuate(i, c, b, dst, op=None):
                dve.wait_ge(chunk_done, at(i, 4, c + 5))
                nc.vector.tensor_tensor(dst, bank[b % 4][:, :], rs[:, :], ALU.mult)\
                    .then_inc(banks_read, 1)

            def read(b):
                dve.wait_ge(banks_read, b + 5)

            nc.vector.memset(eps, EPS)
            dve.wait_ge(gain_t, 1)
            nc.vector.tensor_copy(par[:, 0:16], bank[4][:, 0:16]).then_inc(gain_done, 1)
            dve.wait_ge(gain_done, 1)
            norm(0, gains("mix_norm"), lambda j: dve.wait_ge(banks_read, j + 1),
                 ((), (), (0,), ()), paced=False)
            split(None, 1)
            split(None, 2)
            dve.wait_ge(par_t, 1)
            link(nc.vector.tensor_copy(par[:, 16:], bank[6][:, 16:N_A + N_B]))
            link(nc.vector.tensor_tensor(lb_a, par[:, COL["lb"]:COL["lb"] + 4],
                                         par[:, COL["lb"]:COL["lb"] + 4], ALU.subtract))
            nc.vector.memset(small[32:33, 84:92], MASKED).then_inc(relb_pad, 1)
            nc.vector.tensor_scalar(q_gain, col("q_gain"), 0.125, None, ALU.mult).then_inc(par_done, 1)
            norm_factor(0)

            def lru_constants():
                lam = par[:, COL["lam"]:COL["lam"] + 8]
                dve.wait_ge(sp_abs, 1)
                link(nc.vector.tensor_scalar(sp_b, lam, -1.0, 0.0, ALU.mult, ALU.max))
                link(nc.vector.tensor_tensor(sp_b, sp_b, sp_a, ALU.add))
                nc.vector.tensor_scalar(c8, sp_b, LRU_C, None, ALU.mult)
                link(nc.vector.tensor_scalar(nc8, sp_b, -LRU_C, None, ALU.mult))
                link(nc.vector.reciprocal(lb_a, lb_b))
                link(nc.vector.tensor_tensor(lb_a, lb_a, lb_b, ALU.mult))
                link(nc.vector.tensor_tensor(lbv, lb_a, lb_a, ALU.subtract))
                nc.vector.tensor_scalar(omlb, lbv, -1.0, 1.0, ALU.mult, ALU.add).then_inc(lru_const, 1)

            b_rec = par[:, COL["b_in"] + DT:COL["b_in"] + 2 * DT]
            nc.vector.tensor_scalar(recp[:, :, 0:3],
                                    b_rec.rearrange("p (f o) -> p f o", o=1).broadcast_to([P, DT, 3]),
                                    -1.0, None, ALU.mult)
            taps = [par[:, COL["conv_w"] + n * DT:COL["conv_w"] + (n + 1) * DT] for n in range(4)]
            link(nc.vector.tensor_tensor(conv_bias, taps[0], taps[1], ALU.add))
            link(nc.vector.tensor_tensor(conv_bias, conv_bias, taps[2], ALU.add))
            link(nc.vector.tensor_tensor(conv_bias, conv_bias, taps[3], ALU.add))
            link(nc.vector.tensor_tensor(conv_bias, conv_bias, b_rec, ALU.mult))
            link(nc.vector.tensor_tensor(conv_bias, conv_bias, par[:, COL["conv_b"]:COL["conv_b"] + DT],
                                         ALU.add))

            def recurrent(name, c, j):
                c0, _, b0 = STAGES[name]
                dve.wait_ge(banks_read, b0 + c - 1 + 5)
                dve.wait_ge(chunk_done, c0 + c + 5)
                nc.vector.tensor_tensor(recp[:, 2 * j:2 * j + 2, 3:],
                                        bank[(b0 + c) % 4][:, :].rearrange("p (a n) -> p a n", a=2),
                                        rs[:, :].rearrange("p (a n) -> p a n", a=2), ALU.mult)\
                    .then_inc(banks_read, 1)
                read(b0 + c)

            def convolve(j):
                dve.wait_ge(tap_ready, j + 1)
                for tap in (2, 1, 0):
                    marks = []
                    for m in range(2):
                        f = 2 * j + m
                        dst = rc[:, j, m * S:(m + 1) * S]
                        if tap < 2:
                            dve.wait_ge(dve_own, before[m])
                        ins = nc.vector.scalar_tensor_tensor(
                            out=dst, in0=recp[:, f, tap:tap + S], scalar=col("conv_w", tap * DT + f),
                            in1=dst, op0=ALU.mult, op1=ALU.add)
                        if tap == 0 and m == 1:
                            ins.then_inc(rc_ready, 1)
                        else:
                            marks.append(mark(ins))
                    before = marks

            def conv_lo(j):
                dve.wait_ge(rc_ready, j + 1)
                dve.wait_ge(rc_hi, j + 1)
                nc.vector.tensor_tensor(pair(rclo, j), rc[:, j, :], pair(rchi, j).bitcast(F32),
                                        ALU.subtract).then_inc(rc_lo, 1)

            def branch(name, c, j):
                c0, _, b0 = STAGES[name]
                dve.wait_ge(banks_read, b0 + c - 1 + 5)
                evacuate(None, c0 + c, b0 + c, gel[:, j, :])
                read(b0 + c)
                for m in range(2):
                    z = gel[:, j, m * S:(m + 1) * S]
                    ins = nc.vector.tensor_scalar(z, z, col("b_in", 2 * j + m), None, ALU.add)
                ins.then_inc(br_z, 1)

            def branch_poly(j):
                dve.wait_ge(br_sq, j + 1)
                nc.vector.tensor_scalar(gsq[:, j % 2, :], gsq[:, j % 2, :], GELU_CUBE, 1.0,
                                        ALU.mult, ALU.add).then_inc(br_cube, 1)

            def branch_cube(j):
                dve.wait_ge(br_cube, j + 1)
                nc.vector.tensor_tensor(gsq[:, j % 2, :], gsq[:, j % 2, :], gel[:, j, :], ALU.mult)\
                    .then_inc(br_in, 1)

            def branch_gelu(j):
                dve.wait_ge(br_tanh, j + 1)
                link(nc.vector.scalar_tensor_tensor(out=gel[:, j, :], in0=gsq[:, j % 2, :], scalar=1.0,
                                                    in1=gel[:, j, :], op0=ALU.add, op1=ALU.mult))

            def one_less_a2(n):
                dve.wait_ge(a_ready, 8 * (n // 2) + 6 + 2 * (n % 2))
                link(nc.vector.tensor_tensor(xg[:, n % 2, :], av[:, n, :], av[:, n, :], ALU.mult))
                nc.vector.scalar_tensor_tensor(out=rg[:, n, :], in0=xg[:, n % 2, :], scalar=1.0,
                                               in1=rg[:, n, :], op0=ALU.add, op1=ALU.mult)\
                    .then_inc(m2_ready, 1)
                dve.wait_ge(m2_ready, n + 1)

            def scan(n):
                dve.wait_ge(ix_ready, n + 1)
                dve.wait_ge(mult_ready, n + 1)
                link(nc.vector.tensor_tensor(rg[:, n, :], rg[:, n, :], ig[:, n, :], ALU.mult))
                for m in range(2):
                    cols = slice(m * S, (m + 1) * S)
                    ins = nc.vector.tensor_tensor_scan(ig[:, n, cols], av[:, n, cols], rg[:, n, cols],
                                                       0.0, ALU.mult, ALU.add)
                link(ins)

            def output(n):
                nc.vector.scalar_tensor_tensor(out=rc[:, n, :], in0=gel[:, n, :], scalar=0.5,
                                               in1=ig[:, n, :], op0=ALU.mult, op1=ALU.mult)\
                    .then_inc(y_ready, 1)

            def output_lo(n):
                dve.wait_ge(y_ready, n + 1)
                dve.wait_ge(y_hi, n + 1)
                nc.vector.tensor_tensor(pair(ylo, n), rc[:, n, :], pair(yhi, n).bitcast(F32),
                                        ALU.subtract).then_inc(y_lo, 1)

            c0 = STAGES["rec_a"][0]
            recurrent("rec_a", 0, 0)
            ahead(c0)
            recurrent("rec_a", 1, 1)
            convolve(0)
            convolve(1)
            conv_lo(0)
            ahead(c0 + 1)
            conv_lo(1)
            recurrent("rec_a", 2, 2)
            ahead(c0 + 2)
            convolve(2)
            conv_lo(2)
            dve.wait_ge(bkt_t, 1)
            nc.vector.tensor_copy(bucket_bias[:, :], bank[5][0:8, 0:384]).then_inc(bkt_done, 1)
            ahead(STAGES["gates_a"][0])
            recurrent("rec_b", 0, 3)
            lru_constants()
            convolve(3)
            ahead(STAGES["rec_b"][0])
            conv_lo(3)
            branch("branch_a", 0, 0)
            one_less_a2(0)
            one_less_a2(1)
            ahead(STAGES["branch_a"][0])
            dve.wait_ge(p_hi, 1)
            nc.vector.tensor_tensor(whole(plo), bank[6][:, :], whole(phi).bitcast(F32),
                                    ALU.subtract).then_inc(p_lo, 1)
            ahead(STAGES["gates_b"][0])
            branch_poly(0)
            scan(0)
            scan(1)
            c0 = STAGES["branch_b"][0]
            ahead(c0)
            branch_gelu(0)
            output(0)
            branch("branch_b", 0, 1)
            one_less_a2(2)
            one_less_a2(3)
            output_lo(0)
            ahead(c0 + 1)
            branch_poly(1)
            branch("branch_b", 1, 2)
            scan(2)
            scan(3)
            branch_gelu(1)
            output(1)
            ahead(c0 + 2)
            branch_poly(2)
            branch_cube(2)
            output_lo(1)
            branch_gelu(2)
            output(2)
            branch("branch_b", 2, 3)
            ahead(STAGES["lru_out"][0])
            output_lo(2)
            branch_poly(3)
            branch_cube(3)
            branch_gelu(3)
            output(3)
            output_lo(3)

            c0l, _, b0l = STAGES["lru_out"]

            def lru_residual(j):
                dve.wait_ge(chunk_done, c0l + j + 5)
                for m in range(2):
                    cols = slice(m * S, (m + 1) * S)
                    ins = nc.vector.scalar_tensor_tensor(
                        out=h[:, j, cols], in0=bank[(b0l + j) % 4][:, cols],
                        scalar=col("b_out", 2 * j + m), in1=h[:, j, cols], op0=ALU.add, op1=ALU.add)
                ins.then_inc(banks_read, 1)
                read(b0l + j)

            nxt = c0l + AHEAD
            norm(1, gains("ffn_norm"), lru_residual, ((nxt + 1,), (), (), (nxt + 2, nxt + 3)))

            def ffn(layer):
                n = 1 + 2 * layer
                norm_factor(n)
                c0, _, b0 = STAGES[f"ffn_in{layer}"]

                def gated(i, c, q, par_q):
                    split(i, c0 + c + AHEAD)
                    evacuate(i, c0 + c, b0 + c, tg[:, par_q, :])
                    split(i, c0 + c + 1 + AHEAD)
                    dve.wait_ge(sig_ready, at(i, 2, FFN_PAIRS * layer + q + 1))
                    dve.wait_ge(banks_read, at(i, 4, b0 + c + 5))
                    nc.vector.tensor_tensor(tg[:, par_q, :], tg[:, par_q, :], sg[:, par_q, :], ALU.mult)\
                        .then_inc(silu_ready, 1)
                    evacuate(i, c0 + c + 1, b0 + c + 1, tu[:, par_q, :])
                    dve.wait_ge(banks_read, at(i, 4, b0 + c + 6))
                    dve.wait_ge(silu_ready, at(i, 2, FFN_PAIRS * layer + q + 1))
                    nc.vector.tensor_tensor(tu[:, par_q, :], tg[:, par_q, :], tu[:, par_q, :], ALU.mult)\
                        .then_inc(act_ready, 1)
                    dve.wait_ge(act_ready, at(i, 2, FFN_PAIRS * layer + q + 1))
                    dve.wait_ge(g_hi, at(i, 2, FFN_PAIRS * layer + q + 1))
                    dst, hi = (glo[:, q, :], ghi[:, q, :]) if i is None else \
                        (glo[:, i * 2 + q, :], ghi[:, i * 2 + q, :])
                    nc.vector.tensor_tensor(dst, tu[:, par_q, :], hi.bitcast(F32), ALU.subtract)\
                        .then_inc(g_lo, 1)
                    dve.wait_ge(g_lo, at(i, 2, FFN_PAIRS * layer + q + 1))

                gated(None, 0, 0, 0)
                with dve.Fori(0, 5) as i:
                    for j in range(2):
                        gated(i, 2 + 2 * j, 1 + j, (1 + j) % 2)
                c0 = STAGES[f"ffn_out{layer}"][0]
                split(None, c0 + AHEAD)
                with dve.Fori(0, 2) as i:
                    for j in range(4):
                        split(i, c0 + 1 + j + AHEAD)
                split(None, c0 + 9 + AHEAD)

            def ffn_residual(layer):
                def update(j):
                    if j < 3:
                        dve.wait_ge(acc_mm, 3 * layer + j + 1)
                    else:
                        dve.wait_ge(chunk_done, STAGES[f"ffn_out{layer}"][0] + 10 + 5)
                    nc.vector.tensor_tensor(h[:, j, :], bank[4 + j][:, :], h[:, j, :], ALU.add)\
                        .then_inc(acc_read, 1)
                    dve.wait_ge(acc_read, 4 * layer + j + 1)
                return update

            ffn(0)
            norm(2, gains("mix_norm", 1), ffn_residual(0),
                 ((), (), (), ()), paced=False)
            split(None, STAGES["qkv"][0] + AHEAD - 1)
            norm_factor(2)

            c0, _, b0 = STAGES["qkv"]

            def masked_logits(g, heads):
                for n in heads:
                    dve.wait_ge(z_mm, 4 * g + HEAD_ORDER.index(n) + 1)
                    nc.vector.tensor_tensor(zz[:, n, :], bank[4 + n][:, 0:384], cst("causal", 384), ALU.add)\
                        .then_inc(z_read, 1)

            def neg_log_fail(g):
                dve.wait_ge(z_read, 4 * g + 4)
                for n in range(4):
                    dve.wait_ge(l_ready, 2 * g + n // 2 + 1)
                    nc.vector.scalar_tensor_tensor(out=ee[:, n, :], in0=zz[:, n, :], scalar=0.0,
                                                   in1=ee[:, n, :], op0=ALU.max, op1=ALU.add)\
                        .then_inc(sp_ready, 1)
                for n in range(4):
                    dve.wait_ge(nl_hi, 4 * g + n + 1)
                    nc.vector.tensor_tensor(nllo[:, n, :], ee[:, n, :], nlhi[:, n, :].bitcast(F32),
                                            ALU.subtract).then_inc(nl_ready, 1)

            def exponents(g):
                dve.wait_ge(nl_ready, 4 * g + 4)
                for n in range(4):
                    dve.wait_ge(s_mm, 4 * g + n + 1)
                    nc.vector.tensor_tensor(zz[:, n, :], zz[:, n, :], bank[4 + n][:, 0:384], ALU.add)\
                        .then_inc(arg_ready, 1)

            def outputs(g):
                dve.wait_ge(o_hi, g + 1)
                nc.vector.tensor_tensor(olo[:, g, :], bank[4][:, :], ohi[:, g, :].bitcast(F32),
                                        ALU.subtract).then_inc(o_lo, 1)

            def logits_out(g):
                if g:
                    dve.wait_ge(w_ready, 4 * g)
                masked_logits(g, HEAD_ORDER[:1])
                if g:
                    outputs(g - 1)
                masked_logits(g, HEAD_ORDER[1:])

            for g in range(GROUPS):
                for q in range(3):
                    c, b = c0 + 3 * g + q, b0 + 3 * g + q
                    if g and q == 0:
                        logits_out(g - 1)
                    if g and q == 1:
                        neg_log_fail(g - 1)
                    ahead(c)
                    if g and q == 2:
                        exponents(g - 1)
                    if q == 0:
                        dve.wait_ge(chunk_done, c + 5)
                        nc.vector.scalar_tensor_tensor(out=whole(qa[:, g % 2]), in0=bank[b % 4][:, :],
                                                       scalar=0.125, in1=rs[:, :], op0=ALU.mult,
                                                       op1=ALU.mult).then_inc(banks_read, 1)
                    if q == 1:
                        evacuate(None, c, b, whole(ka[:, g % 2]))
                    if q == 2:
                        if g == 0:
                            token_factors(0)
                        dve.wait_ge(chunk_done, c + 5)
                        for m in range(2):
                            ins = nc.vector.tensor_scalar(va[:, g % 2, m, :], bank[b % 4][:, m * S:(m + 1) * S],
                                                          rs_tok[:, m:m + 1], None, ALU.mult)
                        ins.then_inc(banks_read, 1)
            c0a, _, b0a = STAGES["attn_out"]
            logits_out(GROUPS - 1)
            ahead(c0a)
            neg_log_fail(GROUPS - 1)
            exponents(GROUPS - 1)
            outputs(GROUPS - 1)

            def attn_residual(j):
                dve.wait_ge(chunk_done, c0a + j + 5)
                nc.vector.tensor_tensor(h[:, j, :], bank[(b0a + j) % 4][:, :], h[:, j, :], ALU.add)\
                    .then_inc(banks_read, 1)
                read(b0a + j)

            nxt = c0a + AHEAD
            norm(3, gains("ffn_norm", 1), attn_residual,
                 ((nxt + 1,), (), (), ()), paced=False)
            split(None, nxt + 2)
            split(None, nxt + 3)
            ffn(1)
            link(nc.vector.tensor_tensor(two_gains, gains("final_norm"), gains("norm_gain"), ALU.mult))
            norm(4, two_gains, ffn_residual(1),
                 ((), (), (), ()), paced=False)
            split(None, STAGES["mix_in"][0] + AHEAD - 1)
            rs1 = xg[:, 1, 0:S]

            def first_factor():
                norm_factor(4)
                link(nc.vector.tensor_copy(rs1, rs[:, 0:S]))

            def second_factor():
                dve.wait_ge(mean_ready, 6)
                link(nc.vector.tensor_tensor(xg[:, 0, 0:S], bank[7][:, 0:S], rs1, ALU.mult))
                nc.vector.tensor_tensor(xg[:, 0, 0:S], xg[:, 0, 0:S], rs1, ALU.mult).then_inc(ms_ready, 1)

            def both_factors():
                dve.wait_ge(sd_ready, 6)
                link(nc.vector.reciprocal(xg[:, 0, 0:S], sq[:, 0, 0:S]))
                nc.vector.tensor_tensor(rs[:, 0:S], xg[:, 0, 0:S], rs1, ALU.mult)
                nc.vector.tensor_tensor(rs[:, S:], xg[:, 0, 0:S], rs1, ALU.mult).then_inc(rs_ready, 1)
                dve.wait_ge(rs_ready, 6)

            def final_norm(j):
                dve.wait_ge(sq_ready, 24)
                for m in range(2):
                    cols = slice(m * S, (m + 1) * S)
                    ins = nc.vector.scalar_tensor_tensor(
                        out=h[:, j, cols], in0=h[:, j, cols], scalar=col("final_norm", 2 * j + m),
                        in1=rs1, op0=ALU.mult, op1=ALU.mult)
                if j == 3:
                    link(ins)

            c0, _, b0 = STAGES["mix_in"]

            def silu(c, tensor, j, k):
                dve.wait_ge(gate_sig, k)
                link(nc.vector.tensor_tensor(tensor[:, j, :], tensor[:, j, :], xg[:, c % 2, :], ALU.mult))

            def token_values(c, dst, c_cols):
                dve.wait_ge(chunk_done, c0 + c + 5)
                for m in range(2):
                    ins = nc.vector.tensor_scalar(dst[:, m, c_cols:c_cols + S],
                                                  bank[(b0 + c) % 4][:, m * S:(m + 1) * S],
                                                  rs_tok[:, m:m + 1], None, ALU.mult)
                ins.then_inc(banks_read, 1)

            def head_norm(kind):
                src, den, gain = ((mq, e_even, q_gain), (mk, qe, col("k_gain")))[kind]
                dve.wait_ge(msd, kind + 1)
                nc.vector.scalar_tensor_tensor(out=whole(src), in0=whole(src), scalar=gain,
                                               in1=den[:, :], op0=ALU.mult, op1=ALU.mult)\
                    .then_inc(mn_ready, 1)

            def moba_max(g):
                dve.wait_ge(bias_read, 4)
                for n in range(4):
                    dve.wait_ge(sc_mm, 4 * g + n + 1)
                    for m, (s0, s1, o0) in enumerate(((0, S, 0), (S, 384, P))):
                        k = 2 * n + m
                        ins = nc.vector.tensor_tensor_reduce(
                            out=pp_[:, n, s0:s1], in0=bank[4 + n][:, s0:s1],
                            in1=bias[:, 4 * g + n, o0:S], scale=1.0, scalar=3.0 * MASKED,
                            op0=ALU.add, op1=ALU.max, accum_out=mx[:, k:k + 1])
                link(ins)
                nc.vector.tensor_scalar(nmx, mx, -1.0, None, ALU.mult).then_inc(nm_ready, 1)

            def moba_scale(g):
                dve.wait_ge(p_exp, 8 * (g + 1))
                link(nc.vector.reciprocal(rsm, sm))
                for n in range(4):
                    for m, (s0, s1) in enumerate(((0, S), (S, 384))):
                        ins = nc.vector.tensor_scalar(pp_[:, n, s0:s1], pp_[:, n, s0:s1],
                                                      rsm[:, 2 * n + m:2 * n + m + 1], None, ALU.mult)
                    ins.then_inc(p_ready, 1)

            def moba_out(g):
                dve.wait_ge(mpv_mm, g + 1)
                nc.vector.tensor_copy(ya[:, g, :], bank[4][:, :]).then_inc(mpv_read, 1)

            def decay_start():
                nc.vector.tensor_scalar(lf_b[:, :], whole(fb), -1.0, EXP_CLIP, ALU.mult, ALU.min)\
                    .then_inc(f_in, 1)

            def decay_sum():
                dve.wait_ge(f_ready, 1)
                nc.vector.memset(ones[:, :], 1.0)
                link(nc.vector.scalar_tensor_tensor(out=lf[:, :], in0=whole(fb), scalar=0.0,
                                                    in1=lf[:, :], op0=ALU.min, op1=ALU.subtract))
                link(nc.vector.tensor_tensor(lf[:, :], lf[:, :], lf_b[:, :], ALU.add))
                for n in range(HGRN_HEADS):
                    ins = nc.vector.tensor_tensor_scan(cum[:, n * S:(n + 1) * S], ones[:, :],
                                                       lf[:, n * S:(n + 1) * S], 0.0, ALU.mult, ALU.add)
                link(ins)

            def decay_keys():
                dve.wait_ge(k_sig, 1)
                for n in range(HGRN_HEADS):
                    k = whole(kb)[:, n * S:(n + 1) * S]
                    ins = nc.vector.tensor_scalar(k, k, omlb[:, n:n + 1], None, ALU.mult)
                link(ins)
                nc.vector.memset(whole(score), 0.0).then_inc(lv_ready, 1)
                dve.wait_ge(lv_ready, 1)

            def level_start(j):
                m = LEVELS[j]
                if j >= 3:
                    dve.wait_ge(lv_ready, j - 1)
                e = (e_even, e_odd)[j % 2]
                v = cum[:, :].rearrange("p (b t) -> p b t", t=2 * m)
                mid = v[:, :, m - 1:m].broadcast_to([P, 1024 // (2 * m), 2 * m])
                nc.vector.tensor_tensor(e[:, :].rearrange("p (b t) -> p b t", t=2 * m), v, mid,
                                        ALU.subtract).then_inc(lv_sub, 1)

            def level_factors(j):
                e = (e_even, e_odd)[j % 2]
                dve.wait_ge(lv_exp, j)
                if j >= 2:
                    dve.wait_ge(lv_mm, j)
                if LEVELS[j] == P:
                    def half(x, a):
                        return x.rearrange("p (h a n) -> p h a n", a=2, n=P)[:, :, a, :]
                    pairs = [(half(qe[:, :], 1), half(whole(qb), 1), half(e[:, :], 1)),
                             (half(ke[:, :], 0), half(whole(kb), 0), half(e[:, :], 0))]
                else:
                    def late(x):
                        m = LEVELS[j]
                        return x.rearrange("p (b t) -> p b t", t=2 * m)[:, :, m:]
                    pairs = [(late(qe[:, :]), late(whole(qb)), late(e[:, :])),
                             (ke[:, :], whole(kb), e[:, :])]
                for dst, x, y in pairs:
                    ins = nc.vector.tensor_tensor(dst, x, y, ALU.mult)
                ins.then_inc(lv_ready, 1)

            def level_read(j):
                dve.wait_ge(lv_mm, j + 1)
                pair0 = 4 + 2 * (j % 2)
                if LEVELS[j] == P:
                    nc.vector.tensor_copy(whole(cross), bank[pair0][:, :]).then_inc(lv_read, 1)
                    return
                mask = cst("levels", 1024)[:, j * P:(j + 1) * P].bitcast(U32)
                if j == 0:
                    mask = mask.rearrange("p (o n) -> p o n", o=1).broadcast_to([P, 4, P])
                else:
                    m = LEVELS[j]
                    dve.wait_ge(lv_read, j)
                    mask = mask[:, 0:P // 2].rearrange("p (o b t) -> p o b t", o=1, t=m)\
                        .broadcast_to([P, 4, P // (2 * m), m])
                for n in range(2):
                    dst = score[:, 4 * n:4 * n + 4, :]
                    new = bank[pair0 + n][:, :].rearrange("p (u n) -> p u n", n=P)
                    if j:
                        dst = dst.rearrange("p u (b t) -> p u b t", t=2 * m)[:, :, :, m:]
                        new = new[:, :, 0:P // 2].rearrange("p u (b t) -> p u b t", t=m)
                    ins = nc.vector.copy_predicated(dst, mask, new)
                ins.then_inc(lv_read, 1)

            for c in range(24):
                if c == 12:
                    moba_scale(1)
                ahead(c0 + c)
                b = b0 + c
                if c == 0:
                    first_factor()
                    second_factor()
                if c == 2:
                    for n in range(4):
                        final_norm(n)
                if c == 4:
                    token_factors(1)
                if c == 4:
                    head_norm(0)
                if c == 6:
                    head_norm(1)
                if c == 7:
                    moba_max(0)
                if c == 8:
                    read(b0 + 7)
                    decay_start()
                    moba_scale(0)
                if c == 10:
                    moba_out(0)
                    decay_sum()
                if c == 11:
                    moba_max(1)
                    silu(8, qb, 0, 1)
                    silu(9, qb, 1, 2)
                if c == 12:
                    decay_keys()
                if c == 14:
                    moba_out(1)
                j = c - 14
                if j >= 1:
                    level_read(j - 1)
                    if j + 2 < len(LEVELS):
                        level_start(j + 2)
                    if j + 1 < len(LEVELS):
                        level_factors(j + 1)
                if c == 1:
                    both_factors()
                    evacuate(None, c0, b0, pair(mq, 0))
                if c == 0:
                    continue
                if c < 2:
                    evacuate(None, c0 + c, b, pair(mq, c))
                elif c < 4:
                    evacuate(None, c0 + c, b, pair(mk, c - 2))
                elif c < 6:
                    token_values(c, mv, (c - 4) * S)
                elif c < 8:
                    evacuate(None, c0 + c, b, fb[:, c - 6, :])
                elif c < 10:
                    evacuate(None, c0 + c, b, qb[:, c - 8, :])
                elif c < 12:
                    token_values(c, vb, (c - 10) * S)
                elif c < 14:
                    evacuate(None, c0 + c, b, ag[:, c - 12, :])
                elif c < 16:
                    evacuate(None, c0 + c, b, bg[:, c - 14, :])
                elif c < 20:
                    evacuate(None, c0 + c, b, ga[:, c - 16, :])
                else:
                    evacuate(None, c0 + c, b, gb[:, c - 20, :])
                if c == 14:
                    level_start(1)
                    level_start(2)
                    level_factors(1)
                if c == 22:
                    silu(12, ag, 0, 3)
                    silu(13, ag, 1, 4)
                    dve.wait_ge(mpv_read, 2)
                    for n in range(2):
                        ins = nc.vector.tensor_tensor(ya[:, n, :], ya[:, n, :], ag[:, n, :], ALU.mult)
                        ins.then_inc(ya_ready, 1)
                if c == 23:
                    for n in range(2):
                        dve.wait_ge(ya_ready, n + 1)
                        dve.wait_ge(ya_hi, n + 1)
                        nc.vector.tensor_tensor(pair(yalo, n), ya[:, n, :], pair(yahi, n).bitcast(F32),
                                                ALU.subtract).then_inc(ya_lo, 1)
                if c == 23:
                    silu(14, bg, 0, 9)
                    silu(15, bg, 1, 10)

            dve.wait_ge(yo_sq, 1)
            for n in range(HGRN_HEADS):
                cols = slice(n * S, (n + 1) * S)
                ins = nc.vector.scalar_tensor_tensor(
                    out=ke[:, cols], in0=bank[4 + n // 2][:, n % 2 * S:(n % 2 + 1) * S],
                    scalar=col("hgrn_gain", n), in1=whole(bg)[:, cols], op0=ALU.mult, op1=ALU.mult)
            ins.then_inc(yo_read, 1)
            dve.wait_ge(yo_read, 1)
            ahead(STAGES["up_a"][0])
            for n in range(2):
                cols = slice(n * PAIR, (n + 1) * PAIR)
                dve.wait_ge(yo_sd, n + 1)
                nc.vector.tensor_tensor(ke[:, cols], ke[:, cols], qe[:, cols], ALU.mult).then_inc(yb_ready, 1)
            for n in range(2):
                cols = slice(n * PAIR, (n + 1) * PAIR)
                dve.wait_ge(yb_ready, n + 1)
                dve.wait_ge(yb_hi, n + 1)
                nc.vector.tensor_tensor(pair(yblo, n), ke[:, cols], pair(ybhi, n).bitcast(F32),
                                        ALU.subtract).then_inc(yb_lo, 1)
            c0, _, b0 = STAGES["up_a"]
            for c in range(2):
                if c:
                    ahead(c0 + c)
                dve.wait_ge(chunk_done, c0 + c + 5)
                for n in (2 * c, 2 * c + 1):
                    dve.wait_ge(gate_sig, 4 + n + 1)
                    nc.vector.tensor_tensor(ga[:, n, :], bank[(b0 + n) % 4][:, :], ga[:, n, :], ALU.mult)\
                        .then_inc(banks_read, 1)
            c0, _, b0 = STAGES["up_b"]
            for c in range(2):
                ahead(c0 + c)
                dve.wait_ge(chunk_done, c0 + c + 5)
                for n in (2 * c, 2 * c + 1):
                    dve.wait_ge(gate_sig, 10 + n + 1)
                    nc.vector.tensor_tensor(gb[:, n, :], bank[(b0 + n) % 4][:, :], gb[:, n, :], ALU.mult)\
                        .then_inc(banks_read, 1)
                    read(b0 + n)
                    nc.vector.tensor_tensor(ga[:, n, :], ga[:, n, :], gb[:, n, :], ALU.add)\
                        .then_inc(m_ready, 1)
                for n in (2 * c, 2 * c + 1):
                    dve.wait_ge(m_ready, n + 1)
                    dve.wait_ge(m_hi, n + 1)
                    nc.vector.tensor_tensor(pair(mlo, n), ga[:, n, :], pair(mhi, n).bitcast(F32),
                                            ALU.subtract).then_inc(m_lo, 1)
            c0, _, b0 = STAGES["out2"]
            for c in range(4):
                ahead(c0 + c)
                dve.wait_ge(chunk_done, c0 + c + 5)
                nc.vector.tensor_tensor(h[:, c, :], bank[(b0 + c) % 4][:, :], h[:, c, :], ALU.add)\
                    .then_inc(banks_read, 1)
                read(b0 + c)
                dve.sem_inc(xg_ready, 1)
                dve.wait_ge(x_hi, 20 + c + 1)
                nc.vector.tensor_tensor(pair(xlo, c), h[:, c, :], pair(xhi, c).bitcast(F32),
                                        ALU.subtract).then_inc(x_lo, 1)
            c0, _, b0 = STAGES["ple"]
            dve.wait_ge(chunk_done, c0 + 5)
            for n in range(4):
                nc.vector.tensor_copy(ple[:, n, :], bank[(b0 + n) % 4][:, :]).then_inc(banks_read, 1)
            ahead(c0)
            read(b0 + 3)
            c0, _, b0 = STAGES["ple_gate"]
            for c in range(4):
                ahead(c0 + c)
                read(b0 + c)
                link(nc.vector.tensor_tensor(xg[:, c % 2, :], xg[:, c % 2, :], ple[:, c, :], ALU.mult))
                nc.vector.tensor_tensor(h[:, c, :], h[:, c, :], xg[:, c % 2, :], ALU.add)\
                    .then_inc(fin_ready, 1)


def constants():
    import numpy as np

    c = np.zeros((P, N_CONST), np.float32)

    def put(name, value, off=0):
        value = np.asarray(value, np.float32)
        c[:value.shape[0], CONST[name] + off:CONST[name] + off + value.shape[1]] = value

    k, q = np.arange(P)[:, None], np.arange(P)[None, :]
    put("ident", k == q)
    put("anti", k + q == P - 1)
    put("suffix", -1.0 * (k >= q))
    put("neg", -np.ones((P, P)))
    put("mean_d", np.full((P, P), 1.0 / D))
    put("mean_head", (k // 64 == q // 64) / 64.0)
    put("mean_v", np.full((P, P), 1.0 / P))
    for off in (0, S):
        put("causal", np.where(k < q, 0.0, MASKED), off)
    put("levels", k == q)
    for n, m in enumerate(LEVELS[1:-1]):
        late = np.arange(P)[np.arange(P) // m % 2 == 1][None, :]
        put("levels", (k // (2 * m) == late // (2 * m)) & (k // m % 2 == 0), (n + 1) * P)
    dist = 255 - np.arange(384)
    far = 16 + (np.log(np.maximum(dist, 16) / 16.0) / np.log(2048 / 16.0) * 16).astype(np.int64)
    bucket = np.where(dist < 0, 32, np.where(dist < 16, dist, np.minimum(far, 31)))
    put("bucket", np.arange(33)[:, None] == bucket[None, :])
    return c


_INS = ["x", "mix_norm", "ffn_norm", "final_norm", "lru_w_in", "lru_b_in", "lru_conv_w", "lru_conv_b",
        "lru_gate_w", "lru_gate_b", "lru_lambda", "lru_w_out", "lru_b_out", "attn_w_qkv", "attn_w_o",
        "ffn_w_in", "ffn_w_out", "p_2", "norm_gain_2", "w_in_2", "q_norm_gain_2", "k_norm_gain_2",
        "rel_bias_2", "hgrn_lb_logits_2", "hgrn_out_gain_2", "w_up_a_2", "w_up_b_2", "w_out_2",
        "w_ple_2", "w_ple_gate_2"]


def kernel(**inputs):
    import numpy as _np
    import concourse.bacc as _bacc
    from concourse import mybir as _mybir
    from concourse.bass_utils import run_bass_kernel_spmd as _run

    nc = _bacc.Bacc("TRN2", target_bir_lowering=False, num_devices=1)
    arrays, aps = {}, {}
    given = {name: _np.ascontiguousarray(inputs[name]) for name in _INS}
    given["consts"] = constants()
    for name, a in given.items():
        arrays[f"in_{name}"] = a
        aps[name] = nc.dram_tensor(f"in_{name}", a.shape, _mybir.dt.from_np(a.dtype),
                                   kind="ExternalInput").ap()
    out = nc.dram_tensor("out_0", (1, S, D), _mybir.dt.float32, kind="ExternalOutput").ap()
    build(nc, aps, out)
    r = _run(nc, [arrays], core_ids=[0])
    return r.results[0]["out_0"]
```
